# Optimizing a Trainium2 kernel written in Bass

```python
import math
import jax, jax.numpy as jnp
from jax import lax
import numpy as np

D_MODEL = 1024
BATCH = 1
SEQ = 512
DEPTH = 2

N_EVEN = (DEPTH + 1) // 2
N_ODD = DEPTH // 2
ALPHA = (2 * DEPTH) ** 0.25
BETA = (8 * DEPTH) ** -0.25
LN_EPS = 1e-5

SC_WIDTH = D_MODEL
SC_KERNEL = 3

SSM_INNER = D_MODEL
SSM_HEADDIM = 64
SSM_HEADS = SSM_INNER // SSM_HEADDIM
SSM_GROUPS = 2
SSM_STATE = 128
SSM_CONV = 4
SSM_CHUNK = 128
SSM_XBC = SSM_INNER + 2 * SSM_GROUPS * SSM_STATE
MIX0_IN = 3 * SC_WIDTH + SSM_INNER + SSM_XBC + SSM_HEADS
MIX0_OUT = SC_WIDTH + SSM_INNER

FOX_HEADS = 16
FOX_HEADDIM = D_MODEL // FOX_HEADS
FOX_WIDTH = FOX_HEADS * FOX_HEADDIM
FOX_IN = 3 * FOX_WIDTH + FOX_HEADS
FOX_BLOCK = 128

D_FF = 2816
FFN_KERNEL = 3


def _split(h, sizes):
    idx = np.cumsum(sizes)[:-1].tolist()
    return jnp.split(h, idx, axis=-1)

def causal_dwconv(x, w, b=None):
    k, c = w.shape
    y = lax.conv_general_dilated(x, w[:, None, :].astype(x.dtype), window_strides=(1,), padding=[(k - 1, 0)], dimension_numbers=('NWC', 'WIO', 'NWC'), feature_group_count=c)
    return y if b is None else y + b.astype(y.dtype)

def layer_norm(x, g, b):
    xf = x.astype(jnp.float32)
    mu = jnp.mean(xf, -1, keepdims=True)
    var = jnp.mean(jnp.square(xf - mu), -1, keepdims=True)
    return ((xf - mu) * lax.rsqrt(var + LN_EPS) * g + b).astype(x.dtype)

def gated_rmsnorm(y, z, g):
    bsz, l, _ = y.shape
    u = (y.astype(jnp.float32) * jax.nn.silu(z.astype(jnp.float32))).reshape(bsz, l, SSM_GROUPS, -1)
    u = u * lax.rsqrt(jnp.mean(jnp.square(u), -1, keepdims=True) + LN_EPS)
    return (u.reshape(bsz, l, SSM_INNER) * g).astype(y.dtype)

def ssd_chunked(xs, dt, a, bm, cm):
    bsz, l = xs.shape[:2]
    nc, q, r = l // SSM_CHUNK, SSM_CHUNK, SSM_HEADS // SSM_GROUPS
    x = xs.astype(jnp.float32).reshape(bsz, nc, q, SSM_GROUPS, r, SSM_HEADDIM)
    dtc = dt.reshape(bsz, nc, q, SSM_GROUPS, r)
    xdt = x * dtc[..., None]
    bc = bm.astype(jnp.float32).reshape(bsz, nc, q, SSM_GROUPS, SSM_STATE)
    cc = cm.astype(jnp.float32).reshape(bsz, nc, q, SSM_GROUPS, SSM_STATE)
    a_cs = jnp.cumsum((dtc * a.reshape(SSM_GROUPS, r)).transpose(0, 1, 3, 4, 2), axis=-1)
    causal = jnp.tril(jnp.ones((q, q), dtype=bool))
    seg = jnp.exp(jnp.where(causal, a_cs[..., :, None] - a_cs[..., None, :], -jnp.inf))
    cb = jnp.einsum('bctgn,bcsgn->bcgts', cc, bc)
    y_diag = jnp.einsum('bcgts,bcgrts,bcsgrp->bctgrp', cb, seg, xdt)
    decay_to_end = jnp.exp(a_cs[..., -1:] - a_cs)
    chunk_states = jnp.einsum('bcsgn,bcgrs,bcsgrp->bcgrpn', bc, decay_to_end, xdt)
    chunk_decay = jnp.exp(a_cs[..., -1])

    def step(h, inp):
        st, dec = inp
        return h * dec[..., None, None] + st, h

    h0 = jnp.zeros((bsz, SSM_GROUPS, r, SSM_HEADDIM, SSM_STATE), jnp.float32)
    _, prev = lax.scan(step, h0, (jnp.moveaxis(chunk_states, 1, 0), jnp.moveaxis(chunk_decay, 1, 0)))
    prev = jnp.moveaxis(prev, 0, 1)
    y_off = jnp.einsum('bctgn,bcgrpn,bcgrt->bctgrp', cc, prev, jnp.exp(a_cs))
    return (y_diag + y_off).reshape(bsz, l, SSM_HEADS, SSM_HEADDIM)

def sconv_ssd_mixer(x, w_in, sc_conv_w, ssm_conv_w, ssm_conv_b, dt_bias, a_log, d_skip, norm_g, w_out):
    bsz, l, _ = x.shape
    h = x @ w_in
    sc_b, sc_c, sc_h, z, xbc, dt_raw = _split(h, [SC_WIDTH, SC_WIDTH, SC_WIDTH, SSM_INNER, SSM_XBC, SSM_HEADS])
    y_a = sc_b * causal_dwconv(sc_c * sc_h, sc_conv_w)
    xbc = jax.nn.silu(causal_dwconv(xbc, ssm_conv_w, ssm_conv_b))
    xs, bm, cm = _split(xbc, [SSM_INNER, SSM_GROUPS * SSM_STATE, SSM_GROUPS * SSM_STATE])
    xs = xs.reshape(bsz, l, SSM_HEADS, SSM_HEADDIM)
    dt = jax.nn.softplus(dt_raw.astype(jnp.float32) + dt_bias.astype(jnp.float32))
    a = -jnp.exp(a_log.astype(jnp.float32))
    y = ssd_chunked(xs, dt, a, bm.reshape(bsz, l, SSM_GROUPS, SSM_STATE), cm.reshape(bsz, l, SSM_GROUPS, SSM_STATE))
    y = y + d_skip.astype(jnp.float32)[:, None] * xs.astype(jnp.float32)
    y_b = gated_rmsnorm(y.reshape(bsz, l, SSM_INNER).astype(x.dtype), z, norm_g)
    return jnp.concatenate([y_a, y_b], axis=-1) @ w_out

def fox_mixer(x, w_in, b_f, w_out):
    bsz, l, _ = x.shape
    nb = l // FOX_BLOCK
    h = x @ w_in
    q, k, v, f_logit = _split(h, [FOX_WIDTH, FOX_WIDTH, FOX_WIDTH, FOX_HEADS])
    heads = lambda t: t.reshape(bsz, l, FOX_HEADS, FOX_HEADDIM).transpose(0, 2, 1, 3)
    q, k, v = heads(q), heads(k), heads(v)
    log_f = jax.nn.log_sigmoid(f_logit.astype(jnp.float32) + b_f.astype(jnp.float32))
    cum = jnp.cumsum(log_f, axis=1).transpose(0, 2, 1)
    scale = FOX_HEADDIM ** -0.5
    key_pos = jnp.arange(l)

    def block(args):
        q_blk, cum_blk, i = args
        qpos = i * FOX_BLOCK + jnp.arange(FOX_BLOCK)
        s = jnp.einsum('bhqd,bhkd->bhqk', q_blk, k).astype(jnp.float32) * scale + cum_blk[..., None] - cum[:, :, None, :]
        s = jnp.where(key_pos[None, :] <= qpos[:, None], s, -jnp.inf)
        p = jax.nn.softmax(s, axis=-1)
        return jnp.einsum('bhqk,bhkd->bhqd', p.astype(v.dtype), v)

    q_blocks = q.reshape(bsz, FOX_HEADS, nb, FOX_BLOCK, FOX_HEADDIM).transpose(2, 0, 1, 3, 4)
    cum_blocks = cum.reshape(bsz, FOX_HEADS, nb, FOX_BLOCK).transpose(2, 0, 1, 3)
    o = lax.map(block, (q_blocks, cum_blocks, jnp.arange(nb)))
    o = o.transpose(1, 0, 3, 2, 4).reshape(bsz, l, FOX_WIDTH)
    return o @ w_out

def conv_ffn(x, w_up, conv_w, conv_b, w_down):
    h = causal_dwconv(x @ w_up, conv_w, conv_b)
    u, g = _split(h, [D_FF, D_FF])
    return (u * jax.nn.silu(g)) @ w_down

def first_inputs(seed: int = 0) -> dict:
    key = jax.random.key(seed)
    ks = jax.random.split(key, 21)
    f32 = jnp.float32

    def nrm(k, shape, scale):
        return jax.random.normal(k, shape, f32) * scale

    x = nrm(ks[0], (BATCH, SEQ, D_MODEL), 1.0)
    sc_ssm_w_in = nrm(ks[1], (N_EVEN, D_MODEL, MIX0_IN), D_MODEL ** -0.5)
    sc_conv_w = nrm(ks[2], (N_EVEN, SC_KERNEL, SC_WIDTH), SC_KERNEL ** -0.5)
    ssm_conv_w = nrm(ks[3], (N_EVEN, SSM_CONV, SSM_XBC), SSM_CONV ** -0.5)
    ssm_conv_b = nrm(ks[4], (N_EVEN, SSM_XBC), 0.02)
    dt0 = jnp.exp(jax.random.uniform(ks[5], (N_EVEN, SSM_HEADS), f32, minval=math.log(1e-3), maxval=math.log(1e-1)))
    ssm_dt_bias = dt0 + jnp.log(-jnp.expm1(-dt0))
    ssm_a_log = jnp.log(jax.random.uniform(ks[6], (N_EVEN, SSM_HEADS), f32, minval=1.0, maxval=16.0))
    ssm_d = 1.0 + nrm(ks[7], (N_EVEN, SSM_HEADS), 0.1)
    ssm_norm_g = 1.0 + nrm(ks[8], (N_EVEN, SSM_INNER), 0.02)
    sc_ssm_w_out = nrm(ks[9], (N_EVEN, MIX0_OUT, D_MODEL), BETA * MIX0_OUT ** -0.5)
    col_scale = jnp.concatenate([jnp.ones((2 * FOX_WIDTH,), f32), jnp.full((FOX_WIDTH,), BETA, f32), jnp.ones((FOX_HEADS,), f32)])
    fox_w_in = nrm(ks[10], (N_ODD, D_MODEL, FOX_IN), D_MODEL ** -0.5) * col_scale
    fox_b_f = jax.random.uniform(ks[11], (N_ODD, FOX_HEADS), f32, minval=1.0, maxval=4.0)
    fox_w_out = nrm(ks[12], (N_ODD, FOX_WIDTH, D_MODEL), BETA * FOX_WIDTH ** -0.5)
    ffn_w_up = nrm(ks[13], (DEPTH, D_MODEL, 2 * D_FF), BETA * D_MODEL ** -0.5)
    ffn_conv_w = nrm(ks[14], (DEPTH, FFN_KERNEL, 2 * D_FF), FFN_KERNEL ** -0.5)
    ffn_conv_b = nrm(ks[15], (DEPTH, 2 * D_FF), 0.02)
    ffn_w_down = nrm(ks[16], (DEPTH, D_FF, D_MODEL), BETA * D_FF ** -0.5)
    ln_mix_g = 1.0 + nrm(ks[17], (DEPTH, D_MODEL), 0.02)
    ln_mix_b = nrm(ks[18], (DEPTH, D_MODEL), 0.02)
    ln_ffn_g = 1.0 + nrm(ks[19], (DEPTH, D_MODEL), 0.02)
    ln_ffn_b = nrm(ks[20], (DEPTH, D_MODEL), 0.02)
    return {'x': x, 'sc_ssm_w_in': sc_ssm_w_in, 'sc_conv_w': sc_conv_w, 'ssm_conv_w': ssm_conv_w, 'ssm_conv_b': ssm_conv_b, 'ssm_dt_bias': ssm_dt_bias, 'ssm_a_log': ssm_a_log, 'ssm_d': ssm_d, 'ssm_norm_g': ssm_norm_g, 'sc_ssm_w_out': sc_ssm_w_out, 'fox_w_in': fox_w_in, 'fox_b_f': fox_b_f, 'fox_w_out': fox_w_out, 'ffn_w_up': ffn_w_up, 'ffn_conv_w': ffn_conv_w, 'ffn_conv_b': ffn_conv_b, 'ffn_w_down': ffn_w_down, 'ln_mix_g': ln_mix_g, 'ln_mix_b': ln_mix_b, 'ln_ffn_g': ln_ffn_g, 'ln_ffn_b': ln_ffn_b}

def first_block(x, sc_ssm_w_in, sc_conv_w, ssm_conv_w, ssm_conv_b, ssm_dt_bias, ssm_a_log, ssm_d, ssm_norm_g, sc_ssm_w_out, fox_w_in, fox_b_f, fox_w_out, ffn_w_up, ffn_conv_w, ffn_conv_b, ffn_w_down, ln_mix_g, ln_mix_b, ln_ffn_g, ln_ffn_b):
    for i in range(DEPTH):
        j = i // 2
        if i % 2 == 0:
            mix = sconv_ssd_mixer(x, sc_ssm_w_in[j], sc_conv_w[j], ssm_conv_w[j], ssm_conv_b[j], ssm_dt_bias[j], ssm_a_log[j], ssm_d[j], ssm_norm_g[j], sc_ssm_w_out[j])
        else:
            mix = fox_mixer(x, fox_w_in[j], fox_b_f[j], fox_w_out[j])
        x = layer_norm(ALPHA * x + mix, ln_mix_g[i], ln_mix_b[i])
        x = layer_norm(ALPHA * x + conv_ffn(x, ffn_w_up[i], ffn_conv_w[i], ffn_conv_b[i], ffn_w_down[i]), ln_ffn_g[i], ln_ffn_b[i])
    return x


N_MIXERS = 2
N_ATTN_LAYERS = (DEPTH + N_MIXERS - 1) // N_MIXERS
N_GMLP_LAYERS = DEPTH // N_MIXERS
HEAD_DIM = 64
N_HEADS = D_MODEL // HEAD_DIM
N_KV_HEADS = N_HEADS // 4
KV_GROUP = N_HEADS // N_KV_HEADS
Q_WIDTH = N_HEADS * HEAD_DIM
KV_WIDTH = N_KV_HEADS * HEAD_DIM
QKV_WIDTH = Q_WIDTH + 2 * KV_WIDTH
Q_BLOCK = 128
ROPE_THETA = 10000.0
ROPE_PAIRS_AXIS = HEAD_DIM // 4
GRID_W = 64
GMLP_FFN = 6 * D_MODEL
GMLP_HALF = GMLP_FFN // 2
GMLP_CHUNK = 128
GMLP_GROUPS = 16
GMLP_GROUP_WIDTH = GMLP_HALF // GMLP_GROUPS
MLP_HIDDEN = 4 * D_MODEL
N_MOD = 6
EPS = 1e-6


def rmsnorm(x, g):
    xf = x.astype(jnp.float32)
    y = xf * lax.rsqrt(jnp.mean(xf * xf, axis=-1, keepdims=True) + EPS)
    return (y * g).astype(x.dtype)

def layernorm(x, g, b):
    xf = x.astype(jnp.float32)
    mu = jnp.mean(xf, axis=-1, keepdims=True)
    xc = xf - mu
    y = xc * lax.rsqrt(jnp.mean(xc * xc, axis=-1, keepdims=True) + EPS)
    return (y * g + b).astype(x.dtype)

def modulate(h, shift, scale):
    return h * (1.0 + scale[:, None, :]) + shift[:, None, :]

def axial_rope_tables(seq_len):
    t = jnp.arange(seq_len, dtype=jnp.int32)
    rows = seq_len // GRID_W
    row = (t // GRID_W - rows // 2).astype(jnp.float32)
    col = (t % GRID_W - GRID_W // 2).astype(jnp.float32)
    inv_freq = ROPE_THETA ** (-jnp.arange(ROPE_PAIRS_AXIS, dtype=jnp.float32) / ROPE_PAIRS_AXIS)
    ang = jnp.concatenate([row[:, None] * inv_freq, col[:, None] * inv_freq], axis=-1)
    return jnp.cos(ang), jnp.sin(ang)

def apply_rope(x, cos, sin):
    xp = x.astype(jnp.float32).reshape(*x.shape[:-1], HEAD_DIM // 2, 2)
    x1, x2 = xp[..., 0], xp[..., 1]
    c, s = cos[:, None, :], sin[:, None, :]
    out = jnp.stack([x1 * c - x2 * s, x1 * s + x2 * c], axis=-1)
    return out.reshape(x.shape).astype(x.dtype)

def gqa_attention(h, w_qkv, q_g, k_g, w_o, cos, sin):
    B, T, _ = h.shape
    qkv = h @ w_qkv
    q, k, v = jnp.split(qkv, [Q_WIDTH, Q_WIDTH + KV_WIDTH], axis=-1)
    q = apply_rope(rmsnorm(q.reshape(B, T, N_HEADS, HEAD_DIM), q_g), cos, sin)
    k = apply_rope(rmsnorm(k.reshape(B, T, N_KV_HEADS, HEAD_DIM), k_g), cos, sin)
    v = v.reshape(B, T, N_KV_HEADS, HEAD_DIM)
    n_blocks = T // Q_BLOCK
    qb = q.reshape(B, n_blocks, Q_BLOCK, N_KV_HEADS, KV_GROUP, HEAD_DIM).transpose(1, 0, 2, 3, 4, 5)
    scale = HEAD_DIM ** -0.5

    def one_block(q_blk):
        s = jnp.einsum('bqkgd,bskd->bkgqs', q_blk, k).astype(jnp.float32) * scale
        p = jax.nn.softmax(s, axis=-1).astype(v.dtype)
        return jnp.einsum('bkgqs,bskd->bqkgd', p, v)

    o = lax.map(one_block, qb)
    o = o.transpose(1, 0, 2, 3, 4, 5).reshape(B, T, Q_WIDTH)
    return o @ w_o

def chunked_gmlp(h, w_in, b_in, ln_g, ln_b, w_s, b_s, w_out):
    B, T, _ = h.shape
    z = jax.nn.gelu(h @ w_in + b_in, approximate=False)
    u, v = jnp.split(z, 2, axis=-1)
    v = layernorm(v, ln_g, ln_b)
    v = v.reshape(B, T // GMLP_CHUNK, GMLP_CHUNK, GMLP_GROUPS, GMLP_GROUP_WIDTH)
    v = jnp.einsum('gpq,bnqgc->bnpgc', w_s, v) + b_s.T[None, None, :, :, None]
    v = v.reshape(B, T, GMLP_HALF)
    return (u * v) @ w_out

def sq_relu_mlp(h, w_in, w_out):
    return jnp.square(jax.nn.relu(h @ w_in)) @ w_out

def second_inputs(seed: int = 0) -> dict:
    key = jax.random.key(seed)
    ks = jax.random.split(key, 20)

    def nrm(k, shape, scale):
        return jax.random.normal(k, shape, jnp.float32) * scale

    return {
        "x": nrm(ks[0], (BATCH, SEQ, D_MODEL), 1.0),
        "c": nrm(ks[1], (BATCH, D_MODEL), 1.0),
        "ada_w": nrm(ks[2], (DEPTH, D_MODEL, N_MOD * D_MODEL), 0.5 * D_MODEL ** -0.5),
        "ada_b": nrm(ks[3], (DEPTH, N_MOD * D_MODEL), 0.01),
        "norm1_g": 1.0 + nrm(ks[4], (DEPTH, D_MODEL), 0.05),
        "norm2_g": 1.0 + nrm(ks[5], (DEPTH, D_MODEL), 0.05),
        "attn_w_qkv": nrm(ks[6], (N_ATTN_LAYERS, D_MODEL, QKV_WIDTH), D_MODEL ** -0.5),
        "attn_q_norm_g": 1.0 + nrm(ks[7], (N_ATTN_LAYERS, HEAD_DIM), 0.05),
        "attn_k_norm_g": 1.0 + nrm(ks[8], (N_ATTN_LAYERS, HEAD_DIM), 0.05),
        "attn_w_o": nrm(ks[9], (N_ATTN_LAYERS, Q_WIDTH, D_MODEL), Q_WIDTH ** -0.5),
        "gmlp_w_in": nrm(ks[10], (N_GMLP_LAYERS, D_MODEL, GMLP_FFN), D_MODEL ** -0.5),
        "gmlp_b_in": nrm(ks[11], (N_GMLP_LAYERS, GMLP_FFN), 0.01),
        "gmlp_ln_g": 1.0 + nrm(ks[12], (N_GMLP_LAYERS, GMLP_HALF), 0.05),
        "gmlp_ln_b": nrm(ks[13], (N_GMLP_LAYERS, GMLP_HALF), 0.01),
        "gmlp_w_s": nrm(ks[14], (N_GMLP_LAYERS, GMLP_GROUPS, GMLP_CHUNK, GMLP_CHUNK), GMLP_CHUNK ** -0.5),
        "gmlp_b_s": 1.0 + nrm(ks[15], (N_GMLP_LAYERS, GMLP_GROUPS, GMLP_CHUNK), 0.05),
        "gmlp_w_out": nrm(ks[16], (N_GMLP_LAYERS, GMLP_HALF, D_MODEL), GMLP_HALF ** -0.5),
        "mlp_w_in": nrm(ks[17], (DEPTH, D_MODEL, MLP_HIDDEN), D_MODEL ** -0.5),
        "mlp_w_out": nrm(ks[18], (DEPTH, MLP_HIDDEN, D_MODEL), MLP_HIDDEN ** -0.5),
    }

def second_block(x, c, ada_w, ada_b, norm1_g, norm2_g, attn_w_qkv, attn_q_norm_g,
              attn_k_norm_g, attn_w_o, gmlp_w_in, gmlp_b_in, gmlp_ln_g, gmlp_ln_b,
              gmlp_w_s, gmlp_b_s, gmlp_w_out, mlp_w_in, mlp_w_out):
    cond = jax.nn.silu(c)
    cos, sin = axial_rope_tables(x.shape[1])
    for i in range(DEPTH):
        mod = cond @ ada_w[i] + ada_b[i]
        sh1, sc1, g1, sh2, sc2, g2 = jnp.split(mod, N_MOD, axis=-1)
        h = modulate(rmsnorm(x, norm1_g[i]), sh1, sc1)
        j = i // N_MIXERS
        if i % N_MIXERS == 0:
            y = gqa_attention(h, attn_w_qkv[j], attn_q_norm_g[j], attn_k_norm_g[j],
                              attn_w_o[j], cos, sin)
        else:
            y = chunked_gmlp(h, gmlp_w_in[j], gmlp_b_in[j], gmlp_ln_g[j], gmlp_ln_b[j],
                             gmlp_w_s[j], gmlp_b_s[j], gmlp_w_out[j])
        x = x + g1[:, None, :] * y
        h = modulate(rmsnorm(x, norm2_g[i]), sh2, sc2)
        x = x + g2[:, None, :] * sq_relu_mlp(h, mlp_w_in[i], mlp_w_out[i])
    return x


def setup_inputs(seed=0):
    out = dict(first_inputs(seed))
    for name, value in second_inputs(seed + 1).items():
        if name != "x":
            out[name + "_2"] = value
    return out


def reference(
    x, sc_ssm_w_in, sc_conv_w, ssm_conv_w, ssm_conv_b, ssm_dt_bias, ssm_a_log, ssm_d,
    ssm_norm_g, sc_ssm_w_out, fox_w_in, fox_b_f, fox_w_out, ffn_w_up, ffn_conv_w, ffn_conv_b,
    ffn_w_down, ln_mix_g, ln_mix_b, ln_ffn_g, ln_ffn_b, c_2, ada_w_2, ada_b_2, norm1_g_2,
    norm2_g_2, attn_w_qkv_2, attn_q_norm_g_2, attn_k_norm_g_2, attn_w_o_2, gmlp_w_in_2,
    gmlp_b_in_2, gmlp_ln_g_2, gmlp_ln_b_2, gmlp_w_s_2, gmlp_b_s_2, gmlp_w_out_2, mlp_w_in_2,
    mlp_w_out_2,
):
    x = first_block(
        x, sc_ssm_w_in, sc_conv_w, ssm_conv_w, ssm_conv_b, ssm_dt_bias, ssm_a_log, ssm_d,
        ssm_norm_g, sc_ssm_w_out, fox_w_in, fox_b_f, fox_w_out, ffn_w_up, ffn_conv_w,
        ffn_conv_b, ffn_w_down, ln_mix_g, ln_mix_b, ln_ffn_g, ln_ffn_b,
    )
    return second_block(
        x, c_2, ada_w_2, ada_b_2, norm1_g_2, norm2_g_2, attn_w_qkv_2, attn_q_norm_g_2,
        attn_k_norm_g_2, attn_w_o_2, gmlp_w_in_2, gmlp_b_in_2, gmlp_ln_g_2, gmlp_ln_b_2,
        gmlp_w_s_2, gmlp_b_s_2, gmlp_w_out_2, mlp_w_in_2, mlp_w_out_2,
    )


_drawn_inputs = setup_inputs


def setup_inputs(seed=0):
    import zlib

    import numpy as np

    out = dict(_drawn_inputs(seed))
    spreads = {}
    factors = {'ssm_conv_b': 8.0,
     'ssm_d': 3.624,
     'ssm_norm_g': 8.0,
     'ffn_conv_b': 8.0,
     'norm1_g_2': 3.237,
     'attn_q_norm_g_2': 8.0,
     'attn_k_norm_g_2': 8.0,
     'gmlp_b_in_2': 8.0,
     'gmlp_ln_g_2': 5.559,
     'gmlp_ln_b_2': 44.852,
     'gmlp_b_s_2': 5.918}
    for name, (base, spread) in spreads.items():
        noise = np.random.default_rng([zlib.crc32(name.encode()), seed]).standard_normal(out[name].shape)
        drawn = base * np.exp(spread * noise) if base else spread * noise
        out[name] = __import__('jax').numpy.asarray(drawn.astype(out[name].dtype))
    for name, factor in factors.items():
        out[name] = (out[name] * factor).astype(out[name].dtype)
    return out
```

```python
from contextlib import ExitStack

import numpy as np
import concourse.bass as bass
from concourse import mybir

F32 = mybir.dt.float32
F32R = mybir.dt.float32r
ALU = mybir.AluOpType
ACT = mybir.ActivationFunctionType
AX = mybir.AxisListType

P = 128
T = 512
NT = T // P
D = 1024
KD = D // P
HALF = 512
UNIT = 1024
RING = 4
D_FF = 2816
NFF = D_FF // P
HEADS = 16
HD = 64
SSM_XBC = 1536
GM_HALF = 3072
NGM = GM_HALF // P
GM_GROUPS = 16
GM_GW = GM_HALF // GM_GROUPS
MLP = 4096
NMLP = MLP // P
ALPHA = 4 ** 0.25
LN_EPS = 1e-5
EPS = 1e-6
KB = 256
LEAD = 3

SC_B, SC_C, SC_H, ZCOL = 0, D, 2 * D, 3 * D
XBC_COL = 4 * D
DT_COL = 4 * D + SSM_XBC

UNITS = [("xbc", 12), ("scp", 16), ("scb", 8), ("z", 8), ("out0", 16), ("up0", 44), ("dn0", 22),
         ("fqk", 16), ("fv", 8), ("fo", 8), ("up1", 44), ("dn1", 22), ("qkv", 12), ("o", 8),
         ("mu0", 32), ("md0", 32), ("gu", 24), ("gv", 24), ("go", 24), ("mu1", 32), ("md1", 32)]
U0 = {}
_n = 0
for _name, _k in UNITS:
    U0[_name] = _n
    _n += _k
TOTAL_UNITS = _n
NUNITS = dict(UNITS)
END = {k: U0[k] + NUNITS[k] for k in U0}
JIT = [("out0", 8), ("dn0", 11), ("fo", 4), ("dn1", 11), ("o", 4), ("md0", 16), ("go", 12), ("md1", 16)]
PAIRS = dict(JIT)
A0 = {}
_n = 0
for _name, _k in JIT:
    A0[_name] = _n
    _n += 2 * _k


def host_constants():
    i = np.arange(P)
    c = np.zeros((P, 4, P), np.float32)
    c[:, 0] = i[:, None] == i[None, :]
    c[:, 1] = i[:, None] <= i[None, :]
    c[:, 2] = 1.0
    c[:, 3] = np.where(i[None, :] <= i[:, None], 0.0, -1e30)
    t = np.arange(T)
    row = (t // 64 - (T // 64) // 2).astype(np.float32)
    col = (t % 64 - 32).astype(np.float32)
    inv = (np.float32(10000.0) ** (-np.arange(16, dtype=np.float32) / np.float32(16))).astype(np.float32)
    ang = np.concatenate([row[:, None] * inv, col[:, None] * inv], -1).astype(np.float32)
    cs = np.zeros((T, 2, HD), np.float32)
    cs[:, 0] = np.repeat(np.cos(ang), 2, axis=-1)
    cs[:, 1, 0::2] = -np.sin(ang)
    cs[:, 1, 1::2] = np.sin(ang)
    onehot = np.zeros((P, 16), np.float32)
    for b in range(4):
        onehot[32 * b:32 * b + 16] = np.eye(16)
    return c, cs, onehot


def build(nc, a, out):
    with ExitStack() as ctx:
        build_in(ctx, nc, a, out)


def build_in(ctx, nc, a, out):
    def sb(name, shape, dt=F32):
        return ctx.enter_context(nc.sbuf_tensor(name, shape, dt))

    base = (nc.sbuf_base + 31) // 32 * 32
    slab_words = (nc.sbuf_usable_end - base) // 4 // 8 * 8
    ctx.enter_context(nc.sbuf_tensor("slab", [P, slab_words], F32))
    cursor = [base]

    def at(name, shape, offset, dt=F32):
        return nc.alloc_sbuf_tensor_at(name, shape, dt, offset=offset)

    def take(name, shape, dt=F32):
        words = int(np.prod(shape[1:]))
        t = at(name, shape, cursor[0], dt)
        cursor[0] += (4 * words + 31) // 32 * 32
        assert cursor[0] <= base + 4 * slab_words, (name, cursor[0] - base - 4 * slab_words)
        return t

    raw = take("raw", [P, RING, UNIT])
    whi = take("whi", [P, RING, UNIT], F32R)
    wlo = take("wlo", [P, RING, UNIT], F32R)
    xt_at = cursor[0]
    xhi = take("xhi", [P, KD, T], F32R)
    xlo = take("xlo", [P, KD, T], F32R)
    act_at = cursor[0]
    ahi = take("ahi", [P, 2, 2, T], F32R)
    alo = take("alo", [P, 2, 2, T], F32R)
    xres = take("xres", [P, NT, D])
    arena_at = cursor[0]
    ARENA = 86 * KB
    take("arena", [P, ARENA])

    def arena(name, shape, kb):
        assert kb * KB + int(np.prod(shape[1:])) <= ARENA, name
        return at(name, shape, arena_at + 1024 * kb)

    def scratch(name, shape, kb):
        assert kb * KB + int(np.prod(shape[1:])) <= 32 * KB, name
        return at(name, shape, xt_at + 1024 * kb)

    def actmem(name, shape, kb):
        assert kb * KB + int(np.prod(shape[1:])) <= 16 * KB, name
        return at(name, shape, act_at + 1024 * kb)

    consts = take("consts", [P, 4, P])
    ident, tri, ones, cmask = (consts[:, i] for i in range(4))
    NTAB = 6
    tab = take("tab", [P, NTAB * P])
    wf_hi_t = take("wf_hi_t", [P, KD, 16], F32R)
    wf_lo_t = take("wf_lo_t", [P, KD, 16], F32R)
    onehot = take("onehot", [P, 16])
    small = take("small", [P, 4, 16])
    modc = take("modc", [P, 2, 48])
    ccol = take("ccol", [P, KD])
    nscale = take("nscale", [P, 4, KD])
    stats = take("stats", [P, NT, 6, 6])
    mv = take("mv", [P, NT, 2])
    sumsq = take("sumsq", [P, NT, 2])
    std = take("std", [P, NT])
    rstd = take("rstd", [P, NT])
    eps_ln = take("eps_ln", [P, 2])
    rowst = take("rowst", [P, 3, 64])
    ps = ctx.enter_context(nc.psum_tensor("ps", [P, 8, 512], F32))

    tabraw = arena("tabraw", [P, NTAB, P], 60)
    wf_raw = arena("wf_raw", [P, KD, 16], 84)
    ya_yb = arena("ya_yb", [P, 16, T], 0)
    zs = arena("zs", [P, NT, D], 16)
    xbcT = arena("xbcT", [P, 12, T], 32)
    y_tok = arena("y_tok", [P, NT, D], 32)
    xs_tok = arena("xs_tok", [P, NT, D], 56)
    b_tok = arena("b_tok", [P, NT, 256], 72)
    cv0 = arena("cv0", [P, 2, T], 76)
    hb = actmem("hb", [P, 2, T], 0)
    pb = actmem("pb", [P, 2, T], 4)
    sm = actmem("sm", [P, 16, NT, 16], 12)
    gbuf = scratch("gbuf", [P, 16, P], 0)
    mbuf = scratch("mbuf", [P, 16, P], 8)
    xdt = scratch("xdt", [P, D], 16)
    xdd = scratch("xdd", [P, D], 20)
    prev = scratch("prev", [P, D], 24)
    cbm = scratch("cbm", [P, 2, P], 28)
    ssd_sq = scratch("ssd_sq", [P, HALF], 29)
    nrm = arena("nrm", [P, NT, D], 64)
    xf = arena("xf", [P, 2, T], 80)
    gb = actmem("gb", [P, 2, D], 0)
    gate = scratch("gate", [P, D], 0)
    junk = scratch("junk", [P, D], 4)
    gdiag = scratch("gdiag", [P, KD, P], 8)
    hid_ff = arena("hid_ff", [P, NFF, T], 0)
    gt = arena("gt", [P, 2, T], 44)
    ut = arena("ut", [P, 2, T], 48)
    gs = arena("gs", [P, 2, T], 52)
    acc = arena("acc", [P, 48, P], 56)
    ADA_N = 6 * D // 4
    adaraw = [actmem("adaraw0", [P, ADA_N], 8), arena("adaraw1", [P, ADA_N], 80)]
    qh = arena("qh", [P, 16, T], 0)
    kh = arena("kh", [P, 16, T], 32)
    vtok = arena("vtok", [P, NT, D], 64)
    cumx = actmem("cumx", [P, T], 10)
    oT1 = scratch("oT1", [P, KD, T], 0)
    pbuf = arena("pbuf", [P, 3, T], 80)
    ptb1 = actmem("ptb1", [P, 2, NT, T], 0)
    q_tok = arena("q_tok", [P, NT, D], 0)
    k_tok = arena("k_tok", [P, NT, 256], 16)
    v2 = arena("v2", [P, NT, 256], 20)
    qT2 = arena("qT2", [P, KD, T], 24)
    kT2 = arena("kT2", [P, 2, T], 40)
    cs = arena("cs", [P, NT, 2, HD], 44)
    qkg = arena("qkg", [P, 2, HD], 46)
    oT2 = arena("oT2", [P, KD, T], 48)
    sqb = arena("sqb", [P, NT, T], 64)
    qn = arena("qn", [P, T], 72)
    ra = arena("ra", [P, T], 74)
    rb = arena("rb", [P, T], 76)
    hsum = arena("hsum", [P, 3, NT, 8], 78)
    ptb2 = scratch("ptb2", [P, 2, NT, T], 0)
    hid_mlp = arena("hid_mlp", [P, NMLP, T], 0)
    relu = arena("relu", [P, 2, T], 80)
    uT = arena("uT", [P, NGM, T], 0)
    vt = [arena(f"vt{t}", [P, GM_HALF], 48 + 12 * t) for t in range(3)] + [actmem("vt3", [P, GM_HALF], 0)]
    bb = actmem("bb", [P, 2, HALF], 12)
    wsT = scratch("wsT", [P, GM_GROUPS, P], 0)
    rs_b = scratch("rs_b", [P, GM_GROUPS, P], 8)
    bs_b = scratch("bs_b", [P, GM_GROUPS, P], 16)
    wsraw = scratch("wsraw", [P, GM_GROUPS, P], 24)
    gz = scratch("gz", [P, 2, T], 24)
    gk = scratch("gk", [P, 2, P], 28)

    def sem(name):
        return ctx.enter_context(nc.semaphore(name))

    raw_in = [sem(f"raw_in{i}") for i in range(RING)]
    w_hi, w_lo = sem("w_hi"), sem("w_lo")
    unit_done = sem("unit_done")
    a_hi, a_lo = sem("a_hi"), sem("a_lo")
    consts_in, x_in, small_in = sem("consts_in"), sem("x_in"), sem("small_in")
    tab_zero, tab_in, tab_tp, tab_ready = sem("tab_zero"), sem("tab_in"), sem("tab_tp"), sem("tab_ready")
    prep = sem("prep")
    wf_hi, wf_lo, f_mm = sem("wf_hi"), sem("wf_lo"), sem("f_mm")
    res_add, gated = sem("res_add"), sem("gated")
    stat_done, aggr_done, sq_done, std_done, rstd_done = (
        sem("stat_done"), sem("aggr_done"), sem("sq_done"), sem("std_done"), sem("rstd_done"))
    nrm_done, xt_tp, xt_ev, xt_hi, xt_lo = (
        sem("nrm_done"), sem("xt_tp"), sem("xt_ev"), sem("xt_hi"), sem("xt_lo"))
    gb_in, res_mul, res_done = sem("gb_in"), sem("res_mul"), sem("res_done")
    xbc_aff, xbc_conv, xbc_silu = sem("xbc_aff"), sem("xbc_conv"), sem("xbc_silu")
    sc_h, sc_step, scb_done, z_done = sem("sc_h"), sem("sc_step"), sem("scb_done"), sem("z_done")
    dts, dta = sem("dt_dve"), sem("dt_act")
    tok_tp, tok_ev_a, tok_ev_d = sem("tok_tp"), sem("tok_ev_act"), sem("tok_ev_dve")
    cums_mm, ssd_g, ssd_r, ssd_d, ssd_e, ssd_cbm, ssd_m, ssd_x, ssd_mm, ssd_y, ssd_prev = (
        sem(n) for n in ("cums_mm", "ssd_g", "ssd_r", "ssd_d", "ssd_e", "ssd_cbm", "ssd_m", "ssd_x", "ssd_mm",
                         "ssd_y", "ssd_prev"))
    gt_u, gt_sq, gt_std, gt_r, gt_n, gt_tp, gt_ev = (
        sem(n) for n in ("gate_u", "gate_sq", "gate_std", "gate_r", "gate_n", "gate_tp", "gate_ev"))
    ff_act, ff_dve = sem("ff_act"), sem("ff_dve")
    ada_in = [sem("ada_in0"), sem("ada_in1")]
    ada_acc, mod_mm, mod_done = sem("ada_acc"), sem("mod_mm"), sem("mod_done")
    fl_dve, fl_act, cum_mm, aug = sem("fl_dve"), sem("fl_act"), sem("cum_mm"), sem("aug")
    fqk_ev, fv_ev = sem("fqk_ev"), sem("fv_ev")
    at_s, at_max, at_exp, at_rinv, at_p, at_tp, at_pt, at_pv, at_o = (
        sem(n) for n in ("at_scores", "at_max", "at_exp", "at_rinv", "at_p", "at_tp", "at_pt", "at_pv", "at_o"))
    q_sq, q_sum, q_std, q_step, v_ev, q_tp, q_ev, qkg_in = (
        sem(n) for n in ("q_sq", "q_sum", "q_std", "q_step", "v_ev", "q_tp", "q_ev", "qkg_in"))
    gdiag_done, gate_mm, gate_ev = sem("gdiag_done"), sem("gate_mm2"), sem("gate_ev2")
    relu_done, mlp_done = sem("relu_done"), sem("mlp_done")
    gu_ev, bb_in0, bb_in1, gv_add, gv_gelu, gv_stat, gv_aggr, gv_std, gv_rstd, gv_nrm = (
        sem(n) for n in ("gu_ev", "bb_in0", "bb_in1", "gv_add", "gv_gelu", "gv_stat", "gv_aggr", "gv_std",
                         "gv_rstd", "gv_nrm"))
    bb_in = [bb_in0, bb_in1]
    ws_in, bs_in, ws_tp, ws_ev, rs_mm, rs_ev, gm_mm, gm_k, gm_z, gm_u = (
        sem(n) for n in ("ws_in", "bs_in", "ws_tp", "ws_ev", "rs_mm", "rs_ev", "gm_mm", "gm_k", "gm_z", "gm_u"))
    out_in = sem("out_in")

    def rows(ap):
        return ap.rearrange("(c p) -> c p", p=P)

    blocks = [[("scw", a["sc_conv_w"][0].rearrange("k (c p) -> (k c) p", p=P), 24),
               ("ssmw", a["ssm_conv_w"][0].rearrange("k (c p) -> (k c) p", p=P), 48),
               ("ssmb", rows(a["ssm_conv_b"][0]), 12), ("normg", rows(a["ssm_norm_g"][0]), 8),
               ("n1g", a["norm1_g_2"].rearrange("l (c p) -> (l c) p", p=P), 16),
               ("n2g", a["norm2_g_2"].rearrange("l (c p) -> (l c) p", p=P), 16)]]
    for i in range(2):
        cw = a["ffn_conv_w"][i].rearrange("k (h c p) -> k h c p", p=P, h=2)
        blocks.append([(f"cw{i}_0u", cw[0, 0], 22), (f"cw{i}_0g", cw[0, 1], 22), (f"cw{i}_1u", cw[1, 0], 22),
                       (f"cw{i}_1g", cw[1, 1], 22), (f"lnm{i}g", rows(a["ln_mix_g"][i]), 8),
                       (f"lnm{i}b", rows(a["ln_mix_b"][i]), 8)])
        cb = a["ffn_conv_b"][i].rearrange("(h c p) -> h c p", p=P, h=2)
        blocks.append([(f"cw{i}_2u", cw[2, 0], 22), (f"cw{i}_2g", cw[2, 1], 22), (f"cb{i}u", cb[0], 22),
                       (f"cb{i}g", cb[1], 22), (f"lnf{i}g", rows(a["ln_ffn_g"][i]), 8),
                       (f"lnf{i}b", rows(a["ln_ffn_b"][i]), 8),
                       [("gbin", rows(a["gmlp_b_in_2"][0, 0:GM_HALF]), 24),
                        ("glng", rows(a["gmlp_ln_g_2"][0]), 24)][i]])
    blocks.append([("adab", a["ada_b_2"].rearrange("l (c p) -> (l c) p", p=P), 96),
                   ("glnb", rows(a["gmlp_ln_b_2"][0]), 24), ("c", a["c_2"][0].rearrange("(c p) -> c p", p=P), 8)])
    TAB, loads = {}, []
    for b, items in enumerate(blocks):
        r = 0
        for name, ap, k in items:
            TAB[name] = b * P + r
            loads.append((b, r, k, ap))
            r += k
        assert r <= P
    assert len(blocks) == NTAB

    def col(name, i=0):
        if isinstance(i, int):
            return tab[:, TAB[name] + i:TAB[name] + i + 1]
        return tab[:, bass.ds(i + TAB[name], 1)]

    def kview(w):
        return w.rearrange("(c p) n -> p c n", p=P)

    w_in0, w_out0 = kview(a["sc_ssm_w_in"][0]), kview(a["sc_ssm_w_out"][0])
    w_fox, w_fo = kview(a["fox_w_in"][0]), kview(a["fox_w_out"][0])
    w_up = [kview(a["ffn_w_up"][i]) for i in range(2)]
    w_dn = [kview(a["ffn_w_down"][i]) for i in range(2)]
    w_qkv, w_o = kview(a["attn_w_qkv_2"][0]), kview(a["attn_w_o_2"][0])
    w_gin, w_gout = kview(a["gmlp_w_in_2"][0]), kview(a["gmlp_w_out_2"][0])
    w_mi = [kview(a["mlp_w_in_2"][i]) for i in range(2)]
    w_mo = [kview(a["mlp_w_out_2"][i]) for i in range(2)]
    w_ada = [a["ada_w_2"][i].rearrange("(k p) (m n) -> p k m n", p=P, m=4) for i in range(2)]

    def run(eng, n, body):
        q, r = divmod(n, RING)
        if q > 1:
            with eng.Fori(0, q) as i:
                for j in range(RING):
                    body(i * RING + j, j)
        else:
            for j in range(q * RING):
                body(j, j)
        for j in range(r):
            body(q * RING + j, j)

    def wait_raw(eng, start, e, j):
        s = (start + j) % RING
        if isinstance(e, int):
            eng.wait_ge(raw_in[s], 16 * ((start + e) // RING + 1))
        else:
            eng.wait_ge(raw_in[s], (e - j) * 4 + 16 * ((start + j) // RING + 1))

    def sp_value(sp, x):
        if isinstance(x, int):
            return x
        v = sp.snap(x)
        sp.lower_val(v * 4)
        return v

    def f_src(sp, w, c0, e):
        return w[:, :, bass.ds(sp_value(sp, e * P + c0), P)]

    def f_dst(s):
        return raw[:, s].rearrange("p (k n) -> p k n", k=KD)

    def t_dst(s):
        return raw[:, s].rearrange("p (k n) -> p k n", k=2)

    def t_src(sp, w, pair, c0):
        return w[:, bass.ds(sp_value(sp, pair * 2), 2), c0:c0 + HALF]

    def sp_load(sp, start, e, j, src, dst):
        u = start + e
        s = (start + j) % RING
        if not isinstance(u, int):
            sp.wait_ge(w_lo, e + (start - RING + 1))
        elif u >= RING:
            sp.wait_ge(w_lo, u - RING + 1)
        sp.dma_start(dst, src).then_inc(raw_in[s], 16)

    def sp_f(sp, name, w, c0, n=None, off=0):
        start, n = U0[name] + off, n or NUNITS[name]
        if start == 0:
            for e in range(RING):
                sp_load(sp, 0, e, e, f_src(sp, w, c0, e), f_dst(e))
            start, n, c0 = RING, n - RING, c0 + RING * P
        run(sp, n, lambda e, j: sp_load(sp, start, e, j, f_src(sp, w, c0, e), f_dst((start + j) % RING)))

    def sp_pairs(sp, name, w, c_even, c_odd, n):
        start = U0[name]

        def body(i):
            for j in range(RING):
                c0 = (c_even, c_odd)[j % 2] + (j // 2) * P
                s = (start + j) % RING
                at_col = sp_value(sp, i * (2 * P) + c0)
                sp.wait_ge(w_lo, i * RING + (start + j - RING + 1))
                sp.dma_start(f_dst(s), w[:, :, bass.ds(at_col, P)]).then_inc(raw_in[s], 16)

        with sp.Fori(0, n // RING) as i:
            body(i)

    def sp_t(sp, name, w, pairs, cols):
        for h, c0 in enumerate(cols):
            start = U0[name] + h * pairs
            run(sp, pairs, lambda e, j: sp_load(sp, start, e, j, t_src(sp, w, e, c0), t_dst((start + j) % RING)))

    block = ctx.enter_context(nc.Block())

    @block.sync
    def _(sp):
        sp_f(sp, "xbc", w_in0, XBC_COL)
        sp_pairs(sp, "scp", w_in0, SC_C, SC_H, 16)
        sp_f(sp, "scb", w_in0, SC_B)
        sp_t(sp, "z", w_in0, 4, [ZCOL, ZCOL + HALF])
        sp_t(sp, "out0", w_out0, 8, [0, HALF])
        sp_pairs(sp, "up0", w_up[0], D_FF, 0, 44)
        sp_t(sp, "dn0", w_dn[0], 11, [0, HALF])
        sp_f(sp, "fqk", w_fox, 0)
        sp_t(sp, "fv", w_fox, 4, [2 * D, 2 * D + HALF])
        sp_t(sp, "fo", w_fo, 4, [0, HALF])
        sp_pairs(sp, "up1", w_up[1], D_FF, 0, 44)
        sp_t(sp, "dn1", w_dn[1], 11, [0, HALF])
        sp_t(sp, "qkv", w_qkv, 4, [D, 0, HALF])
        sp_t(sp, "o", w_o, 4, [0, HALF])
        sp_f(sp, "mu0", w_mi[0], 0)
        sp_t(sp, "md0", w_mo[0], 16, [0, HALF])
        sp_f(sp, "gu", w_gin, 0)
        start = U0["gv"]
        with sp.Fori(0, 6) as h:
            for j in range(4):
                s = (start + j) % RING
                at_col = sp_value(sp, h * HALF + GM_HALF)
                sp.wait_ge(w_lo, h * 4 + (start + j - RING + 1))
                sp.dma_start(t_dst(s), w_gin[:, 2 * j:2 * j + 2, bass.ds(at_col, HALF)]).then_inc(raw_in[s], 16)
        sp_t(sp, "go", w_gout, 12, [0, HALF])
        sp_f(sp, "mu1", w_mi[1], 0)
        sp_t(sp, "md1", w_mo[1], 16, [0, HALF])
        sp.wait_ge(res_add, 64)
        sp.dma_start(out[0].rearrange("(t p) d -> p t d", p=P), xres[:]).then_inc(out_in, 16)
        sp.wait_ge(out_in, 16)

    @block.gpsimd
    def _(pool):
        with pool.Fori(0, TOTAL_UNITS // RING) as i:
            for j in range(RING):
                pool.wait_ge(w_hi, i * RING + (j + 1))
                pool.tensor_tensor(wlo[:, j], raw[:, j], whi[:, j].bitcast(F32), ALU.subtract).then_inc(w_lo, 1)

    LAST = TOTAL_UNITS

    def act_whi(act, start, e, j):
        u, s = start + e, (start + j) % RING
        if isinstance(u, int) and u >= LAST:
            return
        wait_raw(act, start, e, j)
        if not isinstance(u, int):
            act.wait_ge(unit_done, e + (start - RING + 1))
        elif u >= RING:
            act.wait_ge(unit_done, u - RING + 1)
        act.activation(whi[:, s], raw[:, s], ACT.Copy).then_inc(w_hi, 1)

    AHEAD = 3

    def bank_f(j):
        return 4 + j % 4

    def act_params(act):
        n = [0]

        def load(dst, src, s):
            act.dma_start(dst, src).then_inc(s, 16)
            n[0] += 16

        act.dma_start(xres[:], a["x"][0].rearrange("(t p) d -> p t d", p=P)).then_inc(x_in, 16)
        act.dma_start(consts[:], a["consts"]).then_inc(consts_in, 16)
        act.dma_start(onehot[:], a["onehot"]).then_inc(consts_in, 16)
        act.wait_ge(tab_zero, 1)
        for b, r, k, ap in loads:
            load(tabraw[r:r + k, b], ap, tab_in)
        for i, name in enumerate(("ssm_dt_bias", "ssm_a_log", "ssm_d", "fox_b_f")):
            act.dma_start(small[:, i], a[name].to_broadcast([P, 16])).then_inc(small_in, 16)
        act.dma_start(wf_raw[:], w_in0[:, :, DT_COL:DT_COL + 16]).then_inc(small_in, 16)

    TAB_LOADS = 16 * len(loads)

    def act_table(act):
        act.wait_ge(tab_tp, 1)
        act.activation(tab[:, 0:4 * P], ps[:, 0, :], ACT.Copy).then_inc(tab_ready, 1)
        act.wait_ge(tab_tp, 2)
        act.activation(tab[:, 4 * P:6 * P], ps[:, 1, 0:2 * P], ACT.Copy).then_inc(tab_ready, 1)
        act.wait_ge(tab_ready, 2)
        act.activation(ccol[:], tab[:, TAB["c"]:TAB["c"] + KD], ACT.Silu).then_inc(prep, 1)
        act.wait_ge(small_in, 16 * 5)
        act.activation(wf_hi_t[:], wf_raw[:], ACT.Copy).then_inc(wf_hi, 1)

    def act_xt(act, q, scale, bias):
        for k in range(KD):
            act.wait_ge(xt_tp, KD * q + k + 1)
            if k >= 2:
                act.wait_ge(xt_lo, KD * q + k - 1)
            if scale is None:
                act.activation(xf[:, k % 2], ps[:, k % 4], ACT.Copy).then_inc(xt_ev, 1)
            else:
                act.activation(xf[:, k % 2], ps[:, k % 4], ACT.Identity, scale=scale(k), bias=bias(k)).then_inc(xt_ev, 1)

    def act_xbc(act):
        S = U0["xbc"]

        def unit(e, j):
            b = j % 2
            act_whi(act, S + AHEAD, e, j)
            act.wait_ge(unit_done, e + (S + 1))
            act.activation(cv0[:, b], ps[:, bank_f(j)], ACT.Identity, scale=col("ssmw", e + 36 if isinstance(e, int) else e + 36),
                           bias=col("ssmb", e)).then_inc(xbc_aff, 1)
            act.wait_ge(xbc_conv, e * 3 + 3)
            dst = xbcT[:, e:e + 1] if isinstance(e, int) else xbcT[:, bass.ds(e, 1)]
            act.activation(dst, cv0[:, b:b + 1], ACT.Silu).then_inc(xbc_silu, 1)

        run(act, 12, unit)

    def act_soft(act, s_dve, s_act):
        act.wait_ge(s_dve, 3)
        act.activation(sm[:, 3], sm[:, 2], ACT.Exp, scale=-1.0).then_inc(s_act, 1)
        act.wait_ge(s_dve, 4)
        act.activation(sm[:, 7], sm[:, 4], ACT.Ln).then_inc(s_act, 1)

    def act_scp(act):
        S = U0["scp"]
        with act.Fori(0, 4) as i:
            for j in range(RING):
                act_whi(act, S + AHEAD, i * RING + j, j)
                if j % 2:
                    act.wait_ge(unit_done, i * RING + (S + j + 1))
                    act.wait_ge(sc_step, i * 8 + (4 * (j // 2) + 1))
                    act.activation(hb[:, j // 2], ps[:, bank_f(j)], ACT.Copy).then_inc(sc_h, 1)

    def act_plain(act, name):
        S, n = U0[name], NUNITS[name]
        run(act, n, lambda e, j: act_whi(act, S + AHEAD, e, j))

    def act_z(act):
        S = U0["z"]
        for e in range(9):
            if e < 8:
                act_whi(act, S + AHEAD, e, e % 4)
            if e and e % 4 == 0:
                h = e // 4 - 1
                act.wait_ge(unit_done, S + 4 * h + 4)
                for t in range(NT):
                    act.activation(zs[:, t, h * HALF:(h + 1) * HALF], ps[:, 4 * h + t], ACT.Silu).then_inc(z_done, 1)

    def act_ssd(act):
        for g in range(0, 12, 2):
            t, r = divmod(g, 3)
            act.wait_ge(tok_tp, g + 1)
            if r < 2:
                act.activation(xs_tok[:, t, r * HALF:(r + 1) * HALF], ps[:, g % 4], ACT.Copy).then_inc(tok_ev_a, 1)
            else:
                act.activation(b_tok[:, t], ps[:, g % 4, 0:256], ACT.Copy).then_inc(tok_ev_a, 1)
        act.wait_ge(dts, 15)
        act.activation(sm[:, 12], sm[:, 15], ACT.Exp).then_inc(dta, 1)
        act.activation(sm[:, 13], sm[:, 11], ACT.Exp).then_inc(dta, 1)
        act.activation(sm[:, 14], ps[:, 1, 64:128].rearrange("p (c h) -> p c h", c=NT), ACT.Exp).then_inc(dta, 1)
        for c in range(NT):
            act.wait_ge(ssd_d, 2 * c + 2)
            act.activation(mbuf[:], mbuf[:], ACT.Exp).then_inc(ssd_e, 1)
        for t in range(NT):
            act.wait_ge(gt_u, t + 1)
            for g in range(2):
                if t or g:
                    act.wait_ge(gt_sq, 2 * t + g)
                act.activation(ssd_sq[:], y_tok[:, t, g * HALF:(g + 1) * HALF], ACT.Square,
                               accum_out=sumsq[:, t, g:g + 1]).then_inc(gt_sq, 1)
        act.wait_ge(gt_sq, 8)
        act.activation(mv[:], sumsq[:], ACT.Sqrt, scale=1.0 / HALF, bias=eps_ln[:, 0:1]).then_inc(gt_std, 1)
        for k in range(KD):
            act.wait_ge(gt_tp, k + 1)
            act.activation(ya_yb[:, 8 + k], ps[:, k % 4], ACT.Copy, scale=col("normg", k)).then_inc(gt_ev, 1)

    def act_jit(act, name, src, after_h0=None, last=False):
        H, S, A = PAIRS[name], U0[name], A0[name]

        def split(m0, e, j, k0):
            k = k0 + e
            x = src[:, 2 * k:2 * k + 2] if isinstance(k, int) else src[:, bass.ds(e * 2 + 2 * k0, 2)]
            act.activation(ahi[:, (m0 + j) % 2], x, ACT.Copy).then_inc(a_hi, 1)

        def step(m0, k0, e, j, whi_too=True):
            if whi_too:
                act_whi(act, S + m0 + 1, e, j)
            act.wait_ge(unit_done, e + (S + m0 - 1))
            split(m0, e, j, k0)

        split(0, 0, 0, 0)
        split(1, 0, 0, 1)
        run(act, H - 2, lambda e, j: step(2, 2, e, j))
        for e in range(3):
            step(H + e, e, 0, 0)
        if after_h0:
            after_h0()
        n = H - 3 - (1 if last else 0)
        if n:
            run(act, n, lambda e, j: step(H + 3, 3, e, j))
        if last:
            step(2 * H - 1, H - 1, 0, 0, whi_too=False)
        else:
            act_whi(act, S + 2 * H + 1, 0, 0)
            act_whi(act, S + 2 * H + 2, 0, 0)

    def act_ln(act, q, name, g_ap, b_ap):
        act.wait_ge(unit_done, END[name])
        act.dma_start(gb[:, 0], g_ap.to_broadcast([P, D])).then_inc(gb_in, 16)
        act.dma_start(gb[:, 1], b_ap.to_broadcast([P, D])).then_inc(gb_in, 16)
        act.wait_ge(aggr_done, NT * (q + 1))
        act.activation(std[:], mv[:, :, 1], ACT.Sqrt, bias=eps_ln[:, 0:1]).then_inc(std_done, 1)

    def act_ffn(act, L):
        S, FA, FD = U0[f"up{L}"], 66 * L, 110 * L
        for lo, hi, ada in ((0, 8, True), (8, 11, False)):
            with act.Fori(lo, hi) as i:
                for b in range(2):
                    pr = i * 2 + b
                    act_whi(act, S + AHEAD, i * RING + 2 * b, 2 * b)
                    act.wait_ge(unit_done, i * RING + (S + 2 * b + 1))
                    act.activation(gt[:, b], ps[:, bank_f(2 * b)], ACT.Identity, scale=col(f"cw{L}_2g", pr),
                                   bias=col(f"cb{L}g", pr)).then_inc(ff_act, 1)
                    if ada:
                        for s in range(2):
                            act.wait_ge(ada_acc, i * 4 + (36 * L + 2 * b + s + 3))
                            act.dma_start(adaraw[s][:], w_ada[L][:, bass.ds(i, 1), 2 * b + s]).then_inc(ada_in[s], 16)
                    act.wait_ge(ff_dve, i * 10 + (FD + 5 * b + 2))
                    act.activation(gs[:, b], gt[:, b], ACT.Silu).then_inc(ff_act, 1)
                    act_whi(act, S + AHEAD, i * RING + 2 * b + 1, 2 * b + 1)
                    act.wait_ge(unit_done, i * RING + (S + 2 * b + 2))
                    act.activation(ut[:, b], ps[:, bank_f(2 * b + 1)], ACT.Identity, scale=col(f"cw{L}_2u", pr),
                                   bias=col(f"cb{L}u", pr)).then_inc(ff_act, 1)

    def act_fox_qk(act):
        S = U0["fqk"]
        for k0, dst, scale in ((0, qh, HD ** -0.5), (8, kh, 1.0)):
            def unit(e, j):
                act_whi(act, S + k0 + AHEAD, e, j)
                act.wait_ge(unit_done, e + (S + k0 + 1))
                for b in range(2):
                    r = slice(64 * b, 64 * b + 64)
                    d = dst[r, 2 * e + b:2 * e + b + 1] if isinstance(e, int) else dst[r, bass.ds(e * 2 + b, 1)]
                    act.activation(d, ps[r, bank_f(j):bank_f(j) + 1], ACT.Copy, scale=scale).then_inc(fqk_ev, 1)

            run(act, 8, unit)

    def act_attn(act, A, ptb, causal):
        B = 64 * A
        for n in range(64 + LEAD):
            if n < 64:
                N = (n % 4 + 1) * P if causal else T
                act.wait_ge(at_max, B + n + 1)
                if n >= 3:
                    act.wait_ge(at_tp, B + n - 2)
                act.activation(pbuf[:, n % 3, 0:N], ps[:, n % 3, 0:N], ACT.Exp, bias=rowst[:, 0, n:n + 1],
                               accum_out=rowst[:, 1, n:n + 1]).then_inc(at_exp, 1)
            m = n - LEAD
            if m >= 0:
                h, i = divmod(m, 4)
                c = i + 1 if causal else NT
                act.wait_ge(at_tp, B + m + 1)
                if i == 0 and h >= 2:
                    act.wait_ge(at_pv, 16 * A + h - 1)
                act.activation(ptb[:, h % 2, 0:c, i * P:(i + 1) * P],
                               ps[:, 3 + m % 2, 0:c * P].rearrange("p (c q) -> p c q", c=c), ACT.Copy).then_inc(at_pt, 1)

    def act_square(act, s, h, tiles_ready):
        for t in range(NT):
            tiles_ready(t)
            if t:
                act.wait_ge(sq_done, 8 * s + 4 * h + t)
            act.activation(junk[:, h * HALF:(h + 1) * HALF], xres[:, t, h * HALF:(h + 1) * HALF], ACT.Square,
                           accum_out=sumsq[:, t, h:h + 1]).then_inc(sq_done, 1)

    def act_rms(act, s):
        act.wait_ge(aggr_done, 16 + s + 1)
        act.activation(std[:], mv[:, :, 0], ACT.Sqrt, scale=1.0 / D, bias=eps_ln[:, 1:2]).then_inc(std_done, 1)

    def act_qkv(act):
        S = U0["qkv"]
        act.dma_start(cs[:], a["cs"].rearrange("(t p) a d -> p t a d", p=P)).then_inc(qkg_in, 16)
        act.dma_start(qkg[:, 0], a["attn_q_norm_g_2"].to_broadcast([P, HD])).then_inc(qkg_in, 16)
        act.dma_start(qkg[:, 1], a["attn_k_norm_g_2"].to_broadcast([P, HD])).then_inc(qkg_in, 16)
        for e in range(13):
            if e < 12:
                act_whi(act, S + AHEAD, e, e % 4)
            if e and e % 4 == 0:
                hh = e // 4 - 1
                nh = 4 if hh == 0 else 8
                act.wait_ge(unit_done, S + 4 * hh + 4)
                if hh:
                    act.wait_ge(q_sum, 5 * hh)
                for t in range(NT):
                    act.activation(sqb[:, t, 0:nh * HD], ps[:, 4 * (hh % 2) + t, 0:nh * HD], ACT.Square).then_inc(q_sq, 1)
                    if hh == 0:
                        act.activation(v2[:, t], ps[:, t, 256:512], ACT.Copy).then_inc(v_ev, 1)
                act.wait_ge(q_sum, 5 * hh + 4)
                act.activation(hsum[:, 1, :, 0:nh], hsum[:, 0, :, 0:nh], ACT.Sqrt, scale=1.0 / HD,
                               bias=eps_ln[:, 1:2]).then_inc(q_std, 1)
        for r in range(10):
            act.wait_ge(q_tp, r + 1)
            if r < 2:
                act.activation(kT2[:, r], ps[:, 4 + r % 4], ACT.Copy).then_inc(q_ev, 1)
            else:
                for b in range(2):
                    h = 2 * (r - 2) + b
                    g = h // 4
                    kb = 64 * (g % 2)
                    act.activation(qT2[kb:kb + 64, (g // 2) * 4 + h % 4], ps[64 * b:64 * b + 64, 4 + r % 4],
                                   ACT.Copy, scale=HD ** -0.5).then_inc(q_ev, 1)

    def act_gate(act, s):
        act.wait_ge(gate_mm, s + 1)
        act.activation(gate[:], ps[:, 4:6], ACT.Copy).then_inc(gate_ev, 1)

    def act_mlp(act, L):
        S = U0[f"mu{L}"]

        def unit(e, j):
            act_whi(act, S + AHEAD, e, j)
            act.wait_ge(unit_done, e + (S + 1))
            v = e + (32 * L - 1)
            if not isinstance(v, int) or v > 0:
                act.wait_ge(mlp_done, v)
            act.activation(relu[:, j % 2], ps[:, bank_f(j)], ACT.Relu).then_inc(relu_done, 1)

        for e in range(4):
            unit(e, e)
        with act.Fori(1, 8) as i:
            for j in range(4):
                unit(i * 4 + j, j)

    def act_gu(act):
        S = U0["gu"]

        def unit(e, j):
            act_whi(act, S + AHEAD, e, j)
            act.wait_ge(unit_done, e + (S + 1))
            d = uT[:, e:e + 1] if isinstance(e, int) else uT[:, bass.ds(e, 1)]
            act.activation(d, ps[:, bank_f(j):bank_f(j) + 1], ACT.Gelu, bias=col("gbin", e)).then_inc(gu_ev, 1)

        run(act, 24, unit)

    def act_gv(act):
        S = U0["gv"]

        def load_bias(hh):
            if hh >= 2:
                act.wait_ge(gv_add, 4 * (hh - 1))
            c0 = GM_HALF + hh * HALF
            act.dma_start(bb[:, hh % 2], a["gmlp_b_in_2"][:, c0:c0 + HALF].to_broadcast([P, HALF])
                          ).then_inc(bb_in[hh % 2], 16)

        load_bias(0)
        load_bias(1)
        for e in range(25):
            if e < 24:
                act_whi(act, S + AHEAD, e, e % 4)
            if e and e % 4 == 0:
                hh = e // 4 - 1
                for t in range(NT):
                    act.wait_ge(gv_add, 4 * hh + t + 1)
                    v = vt[t][:, hh * HALF:(hh + 1) * HALF]
                    act.activation(v, v, ACT.Gelu).then_inc(gv_gelu, 1)
                if hh + 2 < 6:
                    load_bias(hh + 2)
        act.wait_ge(unit_done, END["gv"])
        act.dma_start(wsraw[:], a["gmlp_w_s_2"][0].rearrange("g p q -> p g q")).then_inc(ws_in, 16)
        act.dma_start(bs_b[:], a["gmlp_b_s_2"][0].rearrange("g p -> (g p)").unsqueeze(0).to_broadcast([P, GM_GROUPS * P])
                      .rearrange("q (g p) -> q g p", g=GM_GROUPS)).then_inc(bs_in, 16)
        act.wait_ge(gv_aggr, 4)
        act.activation(std[:], mv[:, :, 1], ACT.Sqrt, bias=eps_ln[:, 1:2]).then_inc(gv_std, 1)
        for b in range(4):
            act.wait_ge(ws_tp, b + 1)
            act.activation(wsT[:, 4 * b:4 * b + 4], ps[:, b], ACT.Copy).then_inc(ws_ev, 1)
        for b in range(4):
            act.wait_ge(rs_mm, b + 1)
            act.activation(rs_b[:, 4 * b:4 * b + 4], ps[:, b], ACT.Copy).then_inc(rs_ev, 1)

    @block.scalar
    def _(act):
        act_params(act)
        act.wait_ge(consts_in, 32)
        act_xt(act, 0, None, None)
        for u in range(AHEAD):
            act_whi(act, u, 0, 0)
        act_table(act)
        act_xbc(act)
        act_soft(act, dts, dta)
        act.wait_ge(small_in, 16 * 5)
        act.activation(sm[:, 8, 0], small[:, 1], ACT.Exp).then_inc(dta, 1)
        act_scp(act)
        act_plain(act, "scb")
        act_z(act)
        act_ssd(act)
        act.wait_ge(gt_ev, 8)
        act_jit(act, "out0", ya_yb)
        act_ln(act, 0, "out0", a["ln_mix_g"][0:1], a["ln_mix_b"][0:1])
        act_xt(act, 1, lambda k: col("lnm0g", k), lambda k: col("lnm0b", k))
        act_ffn(act, 0)
        act.wait_ge(ff_dve, 110)
        act_jit(act, "dn0", hid_ff)
        act_ln(act, 1, "dn0", a["ln_ffn_g"][0:1], a["ln_ffn_b"][0:1])
        act.dma_start(wf_raw[:], w_fox[:, :, 3 * D:3 * D + 16]).then_inc(small_in, 16)
        act_xt(act, 2, lambda k: col("lnf0g", k), lambda k: col("lnf0b", k))
        act.wait_ge(small_in, 16 * 6)
        act.activation(wf_hi_t[:], wf_raw[:], ACT.Copy).then_inc(wf_hi, 1)
        act_soft(act, fl_dve, fl_act)
        act_fox_qk(act)
        act_plain(act, "fv")
        act_attn(act, 0, ptb1, True)
        act.wait_ge(at_o, 8)
        act_jit(act, "fo", oT1)
        act_ln(act, 2, "fo", a["ln_mix_g"][1:2], a["ln_mix_b"][1:2])
        act_xt(act, 3, lambda k: col("lnm1g", k), lambda k: col("lnm1b", k))
        act_ffn(act, 1)
        act.wait_ge(ff_dve, 220)
        act_jit(act, "dn1", hid_ff)
        act_ln(act, 3, "dn1", a["ln_ffn_g"][1:2], a["ln_ffn_b"][1:2])
        for h in range(2):
            act_square(act, 0, h, lambda t: act.wait_ge(res_done, 12 + t + 1))
        norm_scale = lambda s: (lambda k: nscale[:, s, k:k + 1])
        norm_shift = lambda s: (lambda k: modc[:, s // 2, 24 * (s % 2) + k:24 * (s % 2) + k + 1])
        act_rms(act, 0)
        act_xt(act, 4, norm_scale(0), norm_shift(0))
        act_qkv(act)
        act_attn(act, 1, ptb2, False)
        act.wait_ge(at_o, 16)
        for s, (name, src) in enumerate((("o", oT2), ("md0", hid_mlp), ("go", uT), ("md1", hid_mlp))):
            if name == "md0":
                act_mlp(act, 0)
                act.wait_ge(mlp_done, 32)
            if name == "go":
                act_gu(act)
                act_gv(act)
                act.wait_ge(gm_u, NGM)
            if name == "md1":
                act_mlp(act, 1)
                act.wait_ge(mlp_done, 64)
            act_gate(act, s)
            r = 4 + s

            def squares(h, r=r, s=s):
                act_square(act, s + 1, h, lambda t: act.wait_ge(res_add, 8 * r + 4 * h + t + 1))

            if name == "md1":
                act_jit(act, name, src, last=True)
            else:
                act_jit(act, name, src, after_h0=lambda: squares(0))
                squares(1)
                act_rms(act, s + 1)
                act_xt(act, 5 + s, norm_scale(s + 1), norm_shift(s + 1))

    def dve_xt(dve, q):
        for k in range(KD):
            dve.wait_ge(xt_ev, KD * q + k + 1)
            dve.tensor_copy(xhi[:, k], xf[:, k % 2]).then_inc(xt_hi, 1)
            dve.wait_ge(xt_hi, KD * q + k + 1)
            dve.tensor_tensor(xlo[:, k], xf[:, k % 2], xhi[:, k].bitcast(F32), ALU.subtract).then_inc(xt_lo, 1)

    def dve_xbc(dve):
        with dve.Fori(0, 3) as i:
            for j in range(4):
                c, src = cv0[:, j % 2], ps[:, bank_f(j)]
                dve.wait_ge(xbc_aff, i * 4 + (j + 1))
                for k in range(3):
                    d = k + 1
                    if k:
                        dve.wait_ge(xbc_conv, i * 12 + (3 * j + k))
                    dve.scalar_tensor_tensor(c[:, d:], src[:, :T - d], col("ssmw", i * 4 + (12 * (2 - k) + j)), c[:, d:],
                                             ALU.mult, ALU.add).then_inc(xbc_conv, 1)

    def dve_soft(dve, s_dve, s_act, base_mm, bias, positive, dst):
        n = [0]

        def step(ins):
            ins.then_inc(s_dve, 1)
            n[0] += 1
            dve.wait_ge(s_dve, n[0])

        dve.wait_ge(f_mm, base_mm)
        step(dve.tensor_tensor(sm[:, 0], ps[:, 0, 0:64].rearrange("p (c h) -> p c h", c=NT),
                               bias.unsqueeze(1).to_broadcast([P, NT, 16]), ALU.add))
        step(dve.tensor_scalar(sm[:, 1], sm[:, 0], -1.0, None, ALU.mult))
        step(dve.tensor_tensor(sm[:, 2], sm[:, 0], sm[:, 1], ALU.max))
        dve.wait_ge(s_act, 1)
        step(dve.tensor_scalar(sm[:, 4], sm[:, 3], 1.0, None, ALU.add))
        step(dve.tensor_scalar(sm[:, 5], sm[:, 4], -1.0, None, ALU.add))
        step(dve.tensor_scalar(sm[:, 6], sm[:, 5], 0.0, None, ALU.is_equal))
        step(dve.tensor_tensor(sm[:, 5], sm[:, 5], sm[:, 6], ALU.add))
        step(dve.reciprocal(sm[:, 5], sm[:, 5]))
        dve.wait_ge(s_act, 2)
        step(dve.tensor_tensor(sm[:, 7], sm[:, 7], sm[:, 6], ALU.add))
        step(dve.tensor_tensor(sm[:, 7], sm[:, 7], sm[:, 5], ALU.mult))
        step(dve.tensor_tensor(sm[:, 7], sm[:, 7], sm[:, 3], ALU.mult))
        if positive:
            step(dve.scalar_tensor_tensor(dst, sm[:, 0], 0.0, sm[:, 7], ALU.max, ALU.add))
        else:
            step(dve.scalar_tensor_tensor(dst, sm[:, 0], 0.0, sm[:, 7], ALU.min, ALU.subtract))
        return n[0]

    def dve_scp(dve):
        with dve.Fori(0, 4) as i:
            for b in range(2):
                p, y = pb[:, b:b + 1], ya_yb[:, bass.ds(i * 2 + b, 1)]
                s = i * 8 + (4 * b + 1)
                dve.wait_ge(sc_h, i * 2 + (b + 1))
                dve.tensor_tensor(p, ps[:, bank_f(2 * b):bank_f(2 * b) + 1], hb[:, b:b + 1], ALU.mult).then_inc(sc_step, 1)
                dve.wait_ge(sc_step, s + 1)
                dve.tensor_scalar(y, p, col("scw", i * 2 + (16 + b)), None, ALU.mult).then_inc(sc_step, 1)
                for k in range(2):
                    d = k + 1
                    dve.wait_ge(sc_step, s + 2 + k)
                    yd = ya_yb[:, bass.ds(i * 2 + b, 1), d:]
                    dve.scalar_tensor_tensor(yd, pb[:, b:b + 1, :T - d], col("scw", i * 2 + (8 * (1 - k) + b)), yd,
                                             ALU.mult, ALU.add).then_inc(sc_step, 1)

    def dve_scb(dve):
        S = U0["scb"]
        dve.wait_ge(sc_step, 33)

        def unit(e, j):
            dve.wait_ge(unit_done, e + (S + 1))
            y = ya_yb[:, bass.ds(e, 1)]
            dve.tensor_tensor(y, ps[:, bank_f(j):bank_f(j) + 1], y, ALU.mult).then_inc(scb_done, 1)

        run(dve, 8, unit)

    def bc_h(x):
        return x.unsqueeze(2).to_broadcast([P, 16, HD])

    def heads(x):
        return x.rearrange("p (h d) -> p h d", d=HD)

    def dve_ssd(dve):
        for g in range(1, 12, 2):
            t, r = divmod(g, 3)
            dve.wait_ge(tok_tp, g + 1)
            if r < 2:
                dve.tensor_copy(xs_tok[:, t, r * HALF:(r + 1) * HALF], ps[:, g % 4]).then_inc(tok_ev_d, 1)
            else:
                dve.tensor_copy(b_tok[:, t], ps[:, g % 4, 0:256]).then_inc(tok_ev_d, 1)
        dve.wait_ge(cums_mm, 1)
        dve.tensor_copy(sm[:, 11], ps[:, 1, 0:64].rearrange("p (c h) -> p c h", c=NT)).then_inc(dts, 1)
        dve.wait_ge(dts, 14)
        dve.tensor_tensor(sm[:, 15], ps[:, 1, 64:128].rearrange("p (c h) -> p c h", c=NT), sm[:, 11], ALU.subtract
                          ).then_inc(dts, 1)
        ny, nprev = 0, 0
        for c in range(NT):
            dt_c, adt_c, acs_c = sm[:, 9, c], sm[:, 10, c], sm[:, 11, c]
            if c:
                dve.wait_ge(ssd_y, ny)
            dve.tensor_tensor(gbuf[:], tri.unsqueeze(1).to_broadcast([P, 16, P]),
                              adt_c.unsqueeze(2).to_broadcast([P, 16, P]), ALU.mult).then_inc(ssd_g, 1)
            if c == 0:
                dve.wait_ge(tok_ev_a, 6)
                dve.wait_ge(tok_ev_d, 6)
            dve.tensor_tensor(heads(xdt[:]), heads(xs_tok[:, c]), bc_h(dt_c), ALU.mult).then_inc(ssd_x, 1)
            if c == 0:
                dve.wait_ge(dta, 6)
            dve.wait_ge(ssd_x, 2 * c + 1)
            dve.tensor_tensor(heads(xdd[:]), heads(xdt[:]), bc_h(sm[:, 12, c]), ALU.mult).then_inc(ssd_x, 1)
            dve.wait_ge(ssd_r, c + 1)
            dve.tensor_tensor(mbuf[:], ps[:, 4:8].rearrange("p b (h t) -> p (b h) t", t=P),
                              acs_c.unsqueeze(2).to_broadcast([P, 16, P]), ALU.subtract).then_inc(ssd_d, 1)
            dve.wait_ge(ssd_d, 2 * c + 1)
            dve.tensor_scalar(mbuf[:], mbuf[:], 0.0, None, ALU.min).then_inc(ssd_d, 1)
            dve.tensor_tensor(cbm[:], ps[:, 0, 0:256].rearrange("p (g t) -> p g t", g=2),
                              tri.unsqueeze(1).to_broadcast([P, 2, P]), ALU.mult).then_inc(ssd_cbm, 1)
            dve.wait_ge(ssd_cbm, c + 1)
            dve.wait_ge(ssd_e, c + 1)
            for g in range(2):
                ins = dve.tensor_tensor(mbuf[:, 8 * g:8 * g + 8], mbuf[:, 8 * g:8 * g + 8],
                                        cbm[:, g].unsqueeze(1).to_broadcast([P, 8, P]), ALU.mult)
            ins.then_inc(ssd_m, 1)
            dve.wait_ge(ssd_mm, c + 1)
            y = y_tok[:, c]

            def ystep(ins):
                nonlocal ny
                ins.then_inc(ssd_y, 1)
                ny += 1

            if c == 0:
                ystep(dve.tensor_copy(y, ps[:, 4:6].rearrange("p b n -> p (b n)")))
            else:
                ystep(dve.tensor_tensor(heads(y), ps[:, 2:4].rearrange("p b (h d) -> p (b h) d", d=HD),
                                        bc_h(sm[:, 13, c]), ALU.mult))
                dve.wait_ge(ssd_y, ny)
                ystep(dve.tensor_tensor(y, ps[:, 4:6].rearrange("p b n -> p (b n)"), y, ALU.add))
            gflat = gbuf[:].rearrange("p h t -> p (h t)")[:, 0:D]
            ystep(dve.tensor_tensor(heads(gflat), heads(xs_tok[:, c]), bc_h(small[:, 2]), ALU.mult))
            dve.wait_ge(ssd_y, ny)
            ystep(dve.tensor_tensor(y, y, gflat, ALU.add))
            if c < NT - 1:
                st = ps[:, 6:8].rearrange("p b n -> p (b n)")
                if c == 0:
                    dve.tensor_copy(prev[:], st).then_inc(ssd_prev, 1)
                    nprev += 1
                else:
                    dve.wait_ge(ssd_prev, nprev)
                    dve.tensor_tensor(heads(prev[:]), heads(prev[:]), bc_h(sm[:, 14, c]), ALU.mult).then_inc(ssd_prev, 1)
                    nprev += 1
                    dve.wait_ge(ssd_prev, nprev)
                    dve.tensor_tensor(prev[:], st, prev[:], ALU.add).then_inc(ssd_prev, 1)
                    nprev += 1
        dve.wait_ge(ssd_y, ny)
        dve.wait_ge(z_done, 8)
        for t in range(NT):
            dve.tensor_tensor(y_tok[:, t], y_tok[:, t], zs[:, t], ALU.mult).then_inc(gt_u, 1)
        dve.wait_ge(gt_std, 1)
        dve.reciprocal(mv[:], mv[:]).then_inc(gt_r, 1)
        dve.wait_ge(gt_r, 1)
        for t in range(NT):
            for g in range(2):
                y = y_tok[:, t, g * HALF:(g + 1) * HALF]
                dve.tensor_scalar(y, y, mv[:, t, g:g + 1], None, ALU.mult).then_inc(gt_n, 1)

    def dve_jit(dve, name, src, after_h0):
        H, A = PAIRS[name], A0[name]

        def step(m0, k0, e, j):
            dve.wait_ge(a_hi, e + (A + m0 + 1))
            x = src[:, 2 * (k0 + e):2 * (k0 + e) + 2] if isinstance(e, int) else src[:, bass.ds(e * 2 + 2 * k0, 2)]
            s = (m0 + j) % 2
            dve.tensor_tensor(alo[:, s], x, ahi[:, s].bitcast(F32), ALU.subtract).then_inc(a_lo, 1)

        run(dve, H, lambda e, j: step(0, 0, e, j))
        for e in range(2):
            step(H, 0, e, e)
        after_h0()
        run(dve, H - 2, lambda e, j: step(H + 2, 2, e, j))

    def dve_ln_half(dve, r, name, h):
        dve.wait_ge(unit_done, U0[name] + (h + 1) * PAIRS[name])
        if h == 0 and r:
            dve.wait_ge(res_done, 4 * r)
        for t in range(NT):
            x = xres[:, t, h * HALF:(h + 1) * HALF]
            n = 8 * r + 4 * h + t + 1
            dve.scalar_tensor_tensor(x, x, ALPHA, ps[:, 4 * h + t], ALU.mult, ALU.add).then_inc(res_add, 1)
            dve.wait_ge(res_add, n)
            dve.bn_stats(stats[:, t, h], x).then_inc(stat_done, 1)

    def dve_ln_end(dve, r):
        dve.wait_ge(stat_done, 8 * r + 8)
        for t in range(NT):
            dve.bn_aggr(mv[:, t], stats[:, t, 0:2].rearrange("p a b -> p (a b)")).then_inc(aggr_done, 1)
        dve.wait_ge(std_done, r + 1)
        dve.reciprocal(rstd[:], std[:]).then_inc(rstd_done, 1)
        dve.wait_ge(rstd_done, r + 1)
        for t in range(NT):
            dve.tensor_scalar(nrm[:, t], xres[:, t], mv[:, t, 0:1], rstd[:, t:t + 1], ALU.subtract, ALU.mult
                              ).then_inc(nrm_done, 1)

    def dve_resid(dve, r):
        dve.wait_ge(gb_in, 32 * (r + 1))
        dve.wait_ge(nrm_done, 4 * r + 4)
        for t in range(NT):
            dve.tensor_tensor(xres[:, t], nrm[:, t], gb[:, 0], ALU.mult).then_inc(res_mul, 1)
        for t in range(NT):
            dve.wait_ge(res_mul, 4 * r + t + 1)
            dve.tensor_tensor(xres[:, t], xres[:, t], gb[:, 1], ALU.add).then_inc(res_done, 1)

    def dve_ffn(dve, L):
        FA, FD = 66 * L, 110 * L
        accf = acc[:].rearrange("p m n -> p (m n)")
        for m in range(4):
            dve.memset(accf[:, m * ADA_N:(m + 1) * ADA_N], 0.0).then_inc(ada_acc, 1)
        for lo, hi, ada in ((0, 8, True), (8, 11, False)):
            with dve.Fori(lo, hi) as i:
                for b in range(2):
                    pr = i * 2 + b
                    for z, (x, half, w) in enumerate(((gt, 2 * b, "g"), (ut, 2 * b + 1, "u"))):
                        dve.wait_ge(ff_act, i * 6 + (FA + 3 * b + 1 + 2 * z))
                        for k in range(2):
                            d = k + 1
                            if k:
                                dve.wait_ge(ff_dve, i * 10 + (FD + 5 * b + 2 * z + 1))
                            dve.scalar_tensor_tensor(x[:, b, d:], ps[:, bank_f(half), :T - d], col(f"cw{L}_{1 - k}{w}", pr),
                                                     x[:, b, d:], ALU.mult, ALU.add).then_inc(ff_dve, 1)
                    dve.wait_ge(ff_dve, i * 10 + (FD + 5 * b + 4))
                    dve.tensor_tensor(hid_ff[:, bass.ds(pr, 1)], ut[:, b:b + 1], gs[:, b:b + 1], ALU.mult
                                      ).then_inc(ff_dve, 1)
                    if ada:
                        for s in range(2):
                            m = 2 * b + s
                            dve.wait_ge(ada_in[s], i * 32 + 16 * (b + 1 + 16 * L))
                            dve.wait_ge(ada_acc, i * 4 + (36 * L + m + 1))
                            x = accf[:, m * ADA_N:(m + 1) * ADA_N]
                            dve.scalar_tensor_tensor(x, adaraw[s][:], ccol[:, bass.ds(i, 1)], x, ALU.mult, ALU.add
                                                     ).then_inc(ada_acc, 1)

    def dve_mod(dve, L):
        dve.wait_ge(mod_mm, L + 1)
        dve.tensor_tensor(modc[:, L], ps[:, 7, 0:48], tab[:, TAB["adab"] + 48 * L:TAB["adab"] + 48 * L + 48], ALU.add
                          ).then_inc(mod_done, 1)

    def dve_fox_aug(dve):
        for x in (qh, kh):
            for par, r in ((0, 64), (1, 0)):
                dve.memset(x[r:r + 64, par::2], 0.0).then_inc(aug, 1)
        dve.wait_ge(fl_dve, 12)
        dve.wait_ge(cum_mm, 1)
        cum = ps[0:16, 1]
        for r in range(0, P, 32):
            dve.tensor_scalar(cumx[r:r + 16], cum, 1.0 if r % 64 else -1.0, None, ALU.mult).then_inc(aug, 1)
        dve.wait_ge(aug, 8)
        for par, r in ((0, 64), (1, 0)):
            def rows16(x, r0):
                return x[r0:r0 + 16, par::2]
            hot = lambda r0: onehot[r0:r0 + 16, par::2].unsqueeze(2).to_broadcast([16, 8, T])
            cumb = lambda r0: cumx[r0:r0 + 16].unsqueeze(1).to_broadcast([16, 8, T])
            dve.tensor_copy(rows16(kh, r), cumb(r)).then_inc(aug, 1)
            dve.memset(rows16(kh, r + 32), 1.0).then_inc(aug, 1)
            dve.tensor_copy(rows16(qh, r), hot(r)).then_inc(aug, 1)
            dve.tensor_tensor(rows16(qh, r + 32), cumb(r + 32), hot(r + 32), ALU.mult).then_inc(aug, 1)

    AUG = 16

    def dve_fv(dve):
        S = U0["fv"]
        for h in range(2):
            dve.wait_ge(unit_done, S + 4 * h + 4)
            for t in range(NT):
                dve.tensor_copy(vtok[:, t, h * HALF:(h + 1) * HALF], ps[:, 4 * h + t]).then_inc(fv_ev, 1)

    def dve_attn(dve, A, oT, causal):
        B = 64 * A

        def pv_out(pr):
            dve.wait_ge(at_pv, 16 * A + 2 * pr + 2)
            dve.tensor_copy(oT[:, pr], ps[:, 5 + pr % 2]).then_inc(at_o, 1)

        for n in range(65):
            if n < 64:
                N = (n % 4 + 1) * P if causal else T
                dve.wait_ge(at_s, B + n + 1)
                dve.tensor_reduce(rowst[:, 0, n:n + 1], ps[:, n % 3, 0:N], AX.X, ALU.max, negate=True).then_inc(at_max, 1)
            m = n - 1
            if m >= 0:
                N = (m % 4 + 1) * P if causal else T
                dve.wait_ge(at_exp, B + m + 1)
                dve.reciprocal(rowst[:, 2, m:m + 1], rowst[:, 1, m:m + 1]).then_inc(at_rinv, 1)
                dve.wait_ge(at_rinv, B + m + 1)
                dve.tensor_scalar(pbuf[:, m % 3, 0:N], pbuf[:, m % 3, 0:N], rowst[:, 2, m:m + 1], None, ALU.mult
                                  ).then_inc(at_p, 1)
            if n >= 12 and n % 8 == 4:
                pv_out((n - 12) // 8)
        pv_out(7)

    def dve_rms_end(dve, s):
        dve.wait_ge(sq_done, 8 * (s + 1))
        dve.tensor_tensor(mv[:, :, 0], sumsq[:, :, 0], sumsq[:, :, 1], ALU.add).then_inc(aggr_done, 1)
        dve.wait_ge(std_done, 4 + s + 1)
        dve.reciprocal(rstd[:], std[:]).then_inc(rstd_done, 1)
        dve.wait_ge(rstd_done, 4 + s + 1)
        for t in range(NT):
            dve.tensor_scalar(nrm[:, t], xres[:, t], rstd[:, t:t + 1], None, ALU.mult).then_inc(nrm_done, 1)

    def dve_gated_half(dve, s, name, h):
        r = 4 + s
        dve.wait_ge(unit_done, U0[name] + (h + 1) * PAIRS[name])
        dve.wait_ge(gate_ev, s + 1)
        for t in range(NT):
            c = slice(h * HALF, (h + 1) * HALF)
            dve.tensor_tensor(nrm[:, t, c], ps[:, 4 * h + t], gate[:, c], ALU.mult).then_inc(gated, 1)
            dve.wait_ge(gated, 8 * s + 4 * h + t + 1)
            dve.tensor_tensor(xres[:, t, c], xres[:, t, c], nrm[:, t, c], ALU.add).then_inc(res_add, 1)

    def dve_qkv(dve):
        S = U0["qkv"]
        n = 0
        for hh in range(3):
            nh = 4 if hh == 0 else 8
            w = nh * HD
            for t in range(NT):
                dve.wait_ge(q_sq, 4 * hh + t + 1)
                dve.tensor_reduce(hsum[:, 0, t, 0:nh], sqb[:, t, 0:w].rearrange("p (h d) -> p h d", d=HD), AX.X, ALU.add
                                  ).then_inc(q_sum, 1)
            dve.wait_ge(q_std, hh + 1)
            dve.reciprocal(hsum[:, 2, :, 0:nh], hsum[:, 1, :, 0:nh]).then_inc(q_sum, 1)
            dve.wait_ge(q_sum, 5 * hh + 5)
            if hh == 0:
                dve.wait_ge(qkg_in, 48)
            for t in range(NT):
                src = ps[:, 4 * (hh % 2) + t, 0:w].rearrange("p (h d) -> p h d", d=HD)
                v3 = lambda x: x[:, 0:w].rearrange("p (h d) -> p h d", d=HD)
                pair = lambda x: x[:, 0:w].rearrange("p (h d e) -> p h d e", d=HD // 2, e=2)
                tabs = cs[:, t, 1].rearrange("p (d e) -> p d e", e=2)
                dst = k_tok[:, t] if hh == 0 else q_tok[:, t, (hh - 1) * HALF:hh * HALF]

                def step(ins):
                    nonlocal n
                    ins.then_inc(q_step, 1)
                    n += 1

                step(dve.tensor_tensor(v3(qn), src, hsum[:, 2, t, 0:nh].unsqueeze(2).to_broadcast([P, nh, HD]), ALU.mult))
                dve.wait_ge(q_step, n)
                g = qkg[:, 1 if hh == 0 else 0]
                step(dve.tensor_tensor(v3(qn), v3(qn), g.unsqueeze(1).to_broadcast([P, nh, HD]), ALU.mult))
                dve.wait_ge(q_step, n)
                step(dve.tensor_tensor(v3(ra), v3(qn), cs[:, t, 0].unsqueeze(1).to_broadcast([P, nh, HD]), ALU.mult))
                for e in range(2):
                    step(dve.tensor_tensor(pair(rb)[:, :, :, e], pair(qn)[:, :, :, 1 - e],
                                           tabs[:, :, e].unsqueeze(1).to_broadcast([P, nh, HD // 2]), ALU.mult))
                dve.wait_ge(q_step, n)
                step(dve.tensor_tensor(dst, ra[:, 0:w], rb[:, 0:w], ALU.add))
        assert n == 72

    def dve_gate(dve, s):
        g0 = 24 * (s % 2) + 16
        for k in range(KD):
            dve.tensor_scalar(gdiag[:, k], ident, modc[:, s // 2, g0 + k:g0 + k + 1], None, ALU.mult).then_inc(gdiag_done, 1)

    def dve_mlp(dve, L):
        def unit(e, j):
            dve.wait_ge(relu_done, e + (32 * L + 1))
            dve.scalar_tensor_tensor(hid_mlp[:, bass.ds(e, 1)], ps[:, bank_f(j):bank_f(j) + 1], 0.0,
                                     relu[:, j % 2:j % 2 + 1], ALU.max, ALU.mult).then_inc(mlp_done, 1)

        run(dve, 32, unit)

    def dve_gv(dve):
        S = U0["gv"]
        for hh in range(6):
            c = slice(hh * HALF, (hh + 1) * HALF)
            dve.wait_ge(unit_done, S + 4 * hh + 4)
            dve.wait_ge(bb_in[hh % 2], 16 * (hh // 2 + 1))
            for t in range(NT):
                dve.tensor_tensor(vt[t][:, c], ps[:, 4 * (hh % 2) + t], bb[:, hh % 2], ALU.add).then_inc(gv_add, 1)
            for t in range(NT):
                dve.wait_ge(gv_gelu, 4 * hh + t + 1)
                dve.bn_stats(stats[:, t, hh], vt[t][:, c]).then_inc(gv_stat, 1)
        dve.wait_ge(gv_stat, 24)
        for t in range(NT):
            dve.bn_aggr(mv[:, t], stats[:, t].rearrange("p a b -> p (a b)")).then_inc(gv_aggr, 1)
        dve.wait_ge(gv_std, 1)
        dve.reciprocal(rstd[:], std[:]).then_inc(gv_rstd, 1)
        dve.wait_ge(gv_rstd, 1)
        for t in range(NT):
            dve.tensor_scalar(vt[t][:], vt[t][:], mv[:, t, 0:1], rstd[:, t:t + 1], ALU.subtract, ALU.mult
                              ).then_inc(gv_nrm, 1)
        dve.wait_ge(rs_ev, 4)
        dve.wait_ge(bs_in, 16)
        nk = 0
        for cc in range(NGM):
            b = cc % 2
            for r0, r1, g in gm_pieces(cc):
                dve.scalar_tensor_tensor(gk[r0:r1, b], rs_b[r0:r1, g], col("glnb", cc)[r0:r1], bs_b[r0:r1, g],
                                         ALU.mult, ALU.add).then_inc(gm_k, 1)
                nk += 1
            dve.wait_ge(gm_k, nk)
            dve.wait_ge(gm_mm, cc + 1)
            dve.scalar_tensor_tensor(gz[:, b].rearrange("p (n q) -> p n q", q=P),
                                     ps[:, 4 + cc % 4].rearrange("p (n q) -> p n q", q=P), col("glng", cc),
                                     gk[:, b].unsqueeze(1).to_broadcast([P, NT, P]), ALU.mult, ALU.add).then_inc(gm_z, 1)
            dve.wait_ge(gm_z, cc + 1)
            dve.tensor_tensor(uT[:, cc], uT[:, cc], gz[:, b], ALU.mult).then_inc(gm_u, 1)

    def gm_pieces(cc):
        out, c = [], cc * P
        while c < (cc + 1) * P:
            g = c // GM_GW
            e = min((g + 1) * GM_GW, (cc + 1) * P)
            out.append((c - cc * P, e - cc * P, g))
            c = e
        return out

    @block.vector
    def _(dve):
        dve.memset(tabraw[:], 0.0).then_inc(tab_zero, 1)
        dve.memset(eps_ln[:, 0:1], LN_EPS).then_inc(prep, 1)
        dve.memset(eps_ln[:, 1:2], EPS).then_inc(prep, 1)
        dve_xt(dve, 0)
        dve.wait_ge(wf_hi, 1)
        dve.tensor_tensor(wf_lo_t[:], wf_raw[:], wf_hi_t[:].bitcast(F32), ALU.subtract).then_inc(wf_lo, 1)
        dve.wait_ge(tab_ready, 2)
        dve_xbc(dve)
        assert dve_soft(dve, dts, dta, 1, small[:, 0], True, sm[:, 9]) == 12
        dve.wait_ge(dta, 3)
        dve.scalar_tensor_tensor(sm[:, 10], sm[:, 9], -1.0, sm[:, 8, 0].unsqueeze(1).to_broadcast([P, NT, 16]),
                                 ALU.mult, ALU.mult).then_inc(dts, 1)
        dve.wait_ge(dts, 13)
        dve.memset(mv[:], 0.0).then_inc(sc_step, 1)
        dve_scp(dve)
        dve_scb(dve)
        dve_ssd(dve)
        dve_jit(dve, "out0", ya_yb, lambda: dve_ln_half(dve, 0, "out0", 0))
        dve_ln_half(dve, 0, "out0", 1)
        dve_ln_end(dve, 0)
        dve_xt(dve, 1)
        dve_resid(dve, 0)
        dve_ffn(dve, 0)

        def ffn_mid(L, r):
            dve_mod(dve, L)
            dve_ln_half(dve, r, f"dn{L}", 0)

        dve.wait_ge(ff_dve, 110)
        dve_jit(dve, "dn0", hid_ff, lambda: ffn_mid(0, 1))
        dve_ln_half(dve, 1, "dn0", 1)
        dve_ln_end(dve, 1)
        dve_xt(dve, 2)
        dve.wait_ge(wf_hi, 2)
        dve.tensor_tensor(wf_lo_t[:], wf_raw[:], wf_hi_t[:].bitcast(F32), ALU.subtract).then_inc(wf_lo, 1)
        assert dve_soft(dve, fl_dve, fl_act, 2, small[:, 3], False, sm[:, 9]) == 12
        dve_resid(dve, 1)
        dve_fox_aug(dve)
        dve_fv(dve)
        dve_attn(dve, 0, oT1, True)
        dve_jit(dve, "fo", oT1, lambda: dve_ln_half(dve, 2, "fo", 0))
        dve_ln_half(dve, 2, "fo", 1)
        dve_ln_end(dve, 2)
        dve_xt(dve, 3)
        dve_resid(dve, 2)
        dve_ffn(dve, 1)
        dve.wait_ge(ff_dve, 220)
        dve_jit(dve, "dn1", hid_ff, lambda: ffn_mid(1, 3))
        dve_ln_half(dve, 3, "dn1", 1)
        dve_ln_end(dve, 3)
        dve_resid(dve, 3)
        dve.wait_ge(mod_done, 2)
        for s in range(4):
            m0 = 24 * (s % 2) + 8
            g0 = TAB["n1g" if s % 2 == 0 else "n2g"] + 8 * (s // 2)
            dve.scalar_tensor_tensor(nscale[:, s], modc[:, s // 2, m0:m0 + KD], 1.0, tab[:, g0:g0 + KD], ALU.add, ALU.mult
                                     ).then_inc(prep, 1)
        dve_rms_end(dve, 0)
        dve_xt(dve, 4)
        dve_qkv(dve)
        dve_attn(dve, 1, oT2, False)
        for s, (name, src) in enumerate((("o", oT2), ("md0", hid_mlp), ("go", uT), ("md1", hid_mlp))):
            if name == "md0":
                dve_mlp(dve, 0)
                dve.wait_ge(mlp_done, 32)
            if name == "go":
                dve_gv(dve)
                dve.wait_ge(gm_u, NGM)
            if name == "md1":
                dve_mlp(dve, 1)
                dve.wait_ge(mlp_done, 64)
            dve_gate(dve, s)
            dve_jit(dve, name, src, lambda: dve_gated_half(dve, s, name, 0))
            dve_gated_half(dve, s, name, 1)
            if name != "md1":
                dve_rms_end(dve, s + 1)
                dve_xt(dve, 5 + s)

    def mm3(pe, out, lh, ll, rh, rl, start, stop):
        pe.matmul(out, lh, rh, start=start, stop=False)
        pe.matmul(out, lh, rl, start=False, stop=False)
        return pe.matmul(out, ll, rh, start=False, stop=stop)

    def pe_xt(pe, q):
        if q == 0:
            pe.wait_ge(x_in, 16)
            pe.wait_ge(consts_in, 32)
        else:
            pe.wait_ge(nrm_done, 4 * (q if q < 4 else q + 1))
        src = xres if q == 0 else nrm
        for k in range(KD):
            if k >= 4:
                pe.wait_ge(xt_ev, KD * q + k - 3)
            for t in range(NT):
                ins = pe.transpose(ps[:, k % 4, t * P:(t + 1) * P], src[:, t, k * P:(k + 1) * P], ident)
            ins.then_inc(xt_tp, 1)

    def pe_f(pe, name, freed, q=None, first=()):
        S, n = U0[name], NUNITS[name]

        def unit(e, j):
            slot = (S + j) % RING
            pe.wait_ge(w_lo, e + (S + 1))
            wh = whi[:, slot].rearrange("p (k n) -> p k n", k=KD)
            wl = wlo[:, slot].rearrange("p (k n) -> p k n", k=KD)
            for k in range(KD):
                if q is not None and isinstance(e, int) and e == 0:
                    pe.wait_ge(xt_lo, KD * q + k + 1)
                ins = mm3(pe, ps[:, bank_f(j)], wh[:, k], wl[:, k], xhi[:, k], xlo[:, k], k == 0, k == KD - 1)
            ins.then_inc(unit_done, 1)

        for s, v in first:
            pe.wait_ge(s, v)
        for e in range(RING):
            unit(e, e)
        if n // RING == 2:
            for e in range(RING, n):
                s, v = freed(1, e % RING)
                pe.wait_ge(s, v)
                unit(e, e % RING)
        else:
            with pe.Fori(1, n // RING) as i:
                for j in range(RING):
                    s, v = freed(i, j)
                    pe.wait_ge(s, v)
                    unit(i * RING + j, j)

    def pe_t_unit(pe, start, e, j, bank0, lh, ll, first):
        slot = (start + j) % RING
        pe.wait_ge(w_lo, e + (start + 1))
        wh = whi[:, slot].rearrange("p (k n) -> p k n", k=2)
        wl = wlo[:, slot].rearrange("p (k n) -> p k n", k=2)
        for k in range(2):
            for t in range(NT):
                out = ps[:, bank0 + t]
                st = first and k == 0
                c = slice(t * P, (t + 1) * P)
                pe.matmul(out, lh[:, k, c], wh[:, k], start=st, stop=False, skip_group_check=True)
                pe.matmul(out, lh[:, k, c], wl[:, k], start=False, stop=False, skip_group_check=True)
                ins = pe.matmul(out, ll[:, k, c], wh[:, k], start=False, stop=False, skip_group_check=True)
        ins.then_inc(unit_done, 1)

    def pe_t_x(pe, name, halves, free):
        S = U0[name]
        for h in range(halves):
            for s, v in free(h):
                pe.wait_ge(s, v)
            for j in range(4):
                pe_t_unit(pe, S + 4 * h, j, j, 4 * (h % 2), xhi[:, 2 * j:2 * j + 2], xlo[:, 2 * j:2 * j + 2], j == 0)

    def pe_t_jit(pe, name, free, mid=None):
        H, S, A = PAIRS[name], U0[name], A0[name]
        for h in range(2):
            if h and mid:
                mid()
            for s, v in free(h):
                pe.wait_ge(s, v)

            def unit(m0, e, j, first):
                pe.wait_ge(a_lo, e + (A + m0 + 1))
                s = (m0 + j) % 2
                pe_t_unit(pe, S + m0, e, j, 4 * h, ahi[:, s], alo[:, s], first)

            unit(h * H, 0, 0, True)
            run(pe, H - 1, lambda e, j: unit(h * H + 1, e, j, False))

    def pe_small(pe, q):
        pe.wait_ge(wf_lo, q + 1)
        for t in range(NT):
            for k in range(KD):
                c = slice(t * P, (t + 1) * P)
                ins = mm3(pe, ps[:, 0, t * 16:(t + 1) * 16], xhi[:, k, c], xlo[:, k, c], wf_hi_t[:, k], wf_lo_t[:, k],
                          k == 0, k == KD - 1)
        ins.then_inc(f_mm, 1)

    def pe_ssd(pe):
        pe.wait_ge(xbc_silu, 12)
        pe.wait_ge(z_done, 4)
        for g in range(12):
            t, r = divmod(g, 3)
            if g >= 4:
                pe.wait_ge(tok_ev_d if g % 2 else tok_ev_a, g // 2 - 1)
            for k in range(4 if r < 2 else 2):
                ins = pe.transpose(ps[:, g % 4, k * P:(k + 1) * P], xbcT[:, 4 * r + k, t * P:(t + 1) * P], ident)
            ins.then_inc(tok_tp, 1)
        pe.wait_ge(dts, 13)
        pe.wait_ge(tok_ev_d, 6)
        adt = sm[:, 10].rearrange("p c h -> p (c h)")
        pe.matmul(ps[:, 1, 0:64], tri, adt, start=True, stop=True)
        pe.matmul(ps[:, 1, 64:128], ones, adt, start=True, stop=True).then_inc(cums_mm, 1)
        ny = [2 + 1, 4 * 1 + 3, 4 * 2 + 3]
        nprev = [1, 3, 5]
        for c in range(NT):
            tc = slice(c * P, (c + 1) * P)
            if c == 0:
                pe.wait_ge(z_done, 8)
                pe.wait_ge(tok_ev_a, 6)
            else:
                pe.wait_ge(ssd_y, ny[c - 1])
                pe.wait_ge(ssd_prev, nprev[c - 1])
            pe.wait_ge(ssd_g, c + 1)
            for g in range(2):
                pe.matmul(ps[:, 0, g * P:(g + 1) * P], xbcT[:, 8 + g, tc], xbcT[:, 10 + g, tc], start=True, stop=True)
            for b in range(4):
                ins = pe.matmul(ps[:, 4 + b], ones, gbuf[:, 4 * b:4 * b + 4].rearrange("p h t -> p (h t)"),
                                start=True, stop=True)
            ins.then_inc(ssd_r, 1)
            if c:
                for g in range(2):
                    pe.matmul(ps[:, 2 + g], xbcT[:, 10 + g, tc], prev[:, g * HALF:(g + 1) * HALF], start=True, stop=True)
            pe.wait_ge(ssd_m, c + 1)
            pe.wait_ge(ssd_x, 2 * c + 2)
            for h in range(HEADS):
                ins = pe.matmul(ps[:, 4 + h // 8, (h % 8) * HD:(h % 8 + 1) * HD], mbuf[:, h], xdt[:, h * HD:(h + 1) * HD],
                                start=True, stop=True)
            if c < NT - 1:
                for g in range(2):
                    ins = pe.matmul(ps[:, 6 + g], b_tok[:, c, g * P:(g + 1) * P], xdd[:, g * HALF:(g + 1) * HALF],
                                    start=True, stop=True)
            ins.then_inc(ssd_mm, 1)
        pe.wait_ge(gt_n, 8)
        for k in range(KD):
            if k >= 4:
                pe.wait_ge(gt_ev, k - 3)
            for t in range(NT):
                ins = pe.transpose(ps[:, k % 4, t * P:(t + 1) * P], y_tok[:, t, k * P:(k + 1) * P], ident)
            ins.then_inc(gt_tp, 1)

    def pe_cum(pe):
        pe.wait_ge(fl_dve, 12)
        for t in range(NT):
            for i in range(t + 1):
                ins = pe.matmul(ps[0:16, 1, t * P:(t + 1) * P], sm[:, 9, i], tri if i == t else ones,
                                start=i == 0, stop=i == t)
        ins.then_inc(cum_mm, 1)

    def pe_attn(pe, A, ptb, causal, q_of, k_of, v_of):
        B = 64 * A

        def weigh(h):
            bank, r = 5 + (h // 2) % 2, 64 * (h % 2)
            pe.wait_ge(at_pt, B + 4 * h + 4)
            if h % 2 == 0 and h >= 4:
                pe.wait_ge(at_o, 8 * A + h // 2 - 1)
            for c in range(NT):
                q0 = c * P if causal else 0
                ins = pe.matmul(ps[r:r + 64, bank, q0:T], v_of(h, c), ptb[:, h % 2, c, q0:T], start=c == 0, stop=c == NT - 1)
            ins.then_inc(at_pv, 1)

        for n in range(64 + LEAD):
            if n < 64:
                h, i = divmod(n, 4)
                N = (i + 1) * P if causal else T
                if n >= 3:
                    pe.wait_ge(at_exp, B + n - 2)
                ins = pe.matmul(ps[:, n % 3, 0:N], q_of(h, i), k_of(h, N), start=True, stop=not causal)
                if causal:
                    ins = pe.matmul(ps[:, n % 3, i * P:N], ident, cmask, start=False, stop=True)
                ins.then_inc(at_s, 1)
            m = n - LEAD
            if m >= 0:
                h, i = divmod(m, 4)
                pe.wait_ge(at_p, B + m + 1)
                if m >= 2:
                    pe.wait_ge(at_pt, B + m - 1)
                for c in range(i + 1 if causal else NT):
                    ins = pe.transpose(ps[:, 3 + m % 2, c * P:(c + 1) * P], pbuf[:, m % 3, c * P:(c + 1) * P], ident)
                ins.then_inc(at_tp, 1)
                if i == 0 and h:
                    weigh(h - 1)
        weigh(HEADS - 1)

    def pe_mod(pe, L):
        pe.wait_ge(ada_acc, 36 * (L + 1))
        for m in range(48):
            ins = pe.matmul(ps[:, 7, m:m + 1], acc[:, m], ones[:, 0:1], start=True, stop=True)
        ins.then_inc(mod_mm, 1)

    def pe_gate(pe, s):
        pe.wait_ge(gdiag_done, KD * (s + 1))
        for k in range(KD):
            ins = pe.matmul(ps[:, 4 + k // 4, (k % 4) * P:(k % 4 + 1) * P], ones, gdiag[:, k], start=True, stop=True)
        ins.then_inc(gate_mm, 1)

    def pe_gv(pe):
        S = U0["gv"]

        def half(h, b, e0):
            for j in range(4):
                pe_t_unit(pe, S, e0 + j, j, 4 * b, xhi[:, 2 * j:2 * j + 2], xlo[:, 2 * j:2 * j + 2], j == 0)

        for b in range(2):
            if b:
                pe.wait_ge(gu_ev, NGM)
            half(b, b, 4 * b)
        with pe.Fori(1, 3) as i:
            for b in range(2):
                pe.wait_ge(gv_add, i * 8 + (4 * b - 4))
                half(None, b, i * 8 + 4 * b)
        pe.wait_ge(ws_in, 16)
        pe.wait_ge(gv_add, 20)
        for g in range(GM_GROUPS):
            ins = pe.transpose(ps[:, g // 4, (g % 4) * P:(g % 4 + 1) * P], wsraw[:, g], ident)
            if g % 4 == 3:
                ins.then_inc(ws_tp, 1)
        for b in range(4):
            pe.wait_ge(ws_ev, b + 1)
            pe.matmul(ps[:, b], ones, wsT[:, 4 * b:4 * b + 4].rearrange("p g q -> p (g q)"), start=True, stop=True
                      ).then_inc(rs_mm, 1)
        pe.wait_ge(gv_nrm, 4)
        for cc in range(NGM):
            if cc >= 4:
                pe.wait_ge(gm_z, cc - 3)
            for r0, r1, g in gm_pieces(cc):
                for t in range(NT):
                    ins = pe.matmul(ps[r0:r1, 4 + cc % 4, t * P:(t + 1) * P], vt[t][:, cc * P + r0:cc * P + r1], wsT[:, g],
                                    start=True, stop=True)
            ins.then_inc(gm_mm, 1)

    @block.tensor
    def _(pe):
        pe_xt(pe, 0)
        pe.wait_ge(tab_in, TAB_LOADS)
        pe.wait_ge(xt_ev, 8)
        for b in range(NTAB):
            ins = pe.transpose(ps[:, b // 4, (b % 4) * P:(b % 4 + 1) * P], tabraw[:, b], ident)
            if b in (3, 5):
                ins.then_inc(tab_tp, 1)
        pe_f(pe, "xbc", lambda i, j: (xbc_conv, i * 12 + (3 * j - 9)), q=0)
        pe.wait_ge(tab_ready, 2)
        pe_small(pe, 0)
        pe_f(pe, "scp", lambda i, j: (sc_step, i * 8 + (1 + 4 * (j // 2) - 8 + 1)), first=((xbc_conv, 36),))
        pe_f(pe, "scb", lambda i, j: (scb_done, 4 * i + j - 3), first=((sc_step, 33 - 3),))
        pe_t_x(pe, "z", 2, lambda h: ((dts, 1),) if h == 0 else ((scb_done, 8),))
        pe_ssd(pe)
        pe_t_jit(pe, "out0", lambda h: ((gt_ev, 8),) if h == 0 else ((ssd_y, 15),))
        pe_xt(pe, 1)
        pe_f(pe, "up0", lambda i, j: (ff_dve, i * 10 + (5 * (j // 2) - 10 + 2 + 2 * (j % 2))), q=1, first=((res_add, 8),))
        pe_t_jit(pe, "dn0", lambda h: ((xt_ev, 16),) if h == 0 else ((mod_done, 1),),
                 mid=lambda: (pe.wait_ge(ff_dve, 110), pe_mod(pe, 0)))
        pe_xt(pe, 2)
        pe.wait_ge(xt_lo, 24)
        pe_small(pe, 1)
        pe_f(pe, "fqk", lambda i, j: (fqk_ev, i * 8 + (2 * j - 6)), first=((res_add, 16),))
        pe_cum(pe)
        pe_t_x(pe, "fv", 2, lambda h: ((aug, 8),) if h == 0 else ((fqk_ev, 32),))
        pe.wait_ge(fv_ev, 8)
        pe.wait_ge(aug, AUG)
        pe_attn(pe, 0, ptb1, True, lambda h, i: qh[:, h, i * P:(i + 1) * P], lambda h, N: kh[:, h, 0:N],
                lambda h, c: vtok[:, c, h * HD:(h + 1) * HD])
        pe_t_jit(pe, "fo", lambda h: ((at_exp, 64), (at_pt, 64)) if h == 0 else ((at_o, 8),))
        pe_xt(pe, 3)
        pe_f(pe, "up1", lambda i, j: (ff_dve, i * 10 + (110 + 5 * (j // 2) - 10 + 2 + 2 * (j % 2))), q=3,
             first=((res_add, 24),))
        pe_t_jit(pe, "dn1", lambda h: ((xt_ev, 32),) if h == 0 else ((mod_done, 2),),
                 mid=lambda: (pe.wait_ge(ff_dve, 220), pe_mod(pe, 1)))
        pe_xt(pe, 4)
        pe.wait_ge(xt_lo, 40)
        pe_t_x(pe, "qkv", 3, lambda h: (((xt_ev, 40),), ((res_add, 32),), ((q_step, 6 * 3 + 1), (v_ev, 4)))[h])
        for r in range(10):
            if r == 0:
                pe.wait_ge(q_step, 24)
                pe.wait_ge(q_step, 6 * 7 + 1)
            if r == 2:
                pe.wait_ge(q_step, 72)
            if r >= 4:
                pe.wait_ge(q_ev, {4: 1, 5: 2}.get(r, 2 + 2 * (r - 4 - 1)))
            src, k = (k_tok, r) if r < 2 else (q_tok, r - 2)
            for t in range(NT):
                ins = pe.transpose(ps[:, 4 + r % 4, t * P:(t + 1) * P], src[:, t, k * P:(k + 1) * P], ident)
            ins.then_inc(q_tp, 1)
        pe.wait_ge(q_ev, 18)

        def kb(h):
            return slice(64 * (h // 4 % 2), 64 * (h // 4 % 2) + 64)

        pe_attn(pe, 1, ptb2, False, lambda h, i: qT2[kb(h), h // 8 * 4 + h % 4, i * P:(i + 1) * P],
                lambda h, N: kT2[kb(h), h // 8, 0:N], lambda h, c: v2[:, c, (h // 4) * HD:(h // 4 + 1) * HD])
        pe.wait_ge(at_o, 16)
        pe.wait_ge(at_pt, 128)
        pe_gate(pe, 0)
        pe_t_jit(pe, "o", lambda h: ((at_exp, 128),) if h == 0 else ((gate_ev, 1),))
        pe_xt(pe, 5)
        pe_f(pe, "mu0", lambda i, j: (mlp_done, i * 4 + (j - 3)), q=5, first=((res_add, 40),))
        pe.wait_ge(mlp_done, 32)
        pe_gate(pe, 1)
        pe_t_jit(pe, "md0", lambda h: ((xt_ev, 48),) if h == 0 else ((gate_ev, 2),))
        pe_xt(pe, 6)
        pe_f(pe, "gu", lambda i, j: (gu_ev, i * 4 + (j - 3)), q=6, first=((res_add, 48),))
        pe.wait_ge(xt_ev, 56)
        pe_gv(pe)
        pe.wait_ge(gm_z, NGM)
        pe_gate(pe, 2)
        pe_t_jit(pe, "go", lambda h: ((rs_ev, 4),) if h == 0 else ((gate_ev, 3),))
        pe_xt(pe, 7)
        pe_f(pe, "mu1", lambda i, j: (mlp_done, i * 4 + (j + 29)), q=7, first=((res_add, 56),))
        pe.wait_ge(mlp_done, 64)
        pe_gate(pe, 3)
        pe_t_jit(pe, "md1", lambda h: ((xt_ev, 64),) if h == 0 else ((gate_ev, 4),))


def kernel(**inputs):
    import concourse.bacc as bacc
    from concourse.bass_utils import run_bass_kernel_spmd

    nc = bacc.Bacc("TRN2", target_bir_lowering=False, num_devices=1)
    consts, cs, onehot = host_constants()
    arrays, aps = {}, {}
    for name, x in list(inputs.items()) + [("consts", consts), ("cs", cs), ("onehot", onehot)]:
        x = np.ascontiguousarray(x)
        arrays[f"in_{name}"] = x
        aps[name] = nc.dram_tensor(f"in_{name}", x.shape, mybir.dt.from_np(x.dtype), kind="ExternalInput").ap()
    out = nc.dram_tensor("out", (1, T, D), F32, kind="ExternalOutput").ap()
    build(nc, aps, out)
    r = run_bass_kernel_spmd(nc, [arrays], core_ids=[0])
    return r.results[0]["out"]
```

```python
from contextlib import ExitStack

import numpy as np
import concourse.bass as bass
from concourse import mybir

F32 = mybir.dt.float32
F32R = mybir.dt.float32r
ALU = mybir.AluOpType
ACT = mybir.ActivationFunctionType
AX = mybir.AxisListType

P = 128
T = 512
NT = T // P
D = 1024
KD = D // P
HALF = 512
UNIT = 1024
RING = 4
D_FF = 2816
NFF = D_FF // P
HEADS = 16
HD = 64
SSM_XBC = 1536
GM_HALF = 3072
NGM = GM_HALF // P
GM_GROUPS = 16
GM_GW = GM_HALF // GM_GROUPS
MLP = 4096
NMLP = MLP // P
ALPHA = 4 ** 0.25
LN_EPS = 1e-5
EPS = 1e-6
KB = 256
FFN_PARTS = ((0, 1, True), (1, 8, True), (8, 10, False), (10, 11, False))
SBANKS = (0, 1, 2, 7)
PSLOTS = 6
LEAD = 3

SC_B, SC_C, SC_H, ZCOL = 0, D, 2 * D, 3 * D
XBC_COL = 4 * D
DT_COL = 4 * D + SSM_XBC

UNITS = [("xbc", 12), ("scp", 16), ("scb", 8), ("z", 8), ("out0", 16), ("up0", 44), ("dn0", 22),
         ("fqk", 16), ("fv", 8), ("fo", 8), ("up1", 44), ("dn1", 22), ("qkv", 12), ("o", 8),
         ("mu0", 32), ("md0", 32), ("gu", 24), ("gv", 24), ("go", 24), ("mu1", 32), ("md1", 32)]
U0 = {}
_n = 0
for _name, _k in UNITS:
    U0[_name] = _n
    _n += _k
TOTAL_UNITS = _n
NUNITS = dict(UNITS)
END = {k: U0[k] + NUNITS[k] for k in U0}
JIT = [("out0", 8), ("dn0", 11), ("fo", 4), ("dn1", 11), ("o", 4), ("md0", 16), ("go", 12), ("md1", 16)]
PAIRS = dict(JIT)
A0 = {}
_n = 0
for _name, _k in JIT:
    A0[_name] = _n
    _n += 2 * _k


def host_constants():
    i = np.arange(P)
    c = np.zeros((P, 4, P), np.float32)
    c[:, 0] = i[:, None] == i[None, :]
    c[:, 1] = i[:, None] <= i[None, :]
    c[:, 2] = 1.0
    c[:, 3] = np.where(i[None, :] <= i[:, None], 0.0, -1e30)
    t = np.arange(T)
    row = (t // 64 - (T // 64) // 2).astype(np.float32)
    col = (t % 64 - 32).astype(np.float32)
    inv = (np.float32(10000.0) ** (-np.arange(16, dtype=np.float32) / np.float32(16))).astype(np.float32)
    ang = np.concatenate([row[:, None] * inv, col[:, None] * inv], -1).astype(np.float32)
    cs = np.zeros((T, 2, HD), np.float32)
    cs[:, 0] = np.repeat(np.cos(ang), 2, axis=-1)
    cs[:, 1, 0::2] = -np.sin(ang)
    cs[:, 1, 1::2] = np.sin(ang)
    onehot = np.zeros((P, 16), np.float32)
    for b in range(4):
        onehot[32 * b:32 * b + 16] = np.eye(16)
    return c, cs, onehot


def build(nc, a, out):
    with ExitStack() as ctx:
        build_in(ctx, nc, a, out)


def build_in(ctx, nc, a, out):
    def sb(name, shape, dt=F32):
        return ctx.enter_context(nc.sbuf_tensor(name, shape, dt))

    base = (nc.sbuf_base + 31) // 32 * 32
    slab_words = (nc.sbuf_usable_end - base) // 4 // 8 * 8
    ctx.enter_context(nc.sbuf_tensor("slab", [P, slab_words], F32))
    cursor = [base]

    def at(name, shape, offset, dt=F32):
        return nc.alloc_sbuf_tensor_at(name, shape, dt, offset=offset)

    def take(name, shape, dt=F32):
        words = int(np.prod(shape[1:]))
        t = at(name, shape, cursor[0], dt)
        cursor[0] += (4 * words + 31) // 32 * 32
        assert cursor[0] <= base + 4 * slab_words, (name, cursor[0] - base - 4 * slab_words)
        return t

    raw = take("raw", [P, RING, UNIT])
    whi = take("whi", [P, RING, UNIT], F32R)
    wlo = take("wlo", [P, RING, UNIT], F32R)
    xt_at = cursor[0]
    xhi = take("xhi", [P, KD, T], F32R)
    xlo = take("xlo", [P, KD, T], F32R)
    act_at = cursor[0]
    ahi = take("ahi", [P, 2, 2, T], F32R)
    alo = take("alo", [P, 2, 2, T], F32R)
    xres = take("xres", [P, NT, D])
    arena_at = cursor[0]
    ARENA = 86 * KB
    take("arena", [P, ARENA])

    def arena(name, shape, kb):
        assert kb * KB + int(np.prod(shape[1:])) <= ARENA, name
        return at(name, shape, arena_at + 1024 * kb)

    def scratch(name, shape, kb, dt=F32):
        assert kb * KB + int(np.prod(shape[1:])) <= 32 * KB, name
        return at(name, shape, xt_at + 1024 * kb, dt)

    def actmem(name, shape, kb):
        assert kb * KB + int(np.prod(shape[1:])) <= 16 * KB, name
        return at(name, shape, act_at + 1024 * kb)

    consts = take("consts", [P, 4, P])
    ident, tri, ones, cmask = (consts[:, i] for i in range(4))
    NTAB = 6
    tab = take("tab", [P, NTAB * P])
    wf_hi_t = take("wf_hi_t", [P, KD, 16], F32R)
    wf_lo_t = take("wf_lo_t", [P, KD, 16], F32R)
    onehot = take("onehot", [P, 16])
    small = take("small", [P, 4, 16])
    modc = take("modc", [P, 2, 48])
    ccol = take("ccol", [P, KD])
    nscale = take("nscale", [P, 4, KD])
    stats = take("stats", [P, NT, 6, 6])
    mv = take("mv", [P, NT, 2])
    sumsq = take("sumsq", [P, NT, 2])
    std = take("std", [P, NT])
    rstd = take("rstd", [P, NT])
    eps_ln = take("eps_ln", [P, 2])
    warm = take("warm", [P, 8])
    rowst = take("rowst", [P, 3, 64])
    ps = ctx.enter_context(nc.psum_tensor("ps", [P, 8, 512], F32))

    tabraw = arena("tabraw", [P, NTAB, P], 60)
    wf_raw = arena("wf_raw", [P, KD, 16], 84)
    ya_yb = arena("ya_yb", [P, 16, T], 0)
    zs = arena("zs", [P, NT, D], 16)
    xbcT = arena("xbcT", [P, 12, T], 32)
    y_tok = arena("y_tok", [P, NT, D], 32)
    xs_tok = arena("xs_tok", [P, NT, D], 56)
    b_tok = arena("b_tok", [P, NT, 256], 72)
    cv0 = arena("cv0", [P, 2, T], 76)
    hb = actmem("hb", [P, 2, T], 0)
    pb = actmem("pb", [P, 2, T], 4)
    narrow = actmem("narrow", [P, T], 8)
    sm = actmem("sm", [P, 16, NT, 16], 12)
    gbuf = scratch("gbuf", [P, 16, P], 0)
    mbuf = scratch("mbuf", [P, 16, P], 8)
    xdt = [scratch("xdt0", [P, D], 16), actmem("xdt1", [P, D], 0)]
    xdd = [scratch("xdd0", [P, D], 20), actmem("xdd1", [P, D], 4)]
    dskip = arena("dskip", [P, D], 76)
    prev = scratch("prev", [P, D], 24)
    cbm = scratch("cbm", [P, 2, P], 28)
    ssd_sq = scratch("ssd_sq", [P, HALF], 29)
    nrm = arena("nrm", [P, NT, D], 64)
    xf = arena("xf", [P, 2, T], 80)
    gb = actmem("gb", [P, 2, D], 0)
    gate = scratch("gate", [P, D], 0)
    junk = scratch("junk", [P, D], 4)
    gdiag = scratch("gdiag", [P, KD, P], 8)
    hid_ff = arena("hid_ff", [P, NFF, T], 0)
    gt = arena("gt", [P, 2, T], 44)
    ut = arena("ut", [P, 2, T], 48)
    gs = arena("gs", [P, 2, T], 52)
    acc = arena("acc", [P, 48, P], 56)
    gb3 = arena("gb3", [P, 2, D], 44)
    ADA_N = 6 * D // 4
    adaraw = [actmem("adaraw0", [P, ADA_N], 8), arena("adaraw1", [P, ADA_N], 80)]
    qh = arena("qh", [P, 16, T], 0)
    kh = arena("kh", [P, 16, T], 32)
    vtok = arena("vtok", [P, NT, D], 64)
    cumx = actmem("cumx", [P, T], 10)
    ident_r = scratch("ident_r", [P, P], 16, F32R)
    cmask_r = scratch("cmask_r", [P, P], 17, F32R)
    oT1 = scratch("oT1", [P, KD, T], 0)
    pbuf = scratch("pbuf", [P, PSLOTS, T], 20)
    ptb1 = actmem("ptb1", [P, 2, NT, T], 0)
    q_tok = arena("q_tok", [P, NT, D], 0)
    k_tok = arena("k_tok", [P, NT, 256], 16)
    v2 = arena("v2", [P, NT, 256], 20)
    qT2 = arena("qT2", [P, KD, T], 24)
    kT2 = arena("kT2", [P, 2, T], 40)
    cs = arena("cs", [P, NT, 2, HD], 44)
    qkg = arena("qkg", [P, 2, HD], 46)
    oT2 = arena("oT2", [P, KD, T], 48)
    gcs = arena("gcs", [P, 2, NT, 2, HD], 48)
    sqb = arena("sqb", [P, NT, T], 64)
    qn = arena("qn", [P, T], 72)
    ra = arena("ra", [P, T], 74)
    rb = arena("rb", [P, T], 76)
    hsum = arena("hsum", [P, 3, NT, 8], 78)
    ptb2 = scratch("ptb2", [P, 2, NT, T], 0)
    hid_mlp = arena("hid_mlp", [P, NMLP, T], 0)
    relu = arena("relu", [P, 2, T], 80)
    uT = arena("uT", [P, NGM, T], 0)
    vt = [arena(f"vt{t}", [P, GM_HALF], 48 + 12 * t) for t in range(3)] + [actmem("vt3", [P, GM_HALF], 0)]
    bb = actmem("bb", [P, 2, HALF], 12)
    wsT = scratch("wsT", [P, GM_GROUPS, P], 0)
    rs_b = scratch("rs_b", [P, GM_GROUPS, P], 8)
    bs_b = scratch("bs_b", [P, GM_GROUPS, P], 16)
    wsraw = scratch("wsraw", [P, GM_GROUPS, P], 24)
    gz = scratch("gz", [P, 4, T], 24)
    gk = actmem("gk", [P, 2, P], 12)

    def sem(name):
        return ctx.enter_context(nc.semaphore(name))

    raw_in = [sem(f"raw_in{i}") for i in range(RING)]
    w_hi, w_lo = sem("w_hi"), sem("w_lo")
    unit_done = sem("unit_done")
    tile_done = sem("tile_done")
    a_hi, a_lo = sem("a_hi"), sem("a_lo")
    consts_in, small_in = sem("consts_in"), sem("small_in")
    x_in = sem("x_in")
    tab_zero, tab_in, tab_tp, tab_ready = sem("tab_zero"), sem("tab_in"), sem("tab_tp"), sem("tab_ready")
    prep = sem("prep")
    wf_hi, wf_lo, f_mm = sem("wf_hi"), sem("wf_lo"), sem("f_mm")
    narrow_mm, narrow_ev = sem("narrow_mm"), sem("narrow_ev")
    res_add, gated = sem("res_add"), sem("gated")
    stat_done, aggr_done, sq_done, std_done, rstd_done = (
        sem("stat_done"), sem("aggr_done"), sem("sq_done"), sem("std_done"), sem("rstd_done"))
    nrm_done, xt_tp, xt_ev, xt_hi, xt_lo = (
        sem("nrm_done"), sem("xt_tp"), sem("xt_ev"), sem("xt_hi"), sem("xt_lo"))
    gb_in, res_mul, res_done = sem("gb_in"), sem("res_mul"), sem("res_done")
    xbc_aff, xbc_conv, xbc_silu = sem("xbc_aff"), sem("xbc_conv"), sem("xbc_silu")
    sc_h, sc_step, scb_done, z_done = sem("sc_h"), sem("sc_step"), sem("scb_done"), sem("z_done")
    dts, dta = sem("dt_dve"), sem("dt_act")
    tok_tp, tok_ev_a, tok_ev_d = sem("tok_tp"), sem("tok_ev_act"), sem("tok_ev_dve")
    cums_mm, ssd_off, ssd_g, ssd_r, ssd_d, ssd_e, ssd_cbm, ssd_m, ssd_x, ssd_mm, ssd_y, ssd_prev = (
        sem(n) for n in ("cums_mm", "ssd_off", "ssd_g", "ssd_r", "ssd_d", "ssd_e", "ssd_cbm", "ssd_m", "ssd_x", "ssd_mm",
                         "ssd_y", "ssd_prev"))
    gt_u, gt_sq, gt_std, gt_r, gt_n, gt_tp, gt_ev = (
        sem(n) for n in ("gate_u", "gate_sq", "gate_std", "gate_r", "gate_n", "gate_tp", "gate_ev"))
    ff_act, ff_dve = sem("ff_act"), sem("ff_dve")
    ada_in = [sem("ada_in0"), sem("ada_in1")]
    ada_acc, mod_tp, mod_sum, mod_done = sem("ada_acc"), sem("mod_tp"), sem("mod_sum"), sem("mod_done")
    fl_dve, fl_act, cum_mm, aug = sem("fl_dve"), sem("fl_act"), sem("cum_mm"), sem("aug")
    fqk_ev, fv_ev, mask_ready = sem("fqk_ev"), sem("fv_ev"), sem("mask_ready")
    at_s, at_max, at_exp, at_rinv, at_p, at_tp, at_pt, at_pv, at_o = (
        sem(n) for n in ("at_scores", "at_max", "at_exp", "at_rinv", "at_p", "at_tp", "at_pt", "at_pv", "at_o"))
    q_sq, q_sum, q_std, q_step, v_ev, q_tp, q_ev, qkg_in, q_tab = (
        sem(n) for n in ("q_sq", "q_sum", "q_std", "q_step", "v_ev", "q_tp", "q_ev", "qkg_in", "q_tab"))
    gdiag_done, gate_mm, gate_ev = sem("gdiag_done"), sem("gate_mm2"), sem("gate_ev2")
    relu_done, mlp_done = sem("relu_done"), sem("mlp_done")
    gu_ev, bb_in0, bb_in1, gv_add, gv_gelu, gv_stat, gv_aggr, gv_std, gv_rstd, gv_nrm = (
        sem(n) for n in ("gu_ev", "bb_in0", "bb_in1", "gv_add", "gv_gelu", "gv_stat", "gv_aggr", "gv_std",
                         "gv_rstd", "gv_nrm"))
    bb_in = [bb_in0, bb_in1]
    ws_in, bs_in, ws_tp, ws_ev, rs_mm, rs_ev, gm_mm, gm_k, gm_z, gm_up, gm_ud = (
        sem(n) for n in ("ws_in", "bs_in", "ws_tp", "ws_ev", "rs_mm", "rs_ev", "gm_mm", "gm_k", "gm_z", "gm_u_pool", "gm_u_dve"))
    out_in = sem("out_in")

    def rows(ap):
        return ap.rearrange("(c p) -> c p", p=P)

    blocks = [[("scw", a["sc_conv_w"][0].rearrange("k (c p) -> (k c) p", p=P), 24),
               ("ssmw", a["ssm_conv_w"][0].rearrange("k (c p) -> (k c) p", p=P), 48),
               ("ssmb", rows(a["ssm_conv_b"][0]), 12), ("normg", rows(a["ssm_norm_g"][0]), 8),
               ("n1g", a["norm1_g_2"].rearrange("l (c p) -> (l c) p", p=P), 16),
               ("n2g", a["norm2_g_2"].rearrange("l (c p) -> (l c) p", p=P), 16)]]
    for i in range(2):
        cw = a["ffn_conv_w"][i].rearrange("k (h c p) -> k h c p", p=P, h=2)
        blocks.append([(f"cw{i}_0u", cw[0, 0], 22), (f"cw{i}_0g", cw[0, 1], 22), (f"cw{i}_1u", cw[1, 0], 22),
                       (f"cw{i}_1g", cw[1, 1], 22), (f"lnm{i}g", rows(a["ln_mix_g"][i]), 8),
                       (f"lnm{i}b", rows(a["ln_mix_b"][i]), 8)])
        cb = a["ffn_conv_b"][i].rearrange("(h c p) -> h c p", p=P, h=2)
        blocks.append([(f"cw{i}_2u", cw[2, 0], 22), (f"cw{i}_2g", cw[2, 1], 22), (f"cb{i}u", cb[0], 22),
                       (f"cb{i}g", cb[1], 22), (f"lnf{i}g", rows(a["ln_ffn_g"][i]), 8),
                       (f"lnf{i}b", rows(a["ln_ffn_b"][i]), 8),
                       [("gbin", rows(a["gmlp_b_in_2"][0, 0:GM_HALF]), 24),
                        ("glng", rows(a["gmlp_ln_g_2"][0]), 24)][i]])
    blocks.append([("adab", a["ada_b_2"].rearrange("l (c p) -> (l c) p", p=P), 96),
                   ("glnb", rows(a["gmlp_ln_b_2"][0]), 24), ("c", a["c_2"][0].rearrange("(c p) -> c p", p=P), 8)])
    TAB, loads = {}, []
    for b, items in enumerate(blocks):
        r = 0
        for name, ap, k in items:
            TAB[name] = b * P + r
            loads.append((b, r, k, ap))
            r += k
        assert r <= P
    assert len(blocks) == NTAB

    def col(name, i=0):
        if isinstance(i, int):
            return tab[:, TAB[name] + i:TAB[name] + i + 1]
        return tab[:, bass.ds(i + TAB[name], 1)]

    def kview(w):
        return w.rearrange("(c p) n -> p c n", p=P)

    w_in0, w_out0 = kview(a["sc_ssm_w_in"][0]), kview(a["sc_ssm_w_out"][0])
    w_fox, w_fo = kview(a["fox_w_in"][0]), kview(a["fox_w_out"][0])
    w_up = [kview(a["ffn_w_up"][i]) for i in range(2)]
    w_dn = [kview(a["ffn_w_down"][i]) for i in range(2)]
    w_qkv, w_o = kview(a["attn_w_qkv_2"][0]), kview(a["attn_w_o_2"][0])
    w_gin, w_gout = kview(a["gmlp_w_in_2"][0]), kview(a["gmlp_w_out_2"][0])
    w_mi = [kview(a["mlp_w_in_2"][i]) for i in range(2)]
    w_mo = [kview(a["mlp_w_out_2"][i]) for i in range(2)]
    w_ada = [a["ada_w_2"][i].rearrange("(k p) (m n) -> p k m n", p=P, m=4) for i in range(2)]

    def run(eng, n, body):
        q, r = divmod(n, RING)
        if q > 1:
            with eng.Fori(0, q) as i:
                for j in range(RING):
                    body(i * RING + j, j)
        else:
            for j in range(q * RING):
                body(j, j)
        for j in range(r):
            body(q * RING + j, j)

    def wait_raw(eng, start, e, j):
        s = (start + j) % RING
        if isinstance(e, int):
            eng.wait_ge(raw_in[s], 16 * ((start + e) // RING + 1))
        else:
            eng.wait_ge(raw_in[s], (e - j) * 4 + 16 * ((start + j) // RING + 1))

    def sp_value(sp, x):
        if isinstance(x, int):
            return x
        v = sp.snap(x)
        sp.lower_val(v * 4)
        return v

    def f_src(sp, w, c0, e):
        return w[:, :, bass.ds(sp_value(sp, e * P + c0), P)]

    def f_dst(s):
        return raw[:, s].rearrange("p (k n) -> p k n", k=KD)

    def t_dst(s):
        return raw[:, s].rearrange("p (k n) -> p k n", k=2)

    def t_src(sp, w, pair, c0):
        return w[:, bass.ds(sp_value(sp, pair * 2), 2), c0:c0 + HALF]

    def sp_load(sp, start, e, j, src, dst):
        u = start + e
        s = (start + j) % RING
        if not isinstance(u, int):
            sp.wait_ge(w_lo, e + (start - RING + 1))
        elif u >= RING:
            sp.wait_ge(w_lo, u - RING + 1)
        sp.dma_start(dst, src).then_inc(raw_in[s], 16)

    def sp_params(sp):
        sp.wait_ge(tab_zero, 1)
        for b, r, k, ap in loads:
            sp.dma_start(tabraw[r:r + k, b], ap).then_inc(tab_in, 16)
        for i, name in enumerate(("ssm_dt_bias", "ssm_a_log", "ssm_d", "fox_b_f")):
            sp.dma_start(small[:, i], a[name].to_broadcast([P, 16])).then_inc(small_in, 16)
        sp.dma_start(wf_raw[:], w_in0[:, :, DT_COL:DT_COL + 16]).then_inc(small_in, 16)

    def sp_f(sp, name, w, c0, n=None, off=0):
        start, n = U0[name] + off, n or NUNITS[name]
        if start == 0:
            for e in range(RING):
                sp_load(sp, 0, e, e, f_src(sp, w, c0, e), f_dst(e))
            sp_params(sp)
            start, n, c0 = RING, n - RING, c0 + RING * P
        run(sp, n, lambda e, j: sp_load(sp, start, e, j, f_src(sp, w, c0, e), f_dst((start + j) % RING)))

    def sp_pairs(sp, name, w, c_even, c_odd, n):
        start = U0[name]

        def body(i):
            for j in range(RING):
                c0 = (c_even, c_odd)[j % 2] + (j // 2) * P
                s = (start + j) % RING
                at_col = sp_value(sp, i * (2 * P) + c0)
                sp.wait_ge(w_lo, i * RING + (start + j - RING + 1))
                sp.dma_start(f_dst(s), w[:, :, bass.ds(at_col, P)]).then_inc(raw_in[s], 16)

        with sp.Fori(0, n // RING) as i:
            body(i)

    def sp_t(sp, name, w, pairs, cols):
        for h, c0 in enumerate(cols):
            start = U0[name] + h * pairs
            run(sp, pairs, lambda e, j: sp_load(sp, start, e, j, t_src(sp, w, e, c0), t_dst((start + j) % RING)))

    block = ctx.enter_context(nc.Block())

    @block.sync
    def _(sp):
        sp.dma_start(consts[:], a["consts"]).then_inc(consts_in, 16)
        sp_f(sp, "xbc", w_in0, XBC_COL)
        sp_pairs(sp, "scp", w_in0, SC_C, SC_H, 16)
        sp_f(sp, "scb", w_in0, SC_B)
        sp_t(sp, "z", w_in0, 4, [ZCOL, ZCOL + HALF])
        sp_t(sp, "out0", w_out0, 8, [0, HALF])
        sp_pairs(sp, "up0", w_up[0], D_FF, 0, 44)
        sp_t(sp, "dn0", w_dn[0], 11, [0, HALF])
        sp_f(sp, "fqk", w_fox, 0)
        sp_t(sp, "fv", w_fox, 4, [2 * D, 2 * D + HALF])
        sp_t(sp, "fo", w_fo, 4, [0, HALF])
        sp_pairs(sp, "up1", w_up[1], D_FF, 0, 44)
        sp_t(sp, "dn1", w_dn[1], 11, [0, HALF])
        sp_t(sp, "qkv", w_qkv, 4, [D, 0, HALF])
        sp_t(sp, "o", w_o, 4, [0, HALF])
        sp_f(sp, "mu0", w_mi[0], 0)
        sp_t(sp, "md0", w_mo[0], 16, [0, HALF])
        sp_f(sp, "gu", w_gin, 0)
        start = U0["gv"]
        with sp.Fori(0, 6) as h:
            for j in range(4):
                s = (start + j) % RING
                at_col = sp_value(sp, h * HALF + GM_HALF)
                sp.wait_ge(w_lo, h * 4 + (start + j - RING + 1))
                sp.dma_start(t_dst(s), w_gin[:, 2 * j:2 * j + 2, bass.ds(at_col, HALF)]).then_inc(raw_in[s], 16)
        sp_t(sp, "go", w_gout, 12, [0, HALF])
        sp_f(sp, "mu1", w_mi[1], 0)
        sp_t(sp, "md1", w_mo[1], 16, [0, HALF])
        y_out = out[0].rearrange("(t p) d -> p t d", p=P)
        for h in range(2):
            sp.wait_ge(res_add, 60 + 4 * h)
            sp.dma_start(y_out[:, :, h * HALF:(h + 1) * HALF], xres[:, :, h * HALF:(h + 1) * HALF]).then_inc(out_in, 16)
        sp.wait_ge(out_in, 32)

    @block.gpsimd
    def _(pool):
        def lo_part(u, j):
            pool.wait_ge(w_hi, u + 1)
            pool.tensor_tensor(wlo[:, j], raw[:, j], whi[:, j].bitcast(F32), ALU.subtract).then_inc(w_lo, 1)

        turn = U0["go"] // RING
        assert U0["go"] % RING == 0
        with pool.Fori(0, turn) as i:
            for j in range(RING):
                lo_part(i * RING + j, j)
        for j in range(RING - 1):
            lo_part(U0["go"] + j, j)
        for cc in range(NGM):
            if cc % 4 < 3:
                pool.wait_ge(gm_z, cc + 1)
                pool.tensor_tensor(uT[:, cc], uT[:, cc], gz[:, cc % 4], ALU.mult).then_inc(gm_up, 1)
        lo_part(U0["go"] + RING - 1, RING - 1)
        with pool.Fori(turn + 1, TOTAL_UNITS // RING) as i:
            for j in range(RING):
                lo_part(i * RING + j, j)

    LAST = TOTAL_UNITS

    def act_whi(act, start, e, j):
        u, s = start + e, (start + j) % RING
        if isinstance(u, int) and u >= LAST:
            return
        wait_raw(act, start, e, j)
        if not isinstance(u, int):
            act.wait_ge(unit_done, e + (start - RING + 1))
        elif u >= RING:
            act.wait_ge(unit_done, u - RING + 1)
        act.activation(whi[:, s], raw[:, s], ACT.Copy).then_inc(w_hi, 1)

    AHEAD = 3

    def bank_f(j):
        return 4 + j % 4

    def act_params(act):
        act.dma_start(xres[:], a["x"][0].rearrange("(t p) d -> p t d", p=P)).then_inc(x_in, 16)
        act.dma_start(onehot[:], a["onehot"]).then_inc(consts_in, 16)

    TAB_LOADS = 16 * len(loads)

    def act_table(act):
        act.wait_ge(tab_tp, 1)
        act.activation(tab[:, 0:4 * P], ps[:, 0, :], ACT.Copy).then_inc(tab_ready, 1)
        act.wait_ge(tab_tp, 2)
        act.activation(tab[:, 4 * P:6 * P], ps[:, 1, 0:2 * P], ACT.Copy).then_inc(tab_ready, 1)
        act.wait_ge(small_in, 16 * 5)
        act.activation(wf_hi_t[:], wf_raw[:], ACT.Copy).then_inc(wf_hi, 1)
        act.wait_ge(tab_ready, 2)

    def act_xt(act, q, scale, bias):
        for k in range(KD):
            act.wait_ge(xt_tp, KD * q + k + 1)
            if k >= 2:
                act.wait_ge(xt_lo, KD * q + k - 1)
            if scale is None:
                act.activation(xf[:, k % 2], ps[:, k % 4], ACT.Copy).then_inc(xt_ev, 1)
            else:
                act.activation(xf[:, k % 2], ps[:, k % 4], ACT.Identity, scale=scale(k), bias=bias(k)).then_inc(xt_ev, 1)

    def act_xbc(act):
        S = U0["xbc"]

        def tap(e, j):
            act_whi(act, S + AHEAD, e, j)
            act.wait_ge(unit_done, e + (S + 1))
            if not isinstance(e, int) or e >= 2:
                act.wait_ge(xbc_silu, e - 1)
            act.activation(cv0[:, j % 2], ps[:, bank_f(j)], ACT.Identity, scale=col("ssmw", e + 36), bias=col("ssmb", e)
                           ).then_inc(xbc_aff, 1)

        def silu(e, j):
            act.wait_ge(xbc_conv, e * 3 + 3)
            dst = xbcT[:, e:e + 1] if isinstance(e, int) else xbcT[:, bass.ds(e, 1)]
            act.activation(dst, cv0[:, j % 2:j % 2 + 1], ACT.Silu).then_inc(xbc_silu, 1)

        for e in range(RING):
            tap(e, e)
            if e:
                silu(e - 1, e - 1)
        with act.Fori(1, 3) as i:
            for j in range(RING):
                tap(i * RING + j, j)
                silu(i * RING + (j - 1), (j - 1) % RING)
        silu(11, 3)

    def act_narrow(act, q):
        act.wait_ge(narrow_mm, q + 1)
        act.activation(narrow[0:16], ps[0:16, 1], ACT.Copy).then_inc(narrow_ev, 1)

    def act_soft(act, s_dve, s_act):
        act.wait_ge(s_dve, 3)
        act.activation(sm[:, 3], sm[:, 2], ACT.Exp, scale=-1.0).then_inc(s_act, 1)
        act.wait_ge(s_dve, 4)
        act.activation(sm[:, 7], sm[:, 4], ACT.Ln).then_inc(s_act, 1)

    def act_scp(act):
        S = U0["scp"]
        with act.Fori(0, 4) as i:
            for j in range(RING):
                act_whi(act, S + AHEAD, i * RING + j, j)
                if j % 2:
                    act.wait_ge(unit_done, i * RING + (S + j + 1))
                    act.wait_ge(sc_step, i * 8 + (4 * (j // 2) + 1))
                    act.activation(hb[:, j // 2], ps[:, bank_f(j)], ACT.Copy).then_inc(sc_h, 1)

    def act_plain(act, name):
        S, n = U0[name], NUNITS[name]
        run(act, n, lambda e, j: act_whi(act, S + AHEAD, e, j))

    def act_z(act):
        S = U0["z"]
        for e in range(9):
            if e < 8:
                act_whi(act, S + AHEAD, e, e % 4)
            if e and e % 4 == 0:
                h = e // 4 - 1
                act.wait_ge(unit_done, S + 4 * h + 4)
                for t in range(NT):
                    act.activation(zs[:, t, h * HALF:(h + 1) * HALF], ps[:, 4 * h + t], ACT.Silu).then_inc(z_done, 1)

    def act_ssd(act):
        for g in range(0, 12, 2):
            t, r = divmod(g, 3)
            act.wait_ge(tok_tp, g + 1)
            if r < 2:
                act.activation(xs_tok[:, t, r * HALF:(r + 1) * HALF], ps[:, g % 4], ACT.Copy).then_inc(tok_ev_a, 1)
            else:
                act.activation(b_tok[:, t], ps[:, g % 4, 0:256], ACT.Copy).then_inc(tok_ev_a, 1)
        act.wait_ge(dts, 15)
        act.activation(sm[:, 12], sm[:, 15], ACT.Exp).then_inc(dta, 1)
        act.activation(sm[:, 13], sm[:, 11], ACT.Exp).then_inc(dta, 1)
        act.activation(sm[:, 14], ps[:, 1, 64:128].rearrange("p (c h) -> p c h", c=NT), ACT.Exp).then_inc(dta, 1)
        for c in range(NT):
            for g in range(2):
                act.wait_ge(ssd_d, 4 * c + 2 * g + 2)
                act.activation(mbuf[:, 8 * g:8 * g + 8], mbuf[:, 8 * g:8 * g + 8], ACT.Exp).then_inc(ssd_e, 1)
            if c:
                act_gate_squares(act, c - 1)

    def act_gate_squares(act, t):
        act.wait_ge(gt_u, t + 1)
        for g in range(2):
            if t or g:
                act.wait_ge(gt_sq, 2 * t + g)
            act.activation(ssd_sq[:], y_tok[:, t, g * HALF:(g + 1) * HALF], ACT.Square,
                           accum_out=sumsq[:, t, g:g + 1]).then_inc(gt_sq, 1)

    def act_out0_head(act, split, step):
        act.wait_ge(ssd_mm, 4)
        split(0, 0, 0, 0)
        split(1, 0, 0, 1)
        act_gate_squares(act, NT - 1)
        act.wait_ge(gt_sq, 8)
        act.activation(mv[:], sumsq[:], ACT.Sqrt, scale=1.0 / HALF, bias=eps_ln[:, 0:1]).then_inc(gt_std, 1)
        step(2, 2, 0, 0)
        step(3, 3, 0, 0)
        for k in range(KD):
            act.wait_ge(gt_tp, k + 1)
            act.activation(ya_yb[:, 8 + k], ps[:, 4 + k % 4], ACT.Copy, scale=col("normg", k)).then_inc(gt_ev, 1)
        act.wait_ge(gt_ev, 8)

    def act_first_splits(act, src):
        for m in range(2):
            act.activation(ahi[:, m], src[:, 2 * m:2 * m + 2], ACT.Copy).then_inc(a_hi, 1)

    def act_jit(act, name, src, after_h0=None, last=False, head=None):
        H, S, A = PAIRS[name], U0[name], A0[name]

        def split(m0, e, j, k0):
            k = k0 + e
            x = src[:, 2 * k:2 * k + 2] if isinstance(k, int) else src[:, bass.ds(e * 2 + 2 * k0, 2)]
            act.activation(ahi[:, (m0 + j) % 2], x, ACT.Copy).then_inc(a_hi, 1)

        def step(m0, k0, e, j, whi_too=True):
            if whi_too:
                act_whi(act, S + m0 + 1, e, j)
            act.wait_ge(unit_done, e + (S + m0 - 1))
            split(m0, e, j, k0)

        first = 2
        if head:
            head(act, split, step)
            first = 4
        else:
            split(0, 0, 0, 0)
            split(1, 0, 0, 1)
        run(act, H - first, lambda e, j: step(first, first, e, j))
        for e in range(3):
            step(H + e, e, 0, 0)
        if after_h0:
            after_h0()
        n = H - 3 - (1 if last else 0)
        if n:
            run(act, n, lambda e, j: step(H + 3, 3, e, j))
        if last:
            step(2 * H - 1, H - 1, 0, 0, whi_too=False)

    def act_next_whi(act, name):
        act_whi(act, END[name] + 1, 0, 0)
        act_whi(act, END[name] + 2, 0, 0)

    def act_sqrt_table(act, n):
        act.activation(warm[:, n:n + 1], eps_ln[:, 0:1], ACT.Sqrt)

    def load_gb(act, dst, g_ap, b_ap):
        act.dma_start(dst[:, 0], g_ap.to_broadcast([P, D])).then_inc(gb_in, 16)
        act.dma_start(dst[:, 1], b_ap.to_broadcast([P, D])).then_inc(gb_in, 16)

    def act_ln(act, q, name, g_ap, b_ap):
        act.wait_ge(unit_done, END[name])
        if q < 3:
            load_gb(act, gb, g_ap, b_ap)
        act_sqrt_table(act, q)
        act.wait_ge(aggr_done, NT * (q + 1))
        act.activation(std[:], mv[:, :, 1], ACT.Sqrt, bias=eps_ln[:, 0:1]).then_inc(std_done, 1)
        act_next_whi(act, name)

    def act_ffn(act, L):
        S, FA, FD = U0[f"up{L}"], 66 * L, 110 * L
        for lo, hi, ada in FFN_PARTS:
            if lo == 10:
                act_first_splits(act, hid_ff)
            with act.Fori(lo, hi) as i:
                for b in range(2):
                    pr = i * 2 + b
                    act_whi(act, S + AHEAD, i * RING + 2 * b, 2 * b)
                    act.wait_ge(unit_done, i * RING + (S + 2 * b + 1))
                    act.activation(gt[:, b], ps[:, bank_f(2 * b)], ACT.Identity, scale=col(f"cw{L}_2g", pr),
                                   bias=col(f"cb{L}g", pr)).then_inc(ff_act, 1)
                    if ada:
                        for s in range(2):
                            if lo == 0:
                                act.wait_ge(xt_lo, KD * (2 * L + 2))
                            if lo or b:
                                act.wait_ge(ada_acc, i * 4 + (32 * L + 2 * b + s - 1))
                            act.dma_start(adaraw[s][:], w_ada[L][:, bass.ds(i, 1), 2 * b + s]).then_inc(ada_in[s], 16)
                    act.wait_ge(ff_dve, i * 10 + (FD + 5 * b + 2))
                    act.activation(gs[:, b], gt[:, b], ACT.Silu).then_inc(ff_act, 1)
                    act_whi(act, S + AHEAD, i * RING + 2 * b + 1, 2 * b + 1)
                    act.wait_ge(unit_done, i * RING + (S + 2 * b + 2))
                    act.activation(ut[:, b], ps[:, bank_f(2 * b + 1)], ACT.Identity, scale=col(f"cw{L}_2u", pr),
                                   bias=col(f"cb{L}u", pr)).then_inc(ff_act, 1)

    def act_fox_qk(act):
        S = U0["fqk"]
        for k0, dst, scale in ((0, qh, HD ** -0.5), (8, kh, 1.0)):
            def unit(e, j):
                act_whi(act, S + k0 + AHEAD, e, j)
                act.wait_ge(unit_done, e + (S + k0 + 1))
                for b in range(2):
                    r = slice(64 * b, 64 * b + 64)
                    d = dst[r, 2 * e + b:2 * e + b + 1] if isinstance(e, int) else dst[r, bass.ds(e * 2 + b, 1)]
                    act.activation(d, ps[r, bank_f(j):bank_f(j) + 1], ACT.Copy, scale=scale).then_inc(fqk_ev, 1)

            run(act, 8, unit)

    def act_attn(act, A, ptb, causal, hook=None):
        B = 64 * A
        for n in range(64 + LEAD):
            if n == 56 and hook:
                hook()
            if n < 64:
                N = (n % 4 + 1) * P if causal else T
                act.wait_ge(at_max, B + n + 1)
                if n >= PSLOTS:
                    act.wait_ge(at_tp, B + n - PSLOTS + 1)
                act.activation(pbuf[:, n % PSLOTS, 0:N], ps[:, SBANKS[n % 4], 0:N], ACT.Exp, bias=rowst[:, 0, n:n + 1],
                               accum_out=rowst[:, 1, n:n + 1]).then_inc(at_exp, 1)
            m = n - LEAD
            if m >= 0:
                h, i = divmod(m, 4)
                c = i + 1 if causal else NT
                act.wait_ge(at_tp, B + m + 1)
                if i == 0 and h >= 2:
                    act.wait_ge(at_pv, 16 * A + h - 1)
                act.activation(ptb[:, h % 2, 0:c, i * P:(i + 1) * P],
                               ps[:, 3 + m % 2, 0:c * P].rearrange("p (c q) -> p c q", c=c), ACT.Copy).then_inc(at_pt, 1)

    def act_square(act, s, h, tiles_ready):
        for t in range(NT):
            tiles_ready(t)
            if t:
                act.wait_ge(sq_done, 8 * s + 4 * h + t)
            act.activation(junk[:, h * HALF:(h + 1) * HALF], xres[:, t, h * HALF:(h + 1) * HALF], ACT.Square,
                           accum_out=sumsq[:, t, h:h + 1]).then_inc(sq_done, 1)

    def act_rms(act, s):
        act.wait_ge(aggr_done, 16 + s + 1)
        act.activation(std[:], mv[:, :, 0], ACT.Sqrt, scale=1.0 / D, bias=eps_ln[:, 1:2]).then_inc(std_done, 1)

    def act_qkv(act):
        S = U0["qkv"]
        act.dma_start(cs[:], a["cs"].rearrange("(t p) a d -> p t a d", p=P)).then_inc(qkg_in, 16)
        act.dma_start(qkg[:, 0], a["attn_q_norm_g_2"].to_broadcast([P, HD])).then_inc(qkg_in, 16)
        act.dma_start(qkg[:, 1], a["attn_k_norm_g_2"].to_broadcast([P, HD])).then_inc(qkg_in, 16)
        for e in range(13):
            if e < 12:
                act_whi(act, S + AHEAD, e, e % 4)
            if e and e % 4 == 0:
                hh = e // 4 - 1
                nh = 4 if hh == 0 else 8
                act.wait_ge(unit_done, S + 4 * hh + 4)
                if hh:
                    act.wait_ge(q_sum, 5 * hh)
                for t in range(NT):
                    act.activation(sqb[:, t, 0:nh * HD], ps[:, 4 * (hh % 2) + t, 0:nh * HD], ACT.Square).then_inc(q_sq, 1)
                    if hh == 0:
                        act.activation(v2[:, t], ps[:, t, 256:512], ACT.Copy).then_inc(v_ev, 1)
                act.wait_ge(q_sum, 5 * hh + 4)
                act.activation(hsum[:, 1, :, 0:nh], hsum[:, 0, :, 0:nh], ACT.Sqrt, scale=1.0 / HD,
                               bias=eps_ln[:, 1:2]).then_inc(q_std, 1)
        for r in range(10):
            act.wait_ge(q_tp, r + 1)
            if r < 2:
                act.activation(kT2[:, r], ps[:, 4 + r % 4], ACT.Copy).then_inc(q_ev, 1)
            else:
                for b in range(2):
                    h = 2 * (r - 2) + b
                    g = h // 4
                    kb = 64 * (g % 2)
                    act.activation(qT2[kb:kb + 64, (g // 2) * 4 + h % 4], ps[64 * b:64 * b + 64, 4 + r % 4],
                                   ACT.Copy, scale=HD ** -0.5).then_inc(q_ev, 1)

    def act_gate(act, s):
        act.wait_ge(gate_mm, s + 1)
        act.activation(gate[:], ps[:, 4:6], ACT.Copy).then_inc(gate_ev, 1)

    def act_mlp(act, L):
        S = U0[f"mu{L}"]

        def unit(e, j):
            act_whi(act, S + AHEAD, e, j)
            act.wait_ge(unit_done, e + (S + 1))
            v = e + (32 * L - 1)
            if not isinstance(v, int) or v > 0:
                act.wait_ge(mlp_done, v)
            act.activation(relu[:, j % 2], ps[:, bank_f(j)], ACT.Relu).then_inc(relu_done, 1)

        for e in range(4):
            unit(e, e)
        with act.Fori(1, 7) as i:
            for j in range(4):
                unit(i * 4 + j, j)
        act_first_splits(act, hid_mlp)
        for e in range(28, 32):
            unit(e, e % 4)

    def act_gu(act):
        S = U0["gu"]

        def unit(e, j):
            act_whi(act, S + AHEAD, e, j)
            act.wait_ge(unit_done, e + (S + 1))
            d = uT[:, e:e + 1] if isinstance(e, int) else uT[:, bass.ds(e, 1)]
            act.activation(d, ps[:, bank_f(j):bank_f(j) + 1], ACT.Gelu, bias=col("gbin", e)).then_inc(gu_ev, 1)

        run(act, 24, unit)

    def act_gv(act):
        S = U0["gv"]

        def load_bias(hh):
            if hh >= 2:
                act.wait_ge(gv_add, 4 * (hh - 1))
            c0 = GM_HALF + hh * HALF
            act.dma_start(bb[:, hh % 2], a["gmlp_b_in_2"][:, c0:c0 + HALF].to_broadcast([P, HALF])
                          ).then_inc(bb_in[hh % 2], 16)

        load_bias(0)
        load_bias(1)
        for e in range(25):
            if e < 24:
                act_whi(act, S + AHEAD, e, e % 4)
            if e and e % 4 == 0:
                hh = e // 4 - 1
                for t in range(NT):
                    act.wait_ge(gv_add, 4 * hh + t + 1)
                    v = vt[t][:, hh * HALF:(hh + 1) * HALF]
                    act.activation(v, v, ACT.Gelu).then_inc(gv_gelu, 1)
                if hh + 2 < 6:
                    load_bias(hh + 2)
        act.wait_ge(unit_done, END["gv"])
        act.dma_start(wsraw[:], a["gmlp_w_s_2"][0].rearrange("g p q -> p g q")).then_inc(ws_in, 16)
        act.dma_start(bs_b[:], a["gmlp_b_s_2"][0].rearrange("g p -> (g p)").unsqueeze(0).to_broadcast([P, GM_GROUPS * P])
                      .rearrange("q (g p) -> q g p", g=GM_GROUPS)).then_inc(bs_in, 16)
        act.wait_ge(gv_aggr, 4)
        act.activation(std[:], mv[:, :, 1], ACT.Sqrt, bias=eps_ln[:, 1:2]).then_inc(gv_std, 1)
        for b in range(4):
            act.wait_ge(ws_tp, b + 1)
            act.activation(wsT[:, 4 * b:4 * b + 4], ps[:, b], ACT.Copy).then_inc(ws_ev, 1)
        for b in range(4):
            act.wait_ge(rs_mm, b + 1)
            act.activation(rs_b[:, 4 * b:4 * b + 4], ps[:, b], ACT.Copy).then_inc(rs_ev, 1)

    def ffn_head(L):
        def head(act, split, step):
            step(2, 2, 0, 0)
            step(3, 3, 0, 0)
            act.wait_ge(ff_dve, 110 * (L + 1))
            if L == 1:
                load_gb(act, gb3, a["ln_ffn_g"][1:2], a["ln_ffn_b"][1:2])

        return head

    def gate_head(s):
        def head(act, split, step):
            if s == 2:
                split(0, 0, 0, 0)
                split(1, 0, 0, 1)
                act.wait_ge(gm_up, 18)
                act.wait_ge(gm_ud, 6)
            if s == 0:
                act.wait_ge(at_o, 14)
            step(2, 2, 0, 0)
            if s == 0:
                act.wait_ge(at_o, 16)
            step(3, 3, 0, 0)
            if s == 1 or s == 3:
                act.wait_ge(mlp_done, 32 if s == 1 else 64)
            act_gate(act, s)

        return head

    @block.scalar
    def _(act):
        act_params(act)
        for u in range(AHEAD):
            act_whi(act, u, 0, 0)
        act.wait_ge(consts_in, 32)
        act_xt(act, 0, None, None)
        act_table(act)
        act_xbc(act)
        act.activation(ccol[:], tab[:, TAB["c"]:TAB["c"] + KD], ACT.Silu).then_inc(prep, 1)
        act_narrow(act, 0)
        act_soft(act, dts, dta)
        act.wait_ge(small_in, 16 * 5)
        act.activation(sm[:, 8, 0], small[:, 1], ACT.Exp).then_inc(dta, 1)
        act_scp(act)
        act_plain(act, "scb")
        act_z(act)
        act_ssd(act)
        act_jit(act, "out0", ya_yb, head=act_out0_head)
        act_ln(act, 0, "out0", a["ln_mix_g"][0:1], a["ln_mix_b"][0:1])
        act_xt(act, 1, lambda k: col("lnm0g", k), lambda k: col("lnm0b", k))
        act_ffn(act, 0)
        act_jit(act, "dn0", hid_ff, head=ffn_head(0))
        act_ln(act, 1, "dn0", a["ln_ffn_g"][0:1], a["ln_ffn_b"][0:1])
        act.dma_start(wf_raw[:], w_fox[:, :, 3 * D:3 * D + 16]).then_inc(small_in, 16)
        act_xt(act, 2, lambda k: col("lnf0g", k), lambda k: col("lnf0b", k))
        act.wait_ge(small_in, 16 * 6)
        act.activation(wf_hi_t[:], wf_raw[:], ACT.Copy).then_inc(wf_hi, 1)
        act_narrow(act, 1)
        act_soft(act, fl_dve, fl_act)
        act_fox_qk(act)
        act_plain(act, "fv")
        act.wait_ge(unit_done, END["fv"])
        act.activation(ident_r[:], ident, ACT.Copy).then_inc(mask_ready, 1)
        act.activation(cmask_r[:], cmask, ACT.Copy).then_inc(mask_ready, 1)
        act_attn(act, 0, ptb1, True)
        act.wait_ge(at_o, 8)
        act_jit(act, "fo", oT1)
        act_ln(act, 2, "fo", a["ln_mix_g"][1:2], a["ln_mix_b"][1:2])
        act_xt(act, 3, lambda k: col("lnm1g", k), lambda k: col("lnm1b", k))
        act_ffn(act, 1)
        act_jit(act, "dn1", hid_ff, head=ffn_head(1))
        act_ln(act, 3, "dn1", a["ln_ffn_g"][1:2], a["ln_ffn_b"][1:2])
        for t in range(NT):
            act.wait_ge(res_done, 12 + t + 1)
            for h in range(2):
                if 2 * t + h:
                    act.wait_ge(sq_done, 2 * t + h)
                act.activation(junk[:, h * HALF:(h + 1) * HALF], xres[:, t, h * HALF:(h + 1) * HALF], ACT.Square,
                               accum_out=sumsq[:, t, h:h + 1]).then_inc(sq_done, 1)
        norm_scale = lambda s: (lambda k: nscale[:, s, k:k + 1])
        norm_shift = lambda s: (lambda k: modc[:, s // 2, 24 * (s % 2) + k:24 * (s % 2) + k + 1])
        act_rms(act, 0)
        act_xt(act, 4, norm_scale(0), norm_shift(0))
        act_qkv(act)
        act_attn(act, 1, ptb2, False, hook=lambda: (act.wait_ge(at_o, 12), act_first_splits(act, oT2)))
        for s, (name, src) in enumerate((("o", oT2), ("md0", hid_mlp), ("go", uT), ("md1", hid_mlp))):
            if name == "md0":
                act_mlp(act, 0)
            if name == "go":
                act_gu(act)
                act_gv(act)
                act.wait_ge(gm_mm, NGM)
            if name == "md1":
                act_mlp(act, 1)
            r = 4 + s

            def squares(h, r=r, s=s):
                act_square(act, s + 1, h, lambda t: act.wait_ge(res_add, 8 * r + 4 * h + t + 1))

            if name == "md1":
                act_jit(act, name, src, last=True, head=gate_head(s))
            else:
                act_jit(act, name, src, after_h0=lambda: squares(0), head=gate_head(s))
                act_sqrt_table(act, 4 + s)
                squares(1)
                act_rms(act, s + 1)
                act_next_whi(act, name)
                act_xt(act, 5 + s, norm_scale(s + 1), norm_shift(s + 1))

    def dve_xt(dve, q):
        for k in range(KD):
            dve.wait_ge(xt_ev, KD * q + k + 1)
            dve.tensor_copy(xhi[:, k], xf[:, k % 2]).then_inc(xt_hi, 1)
            dve.wait_ge(xt_hi, KD * q + k + 1)
            dve.tensor_tensor(xlo[:, k], xf[:, k % 2], xhi[:, k].bitcast(F32), ALU.subtract).then_inc(xt_lo, 1)

    def dve_xbc(dve):
        with dve.Fori(0, 3) as i:
            for j in range(4):
                c, src = cv0[:, j % 2], ps[:, bank_f(j)]
                dve.wait_ge(xbc_aff, i * 4 + (j + 1))
                for k in range(3):
                    d = k + 1
                    if k:
                        dve.wait_ge(xbc_conv, i * 12 + (3 * j + k))
                    dve.scalar_tensor_tensor(c[:, d:], src[:, :T - d], col("ssmw", i * 4 + (12 * (2 - k) + j)), c[:, d:],
                                             ALU.mult, ALU.add).then_inc(xbc_conv, 1)

    def dve_soft(dve, s_dve, s_act, base_mm, bias, positive, dst):
        n = [0]

        def step(ins):
            ins.then_inc(s_dve, 1)
            n[0] += 1
            dve.wait_ge(s_dve, n[0])

        dve.wait_ge(f_mm, base_mm)
        step(dve.tensor_tensor(sm[:, 0], ps[:, 0, 0:64].rearrange("p (c h) -> p c h", c=NT),
                               bias.unsqueeze(1).to_broadcast([P, NT, 16]), ALU.add))
        step(dve.tensor_scalar(sm[:, 1], sm[:, 0], -1.0, None, ALU.mult))
        step(dve.tensor_tensor(sm[:, 2], sm[:, 0], sm[:, 1], ALU.max))
        dve.wait_ge(s_act, 1)
        step(dve.tensor_scalar(sm[:, 4], sm[:, 3], 1.0, None, ALU.add))
        step(dve.tensor_scalar(sm[:, 5], sm[:, 4], -1.0, None, ALU.add))
        step(dve.tensor_scalar(sm[:, 6], sm[:, 5], 0.0, None, ALU.is_equal))
        step(dve.tensor_tensor(sm[:, 5], sm[:, 5], sm[:, 6], ALU.add))
        step(dve.reciprocal(sm[:, 5], sm[:, 5]))
        dve.wait_ge(s_act, 2)
        step(dve.tensor_tensor(sm[:, 7], sm[:, 7], sm[:, 6], ALU.add))
        step(dve.tensor_tensor(sm[:, 7], sm[:, 7], sm[:, 5], ALU.mult))
        step(dve.tensor_tensor(sm[:, 7], sm[:, 7], sm[:, 3], ALU.mult))
        if positive:
            step(dve.scalar_tensor_tensor(dst, sm[:, 0], 0.0, sm[:, 7], ALU.max, ALU.add))
        else:
            step(dve.scalar_tensor_tensor(dst, sm[:, 0], 0.0, sm[:, 7], ALU.min, ALU.subtract))
        return n[0]

    def dve_scp(dve):
        with dve.Fori(0, 4) as i:
            for b in range(2):
                p, y = pb[:, b:b + 1], ya_yb[:, bass.ds(i * 2 + b, 1)]
                s = i * 8 + (4 * b + 1)
                dve.wait_ge(sc_h, i * 2 + (b + 1))
                dve.tensor_tensor(p, ps[:, bank_f(2 * b):bank_f(2 * b) + 1], hb[:, b:b + 1], ALU.mult).then_inc(sc_step, 1)
                dve.wait_ge(sc_step, s + 1)
                dve.tensor_scalar(y, p, col("scw", i * 2 + (16 + b)), None, ALU.mult).then_inc(sc_step, 1)
                for k in range(2):
                    d = k + 1
                    dve.wait_ge(sc_step, s + 2 + k)
                    yd = ya_yb[:, bass.ds(i * 2 + b, 1), d:]
                    dve.scalar_tensor_tensor(yd, pb[:, b:b + 1, :T - d], col("scw", i * 2 + (8 * (1 - k) + b)), yd,
                                             ALU.mult, ALU.add).then_inc(sc_step, 1)

    def dve_scb(dve):
        S = U0["scb"]
        dve.wait_ge(sc_step, 33)

        def unit(e, j):
            dve.wait_ge(unit_done, e + (S + 1))
            y = ya_yb[:, bass.ds(e, 1)]
            dve.tensor_tensor(y, ps[:, bank_f(j):bank_f(j) + 1], y, ALU.mult).then_inc(scb_done, 1)

        run(dve, 8, unit)

    def bc_h(x):
        return x.unsqueeze(2).to_broadcast([P, 16, HD])

    def heads(x):
        return x.rearrange("p (h d) -> p h d", d=HD)

    def dve_ssd(dve):
        for g in range(1, 12, 2):
            t, r = divmod(g, 3)
            dve.wait_ge(tok_tp, g + 1)
            if r < 2:
                dve.tensor_copy(xs_tok[:, t, r * HALF:(r + 1) * HALF], ps[:, g % 4]).then_inc(tok_ev_d, 1)
            else:
                dve.tensor_copy(b_tok[:, t], ps[:, g % 4, 0:256]).then_inc(tok_ev_d, 1)
        dve.wait_ge(cums_mm, 1)
        dve.tensor_copy(sm[:, 11], ps[:, 1, 0:64].rearrange("p (c h) -> p c h", c=NT)).then_inc(dts, 1)
        dve.wait_ge(dts, 14)
        dve.tensor_tensor(sm[:, 15], ps[:, 1, 64:128].rearrange("p (c h) -> p c h", c=NT), sm[:, 11], ALU.subtract
                          ).then_inc(dts, 1)
        ny, nprev = 0, 0

        def ystep(ins):
            nonlocal ny
            ins.then_inc(ssd_y, 1)
            ny += 1

        def inputs(c):
            dve.tensor_tensor(gbuf[:], tri.unsqueeze(1).to_broadcast([P, 16, P]),
                              sm[:, 10, c].unsqueeze(2).to_broadcast([P, 16, P]), ALU.mult).then_inc(ssd_g, 1)
            if c == 0:
                dve.wait_ge(tok_ev_a, 6)
                dve.wait_ge(tok_ev_d, 6)
            dve.tensor_tensor(heads(xdt[c % 2][:]), heads(xs_tok[:, c]), bc_h(sm[:, 9, c]), ALU.mult).then_inc(ssd_x, 1)
            if c == 0:
                dve.wait_ge(dta, 6)
            dve.wait_ge(ssd_x, 2 * c + 1)
            dve.tensor_tensor(heads(xdd[c % 2][:]), heads(xdt[c % 2][:]), bc_h(sm[:, 12, c]), ALU.mult).then_inc(ssd_x, 1)

        inputs(0)
        for c in range(NT):
            acs_c = sm[:, 11, c]
            for g in range(2):
                m = mbuf[:, 8 * g:8 * g + 8]
                dve.wait_ge(ssd_r, 2 * c + g + 1)
                dve.tensor_tensor(m, ps[:, 2 + 4 * g:4 + 4 * g].rearrange("p b (h t) -> p (b h) t", t=P),
                                  acs_c[:, 8 * g:8 * g + 8].unsqueeze(2).to_broadcast([P, 8, P]), ALU.subtract
                                  ).then_inc(ssd_d, 1)
                dve.wait_ge(ssd_d, 4 * c + 2 * g + 1)
                dve.tensor_scalar(m, m, 0.0, None, ALU.min).then_inc(ssd_d, 1)
            dve.tensor_tensor(cbm[:], ps[:, 0, 0:256].rearrange("p (g t) -> p g t", g=2),
                              tri.unsqueeze(1).to_broadcast([P, 2, P]), ALU.mult).then_inc(ssd_cbm, 1)
            y = y_tok[:, c]
            if c:
                dve.wait_ge(ssd_off, c)
                ystep(dve.tensor_tensor(heads(y), ps[:, 4:6].rearrange("p b (h d) -> p (b h) d", d=HD),
                                        bc_h(sm[:, 13, c]), ALU.mult))
            dve.wait_ge(ssd_cbm, c + 1)
            for g in range(2):
                dve.wait_ge(ssd_e, 2 * c + g + 1)
                dve.tensor_tensor(mbuf[:, 8 * g:8 * g + 8], mbuf[:, 8 * g:8 * g + 8],
                                  cbm[:, g].unsqueeze(1).to_broadcast([P, 8, P]), ALU.mult).then_inc(ssd_m, 1)
            if c < NT - 1:
                inputs(c + 1)
            if c == 0:
                ystep(dve.tensor_tensor(heads(y), heads(xs_tok[:, c]), bc_h(small[:, 2]), ALU.mult))
            else:
                ystep(dve.tensor_tensor(heads(dskip[:]), heads(xs_tok[:, c]), bc_h(small[:, 2]), ALU.mult))
                if c < NT - 1:
                    dve.tensor_tensor(heads(prev[:]), heads(prev[:]), bc_h(sm[:, 14, c]), ALU.mult).then_inc(ssd_prev, 1)
                    nprev += 1
                dve.wait_ge(ssd_y, ny)
                ystep(dve.tensor_tensor(y, y, dskip[:], ALU.add))
            dve.wait_ge(ssd_y, ny)
            dve.wait_ge(ssd_mm, c + 1)
            if c < NT - 1:
                st = ps[:, 6:8].rearrange("p b n -> p (b n)")
                if c == 0:
                    dve.tensor_copy(prev[:], st).then_inc(ssd_prev, 1)
                else:
                    dve.wait_ge(ssd_prev, nprev)
                    dve.tensor_tensor(prev[:], st, prev[:], ALU.add).then_inc(ssd_prev, 1)
                nprev += 1
            ystep(dve.tensor_tensor(y, ps[:, 4:6].rearrange("p b n -> p (b n)"), y, ALU.add))
            if c == 0:
                dve.wait_ge(z_done, 8)
            dve.wait_ge(ssd_y, ny)
            dve.tensor_tensor(y, y, zs[:, c], ALU.mult).then_inc(gt_u, 1)

    def dve_gate_norm(dve):
        dve.wait_ge(gt_std, 1)
        dve.reciprocal(mv[:], mv[:]).then_inc(gt_r, 1)
        dve.wait_ge(gt_r, 1)
        for t in range(NT):
            for g in range(2):
                y = y_tok[:, t, g * HALF:(g + 1) * HALF]
                dve.tensor_scalar(y, y, mv[:, t, g:g + 1], None, ALU.mult).then_inc(gt_n, 1)

    def dve_first_splits(dve, name, src):
        for m in range(2):
            dve.wait_ge(a_hi, A0[name] + m + 1)
            dve.tensor_tensor(alo[:, m], src[:, 2 * m:2 * m + 2], ahi[:, m].bitcast(F32), ALU.subtract).then_inc(a_lo, 1)

    def dve_jit(dve, name, src, after_h0, head=None, head_at=2, done=0):
        H, A = PAIRS[name], A0[name]

        def step(m0, k0, e, j):
            dve.wait_ge(a_hi, e + (A + m0 + 1))
            x = src[:, 2 * (k0 + e):2 * (k0 + e) + 2] if isinstance(e, int) else src[:, bass.ds(e * 2 + 2 * k0, 2)]
            s = (m0 + j) % 2
            dve.tensor_tensor(alo[:, s], x, ahi[:, s].bitcast(F32), ALU.subtract).then_inc(a_lo, 1)

        first = 0
        if head:
            for e in range(done, head_at):
                step(e, e, 0, 0)
            head(dve)
            first = head_at
        run(dve, H - first, lambda e, j: step(first, first, e, j))
        for e in range(2):
            step(H, 0, e, e)
        after_h0()
        run(dve, H - 2, lambda e, j: step(H + 2, 2, e, j))

    def wait_tile(eng, r, name, t):
        if t < NT - 1:
            eng.wait_ge(tile_done, 3 * r + t + 1)
        else:
            eng.wait_ge(unit_done, END[name])

    def dve_ln_half(dve, r, name, h):
        if h == 0:
            dve.wait_ge(unit_done, U0[name] + PAIRS[name])
            if r:
                dve.wait_ge(res_done, 4 * r)
        for t in range(NT):
            if h:
                wait_tile(dve, r, name, t)
            x = xres[:, t, h * HALF:(h + 1) * HALF]
            n = 8 * r + 4 * h + t + 1
            dve.scalar_tensor_tensor(x, x, ALPHA, ps[:, 4 * h + t], ALU.mult, ALU.add).then_inc(res_add, 1)
            dve.wait_ge(res_add, n)
            dve.bn_stats(stats[:, t, h], x).then_inc(stat_done, 1)

    def dve_ln_end(dve, r, to_nrm=True):
        dve.wait_ge(stat_done, 8 * r + 8)
        for t in range(NT):
            dve.bn_aggr(mv[:, t], stats[:, t, 0:2].rearrange("p a b -> p (a b)")).then_inc(aggr_done, 1)
        dve.wait_ge(std_done, r + 1)
        dve.reciprocal(rstd[:], std[:]).then_inc(rstd_done, 1)
        dve.wait_ge(rstd_done, r + 1)
        if not to_nrm:
            dve.wait_ge(gb_in, 32 * (r + 1))
            for t in range(NT + 1):
                if t < NT:
                    dve.scalar_tensor_tensor(xres[:, t], xres[:, t], mv[:, t, 0:1], gb3[:, 0], ALU.subtract, ALU.mult
                                             ).then_inc(res_mul, 1)
                if t:
                    dve.wait_ge(res_mul, 4 * r + t)
                    dve.scalar_tensor_tensor(xres[:, t - 1], xres[:, t - 1], rstd[:, t - 1:t], gb3[:, 1], ALU.mult, ALU.add
                                             ).then_inc(res_done, 1)
            return
        for h in range(2):
            c = slice(h * HALF, (h + 1) * HALF)
            for t in range(NT):
                dve.tensor_scalar(nrm[:, t, c], xres[:, t, c], mv[:, t, 0:1], rstd[:, t:t + 1], ALU.subtract, ALU.mult
                                  ).then_inc(nrm_done, 1)

    def dve_resid(dve, r):
        dve.wait_ge(gb_in, 32 * (r + 1))
        dve.wait_ge(nrm_done, 8 * r + 8)
        for t in range(NT + 1):
            if t < NT:
                dve.tensor_tensor(xres[:, t], nrm[:, t], gb[:, 0], ALU.mult).then_inc(res_mul, 1)
            if t:
                dve.wait_ge(res_mul, 4 * r + t)
                dve.tensor_tensor(xres[:, t - 1], xres[:, t - 1], gb[:, 1], ALU.add).then_inc(res_done, 1)

    def dve_ffn(dve, L):
        FA, FD = 66 * L, 110 * L
        accf = acc[:].rearrange("p m n -> p (m n)")
        for lo, hi, ada in FFN_PARTS:
            if lo == 10:
                dve_first_splits(dve, f"dn{L}", hid_ff)
            with dve.Fori(lo, hi) as i:
                for b in range(2):
                    pr = i * 2 + b
                    for z, (x, half, w) in enumerate(((gt, 2 * b, "g"), (ut, 2 * b + 1, "u"))):
                        dve.wait_ge(ff_act, i * 6 + (FA + 3 * b + 1 + 2 * z))
                        for k in range(2):
                            d = k + 1
                            if k:
                                dve.wait_ge(ff_dve, i * 10 + (FD + 5 * b + 2 * z + 1))
                            dve.scalar_tensor_tensor(x[:, b, d:], ps[:, bank_f(half), :T - d], col(f"cw{L}_{1 - k}{w}", pr),
                                                     x[:, b, d:], ALU.mult, ALU.add).then_inc(ff_dve, 1)
                    dve.wait_ge(ff_dve, i * 10 + (FD + 5 * b + 4))
                    dve.tensor_tensor(hid_ff[:, bass.ds(pr, 1)], ut[:, b:b + 1], gs[:, b:b + 1], ALU.mult
                                      ).then_inc(ff_dve, 1)
                    if ada:
                        for s in range(2):
                            m = 2 * b + s
                            dve.wait_ge(ada_in[s], i * 32 + 16 * (b + 1 + 16 * L))
                            x = accf[:, m * ADA_N:(m + 1) * ADA_N]
                            if lo == 0:
                                dve.tensor_scalar(x, adaraw[s][:], ccol[:, 0:1], None, ALU.mult).then_inc(ada_acc, 1)
                            else:
                                dve.wait_ge(ada_acc, i * 4 + (32 * L + m - 3))
                                dve.scalar_tensor_tensor(x, adaraw[s][:], ccol[:, bass.ds(i, 1)], x, ALU.mult, ALU.add
                                                         ).then_inc(ada_acc, 1)

    def dve_mod(dve, L):
        for b in range(12):
            dve.wait_ge(mod_tp, 12 * L + b + 1)
            dve.tensor_reduce(modc[:, L, 4 * b:4 * b + 4], ps[:, 4 + b % 4].rearrange("p (m n) -> p m n", n=P), AX.X,
                              ALU.add).then_inc(mod_sum, 1)
        dve.wait_ge(mod_sum, 12 * (L + 1))
        dve.tensor_tensor(modc[:, L], modc[:, L], tab[:, TAB["adab"] + 48 * L:TAB["adab"] + 48 * L + 48], ALU.add
                          ).then_inc(mod_done, 1)

    def dve_fox_aug(dve):
        for x in (qh, kh):
            for par, r in ((0, 64), (1, 0)):
                dve.memset(x[r:r + 64, par::2], 0.0).then_inc(aug, 1)
        dve.wait_ge(fl_dve, 12)
        dve.wait_ge(cum_mm, 1)
        cum = ps[0:16, 1]
        for r in range(0, P, 32):
            dve.tensor_scalar(cumx[r:r + 16], cum, 1.0 if r % 64 else -1.0, None, ALU.mult).then_inc(aug, 1)
        dve.wait_ge(aug, 8)
        for par, r in ((0, 64), (1, 0)):
            def rows16(x, r0):
                return x[r0:r0 + 16, par::2]
            hot = lambda r0: onehot[r0:r0 + 16, par::2].unsqueeze(2).to_broadcast([16, 8, T])
            cumb = lambda r0: cumx[r0:r0 + 16].unsqueeze(1).to_broadcast([16, 8, T])
            dve.tensor_copy(rows16(kh, r), cumb(r)).then_inc(aug, 1)
            dve.memset(rows16(kh, r + 32), 1.0).then_inc(aug, 1)
            dve.tensor_copy(rows16(qh, r), hot(r)).then_inc(aug, 1)
            dve.tensor_tensor(rows16(qh, r + 32), cumb(r + 32), hot(r + 32), ALU.mult).then_inc(aug, 1)

    AUG = 16

    def dve_fv(dve):
        S = U0["fv"]
        for h in range(2):
            dve.wait_ge(unit_done, S + 4 * h + 4)
            for t in range(NT):
                dve.tensor_copy(vtok[:, t, h * HALF:(h + 1) * HALF], ps[:, 4 * h + t]).then_inc(fv_ev, 1)

    def dve_attn(dve, A, oT, causal, hook=None):
        B = 64 * A

        def pv_out(pr):
            dve.wait_ge(at_pv, 16 * A + 2 * pr + 2)
            dve.tensor_copy(oT[:, pr], ps[:, 5 + pr % 2]).then_inc(at_o, 1)

        for n in range(65):
            if n == 58 and hook:
                hook()
            if n < 64:
                N = (n % 4 + 1) * P if causal else T
                dve.wait_ge(at_s, B + n + 1)
                dve.tensor_reduce(rowst[:, 0, n:n + 1], ps[:, SBANKS[n % 4], 0:N], AX.X, ALU.max, negate=True).then_inc(at_max, 1)
            m = n - 1
            if m >= 0:
                N = (m % 4 + 1) * P if causal else T
                dve.wait_ge(at_exp, B + m + 1)
                dve.reciprocal(rowst[:, 2, m:m + 1], rowst[:, 1, m:m + 1]).then_inc(at_rinv, 1)
                dve.wait_ge(at_rinv, B + m + 1)
                dve.tensor_scalar(pbuf[:, m % PSLOTS, 0:N], pbuf[:, m % PSLOTS, 0:N], rowst[:, 2, m:m + 1], None, ALU.mult
                                  ).then_inc(at_p, 1)
            if n >= 14 and n % 8 == 6:
                pv_out((n - 14) // 8)
        pv_out(7)

    def dve_rms_end(dve, s):
        dve.wait_ge(sq_done, 8 * (s + 1))
        dve.tensor_tensor(mv[:, :, 0], sumsq[:, :, 0], sumsq[:, :, 1], ALU.add).then_inc(aggr_done, 1)
        dve.wait_ge(std_done, 4 + s + 1)
        dve.reciprocal(rstd[:], std[:]).then_inc(rstd_done, 1)
        dve.wait_ge(rstd_done, 4 + s + 1)
        for h in range(2):
            c = slice(h * HALF, (h + 1) * HALF)
            for t in range(NT):
                dve.tensor_scalar(nrm[:, t, c], xres[:, t, c], rstd[:, t:t + 1], None, ALU.mult).then_inc(nrm_done, 1)

    def dve_gated_half(dve, s, name, h):
        r = 4 + s
        if h == 0:
            dve.wait_ge(unit_done, U0[name] + PAIRS[name])
            dve.wait_ge(gate_ev, s + 1)
        for t in range(NT):
            if h:
                wait_tile(dve, r, name, t)
            c = slice(h * HALF, (h + 1) * HALF)
            dve.tensor_tensor(nrm[:, t, c], ps[:, 4 * h + t], gate[:, c], ALU.mult).then_inc(gated, 1)
            dve.wait_ge(gated, 8 * s + 4 * h + t + 1)
            dve.tensor_tensor(xres[:, t, c], xres[:, t, c], nrm[:, t, c], ALU.add).then_inc(res_add, 1)

    def dve_qkv(dve):
        n = 0
        dve.wait_ge(qkg_in, 48)
        for z in range(2):
            g2 = qkg[:, z].rearrange("p (d e) -> p d e", e=2)
            dve.tensor_tensor(gcs[:, z, :, 0], cs[:, :, 0], qkg[:, z].unsqueeze(1).to_broadcast([P, NT, HD]), ALU.mult
                              ).then_inc(q_tab, 1)
            for e in range(2):
                sin = lambda x: x.rearrange("p t (d e) -> p t d e", e=2)[:, :, :, e]
                dve.tensor_tensor(sin(gcs[:, z, :, 1]), sin(cs[:, :, 1]),
                                  g2[:, :, 1 - e].unsqueeze(1).to_broadcast([P, NT, HD // 2]), ALU.mult).then_inc(q_tab, 1)
        dve.wait_ge(q_tab, 6)
        for hh in range(3):
            nh = 4 if hh == 0 else 8
            w = nh * HD
            for t in range(NT):
                dve.wait_ge(q_sq, 4 * hh + t + 1)
                dve.tensor_reduce(hsum[:, 0, t, 0:nh], sqb[:, t, 0:w].rearrange("p (h d) -> p h d", d=HD), AX.X, ALU.add
                                  ).then_inc(q_sum, 1)
            dve.wait_ge(q_std, hh + 1)
            dve.reciprocal(hsum[:, 2, :, 0:nh], hsum[:, 1, :, 0:nh]).then_inc(q_sum, 1)
            dve.wait_ge(q_sum, 5 * hh + 5)
            z = 1 if hh == 0 else 0
            for t in range(NT):
                src = ps[:, 4 * (hh % 2) + t, 0:w].rearrange("p (h d) -> p h d", d=HD)
                v3 = lambda x: x[:, 0:w].rearrange("p (h d) -> p h d", d=HD)
                pair = lambda x: x[:, 0:w].rearrange("p (h d e) -> p h d e", d=HD // 2, e=2)
                tabs = gcs[:, z, t, 1].rearrange("p (d e) -> p d e", e=2)
                dst = k_tok[:, t] if hh == 0 else q_tok[:, t, (hh - 1) * HALF:hh * HALF]

                def step(ins):
                    nonlocal n
                    ins.then_inc(q_step, 1)
                    n += 1

                step(dve.tensor_tensor(v3(qn), src, hsum[:, 2, t, 0:nh].unsqueeze(2).to_broadcast([P, nh, HD]), ALU.mult))
                dve.wait_ge(q_step, n)
                step(dve.tensor_tensor(v3(ra), v3(qn), gcs[:, z, t, 0].unsqueeze(1).to_broadcast([P, nh, HD]), ALU.mult))
                for e in range(2):
                    step(dve.tensor_tensor(pair(rb)[:, :, :, e], pair(qn)[:, :, :, 1 - e],
                                           tabs[:, :, e].unsqueeze(1).to_broadcast([P, nh, HD // 2]), ALU.mult))
                dve.wait_ge(q_step, n)
                step(dve.tensor_tensor(dst, ra[:, 0:w], rb[:, 0:w], ALU.add))
        assert n == 60

    def dve_gate(dve, s):
        if s % 2:
            dve.wait_ge(mlp_done, 16 * (s + 1))
        if s == 2:
            dve.wait_ge(gm_up, 18)
            dve.wait_ge(gm_ud, 6)
        g0 = 24 * (s % 2) + 16
        for k in range(KD):
            dve.tensor_scalar(gdiag[:, k], ident, modc[:, s // 2, g0 + k:g0 + k + 1], None, ALU.mult).then_inc(gdiag_done, 1)

    def dve_mlp(dve, L):
        def unit(e, j):
            dve.wait_ge(relu_done, e + (32 * L + 1))
            dve.scalar_tensor_tensor(hid_mlp[:, bass.ds(e, 1)], ps[:, bank_f(j):bank_f(j) + 1], 0.0,
                                     relu[:, j % 2:j % 2 + 1], ALU.max, ALU.mult).then_inc(mlp_done, 1)

        run(dve, 28, unit)
        dve_first_splits(dve, f"md{L}", hid_mlp)
        for e in range(28, 32):
            unit(e, e % 4)

    def dve_gv(dve):
        S = U0["gv"]
        for hh in range(6):
            c = slice(hh * HALF, (hh + 1) * HALF)
            dve.wait_ge(unit_done, S + 4 * hh + 4)
            dve.wait_ge(bb_in[hh % 2], 16 * (hh // 2 + 1))
            for t in range(NT):
                dve.tensor_tensor(vt[t][:, c], ps[:, 4 * (hh % 2) + t], bb[:, hh % 2], ALU.add).then_inc(gv_add, 1)
            for t in range(NT):
                dve.wait_ge(gv_gelu, 4 * hh + t + 1)
                dve.bn_stats(stats[:, t, hh], vt[t][:, c]).then_inc(gv_stat, 1)
        dve.wait_ge(gv_stat, 24)
        for t in range(NT):
            dve.bn_aggr(mv[:, t], stats[:, t].rearrange("p a b -> p (a b)")).then_inc(gv_aggr, 1)
        dve.wait_ge(gv_std, 1)
        dve.reciprocal(rstd[:], std[:]).then_inc(gv_rstd, 1)
        dve.wait_ge(gv_rstd, 1)
        for t in range(NT):
            dve.tensor_scalar(vt[t][:], vt[t][:], mv[:, t, 0:1], rstd[:, t:t + 1], ALU.subtract, ALU.mult
                              ).then_inc(gv_nrm, 1)
        dve.wait_ge(rs_ev, 4)
        dve.wait_ge(bs_in, 16)
        nk = 0
        for cc in range(NGM):
            b = cc % 2
            for r0, r1, g in gm_pieces(cc):
                dve.scalar_tensor_tensor(gk[r0:r1, b], rs_b[r0:r1, g], col("glnb", cc)[r0:r1], bs_b[r0:r1, g],
                                         ALU.mult, ALU.add).then_inc(gm_k, 1)
                nk += 1
            dve.wait_ge(gm_k, nk)
            dve.wait_ge(gm_mm, cc + 1)
            if cc >= 4 and cc % 4 < 3:
                dve.wait_ge(gm_up, (cc // 4 - 1) * 3 + cc % 4 + 1)
            dve.scalar_tensor_tensor(gz[:, cc % 4].rearrange("p (n q) -> p n q", q=P),
                                     ps[:, 4 + cc % 4].rearrange("p (n q) -> p n q", q=P), col("glng", cc),
                                     gk[:, b].unsqueeze(1).to_broadcast([P, NT, P]), ALU.mult, ALU.add).then_inc(gm_z, 1)
            if cc % 4 == 3:
                dve.wait_ge(gm_z, cc + 1)
                dve.tensor_tensor(uT[:, cc], uT[:, cc], gz[:, 3], ALU.mult).then_inc(gm_ud, 1)

    def gm_pieces(cc):
        out, c = [], cc * P
        while c < (cc + 1) * P:
            g = c // GM_GW
            e = min((g + 1) * GM_GW, (cc + 1) * P)
            out.append((c - cc * P, e - cc * P, g))
            c = e
        return out

    @block.vector
    def _(dve):
        dve.memset(tabraw[:], 0.0).then_inc(tab_zero, 1)
        dve.memset(eps_ln[:, 0:1], LN_EPS).then_inc(prep, 1)
        dve.memset(eps_ln[:, 1:2], EPS).then_inc(prep, 1)
        dve_xt(dve, 0)
        dve.wait_ge(wf_hi, 1)
        dve.tensor_tensor(wf_lo_t[:], wf_raw[:], wf_hi_t[:].bitcast(F32), ALU.subtract).then_inc(wf_lo, 1)
        dve.wait_ge(tab_ready, 2)
        dve_xbc(dve)
        assert dve_soft(dve, dts, dta, 1, small[:, 0], True, sm[:, 9]) == 12
        dve.wait_ge(dta, 3)
        dve.scalar_tensor_tensor(sm[:, 10], sm[:, 9], -1.0, sm[:, 8, 0].unsqueeze(1).to_broadcast([P, NT, 16]),
                                 ALU.mult, ALU.mult).then_inc(dts, 1)
        dve.wait_ge(dts, 13)
        dve.memset(mv[:], 0.0).then_inc(sc_step, 1)
        dve_scp(dve)
        dve_scb(dve)
        dve_ssd(dve)
        dve_jit(dve, "out0", ya_yb, lambda: dve_ln_half(dve, 0, "out0", 0), head=dve_gate_norm)
        dve_ln_half(dve, 0, "out0", 1)
        dve_ln_end(dve, 0)
        dve_xt(dve, 1)
        dve_resid(dve, 0)
        dve_ffn(dve, 0)

        dve.wait_ge(ff_dve, 110)
        dve_jit(dve, "dn0", hid_ff, lambda: dve_ln_half(dve, 1, "dn0", 0), head=lambda dve: dve_mod(dve, 0), head_at=4, done=2)
        dve_ln_half(dve, 1, "dn0", 1)
        dve_ln_end(dve, 1)
        dve_xt(dve, 2)
        dve.wait_ge(wf_hi, 2)
        dve.tensor_tensor(wf_lo_t[:], wf_raw[:], wf_hi_t[:].bitcast(F32), ALU.subtract).then_inc(wf_lo, 1)
        assert dve_soft(dve, fl_dve, fl_act, 2, small[:, 3], False, sm[:, 9]) == 12
        dve_resid(dve, 1)
        dve_fox_aug(dve)
        dve_fv(dve)
        dve_attn(dve, 0, oT1, True)
        dve_jit(dve, "fo", oT1, lambda: dve_ln_half(dve, 2, "fo", 0))
        dve_ln_half(dve, 2, "fo", 1)
        dve_ln_end(dve, 2)
        dve_xt(dve, 3)
        dve_resid(dve, 2)
        dve_ffn(dve, 1)
        dve.wait_ge(ff_dve, 220)
        dve_jit(dve, "dn1", hid_ff, lambda: dve_ln_half(dve, 3, "dn1", 0), head=lambda dve: dve_mod(dve, 1), head_at=4, done=2)
        dve_ln_half(dve, 3, "dn1", 1)
        dve_ln_end(dve, 3, to_nrm=False)
        dve.wait_ge(mod_done, 2)
        for s in range(4):
            m0 = 24 * (s % 2) + 8
            g0 = TAB["n1g" if s % 2 == 0 else "n2g"] + 8 * (s // 2)
            dve.scalar_tensor_tensor(nscale[:, s], modc[:, s // 2, m0:m0 + KD], 1.0, tab[:, g0:g0 + KD], ALU.add, ALU.mult
                                     ).then_inc(prep, 1)
        dve_rms_end(dve, 0)
        dve_xt(dve, 4)
        dve_qkv(dve)
        dve_attn(dve, 1, oT2, False, hook=lambda: dve_first_splits(dve, "o", oT2))
        for s, (name, src) in enumerate((("o", oT2), ("md0", hid_mlp), ("go", uT), ("md1", hid_mlp))):
            if name == "md0":
                dve_mlp(dve, 0)
            if name == "go":
                dve_gv(dve)
            if name == "md1":
                dve_mlp(dve, 1)
            dve_jit(dve, name, src, lambda: dve_gated_half(dve, s, name, 0), head=lambda dve: dve_gate(dve, s),
                    done=0 if name == "go" else 2)
            dve_gated_half(dve, s, name, 1)
            if name != "md1":
                dve_rms_end(dve, s + 1)
                dve_xt(dve, 5 + s)

    def mm3(pe, out, lh, ll, rh, rl, start, stop):
        pe.matmul(out, lh, rh, start=start, stop=False)
        pe.matmul(out, lh, rl, start=False, stop=False)
        return pe.matmul(out, ll, rh, start=False, stop=stop)

    def pe_xt(pe, q):
        if q == 0:
            pe.wait_ge(x_in, 16)
            pe.wait_ge(consts_in, 32)
        else:
            pe.wait_ge(nrm_done, 8 * q - 4)
        src = xres if q == 0 else nrm
        for k in range(KD):
            if q and k == 4:
                pe.wait_ge(nrm_done, 8 * q)
            if k >= 4:
                pe.wait_ge(xt_ev, KD * q + k - 3)
            for t in range(NT):
                ins = pe.transpose(ps[:, k % 4, t * P:(t + 1) * P], src[:, t, k * P:(k + 1) * P], ident)
            ins.then_inc(xt_tp, 1)

    def pe_table(pe):
        pe.wait_ge(tab_in, TAB_LOADS)
        pe.wait_ge(xt_ev, 8)
        for b in range(NTAB):
            ins = pe.transpose(ps[:, b // 4, (b % 4) * P:(b % 4 + 1) * P], tabraw[:, b], ident)
            if b in (3, 5):
                ins.then_inc(tab_tp, 1)

    def pe_f(pe, name, freed, q=None, first=(), before_six=None):
        S, n = U0[name], NUNITS[name]

        def parts(j):
            slot = (S + j) % RING
            return (w[:, slot].rearrange("p (k n) -> p k n", k=KD) for w in (whi, wlo))

        def unit(e, j):
            pe.wait_ge(w_lo, e + (S + 1))
            wh, wl = parts(j)
            for k in range(KD):
                ins = mm3(pe, ps[:, bank_f(j)], wh[:, k], wl[:, k], xhi[:, k], xlo[:, k], k == 0, k == KD - 1)
            ins.then_inc(unit_done, 1)

        for s, v in first:
            pe.wait_ge(s, v)
        if q is not None:
            for k in range(KD):
                if k == 5 and before_six:
                    before_six()
                pe.wait_ge(xt_lo, KD * q + k + 1)
                for e in range(3):
                    if k == 0:
                        pe.wait_ge(w_lo, S + e + 1)
                    wh, wl = parts(e)
                    ins = mm3(pe, ps[:, bank_f(e)], wh[:, k], wl[:, k], xhi[:, k], xlo[:, k], k == 0, k == KD - 1)
                    if k == KD - 1:
                        ins.then_inc(unit_done, 1)
        for e in range(0 if q is None else 3, RING):
            unit(e, e)
        if n // RING == 2:
            for e in range(RING, n):
                s, v = freed(1, e % RING)
                pe.wait_ge(s, v)
                unit(e, e % RING)
        else:
            with pe.Fori(1, n // RING) as i:
                for j in range(RING):
                    s, v = freed(i, j)
                    pe.wait_ge(s, v)
                    unit(i * RING + j, j)

    def pe_t_unit(pe, start, e, j, bank0, lh, ll, first):
        slot = (start + j) % RING
        pe.wait_ge(w_lo, e + (start + 1))
        wh = whi[:, slot].rearrange("p (k n) -> p k n", k=2)
        wl = wlo[:, slot].rearrange("p (k n) -> p k n", k=2)
        for k in range(2):
            for t in range(NT):
                out = ps[:, bank0 + t]
                st = first and k == 0
                c = slice(t * P, (t + 1) * P)
                pe.matmul(out, lh[:, k, c], wh[:, k], start=st, stop=False, skip_group_check=True)
                pe.matmul(out, lh[:, k, c], wl[:, k], start=False, stop=False, skip_group_check=True)
                ins = pe.matmul(out, ll[:, k, c], wh[:, k], start=False, stop=False, skip_group_check=True)
        ins.then_inc(unit_done, 1)

    def pe_t_x(pe, name, halves, free):
        S = U0[name]
        for h in range(halves):
            for s, v in free(h):
                pe.wait_ge(s, v)
            for j in range(4):
                pe_t_unit(pe, S + 4 * h, j, j, 4 * (h % 2), xhi[:, 2 * j:2 * j + 2], xlo[:, 2 * j:2 * j + 2], j == 0)

    def pe_t_tail(pe, u0, a_pair, bank0):
        first = [3, 2]
        for i, tiles in ((0, first), (0, [0]), (1, [0]), (0, [1]), (1, [1]), (1, [2]), (1, [3])):
            u, s = u0 + i, (a_pair + i) % 2
            pe.wait_ge(w_lo, u + 1)
            pe.wait_ge(a_lo, a_pair + i + 1)
            wh = whi[:, u % RING].rearrange("p (k n) -> p k n", k=2)
            wl = wlo[:, u % RING].rearrange("p (k n) -> p k n", k=2)
            for t in tiles:
                out, c = ps[:, bank0 + t], slice(t * P, (t + 1) * P)
                for k in range(2):
                    pe.matmul(out, ahi[:, s, k, c], wh[:, k], start=False, stop=False, skip_group_check=True)
                    pe.matmul(out, ahi[:, s, k, c], wl[:, k], start=False, stop=False, skip_group_check=True)
                    ins = pe.matmul(out, alo[:, s, k, c], wh[:, k], start=False, stop=False, skip_group_check=True)
            if i == 1:
                if tiles[0] < NT - 1:
                    ins.then_inc(tile_done, 1)
                else:
                    ins.then_inc(unit_done, 2)

    def pe_t_jit(pe, name, free, head=None):
        H, S, A = PAIRS[name], U0[name], A0[name]
        for h in range(2):
            for s, v in free(h):
                pe.wait_ge(s, v)

            def unit(m0, e, j, first):
                pe.wait_ge(a_lo, e + (A + m0 + 1))
                s = (m0 + j) % 2
                pe_t_unit(pe, S + m0, e, j, 4 * h, ahi[:, s], alo[:, s], first)

            unit(h * H, 0, 0, True)
            if h:
                run(pe, H - 3, lambda e, j: unit(H + 1, e, j, False))
                pe_t_tail(pe, S + 2 * H - 2, A + 2 * H - 2, 4)
            elif head:
                unit(1, 0, 0, False)
                unit(2, 0, 0, False)
                head(pe)
                run(pe, H - 3, lambda e, j: unit(3, e, j, False))
            else:
                run(pe, H - 1, lambda e, j: unit(1, e, j, False))

    def pe_small(pe, q):
        pe.wait_ge(wf_lo, q + 1)
        for k in range(KD):
            ins = mm3(pe, ps[0:16, 1], wf_hi_t[:, k], wf_lo_t[:, k], xhi[:, k], xlo[:, k], k == 0, k == KD - 1)
        ins.then_inc(narrow_mm, 1)
        pe.wait_ge(narrow_ev, q + 1)
        for t in range(NT):
            ins = pe.transpose(ps[:, 0, t * 16:(t + 1) * 16], narrow[0:16, t * P:(t + 1) * P], ident[0:16, 0:16])
        ins.then_inc(f_mm, 1)

    def pe_ssd(pe):
        pe.wait_ge(xbc_silu, 12)
        pe.wait_ge(z_done, 4)
        for g in range(12):
            t, r = divmod(g, 3)
            if g >= 4:
                pe.wait_ge(tok_ev_d if g % 2 else tok_ev_a, g // 2 - 1)
            for k in range(4 if r < 2 else 2):
                ins = pe.transpose(ps[:, g % 4, k * P:(k + 1) * P], xbcT[:, 4 * r + k, t * P:(t + 1) * P], ident)
            ins.then_inc(tok_tp, 1)
        pe.wait_ge(dts, 13)
        pe.wait_ge(tok_ev_d, 6)
        adt = sm[:, 10].rearrange("p c h -> p (c h)")
        pe.matmul(ps[:, 1, 0:64], tri, adt, start=True, stop=True)
        pe.matmul(ps[:, 1, 64:128], ones, adt, start=True, stop=True).then_inc(cums_mm, 1)
        ny = [2, 6, 10]
        nprev = [1, 3, 5]
        for c in range(NT):
            tc = slice(c * P, (c + 1) * P)
            if c == 0:
                pe.wait_ge(z_done, 8)
                pe.wait_ge(tok_ev_a, 6)
            pe.wait_ge(ssd_g, c + 1)
            for g in range(2):
                pe.matmul(ps[:, 0, g * P:(g + 1) * P], xbcT[:, 8 + g, tc], xbcT[:, 10 + g, tc], start=True, stop=True)
            for g in range(2):
                if c and g:
                    pe.wait_ge(ssd_prev, nprev[c - 1])
                for b in range(2):
                    ins = pe.matmul(ps[:, 2 + 4 * g + b], ones,
                                    gbuf[:, 8 * g + 4 * b:8 * g + 4 * b + 4].rearrange("p h t -> p (h t)"),
                                    start=True, stop=True)
                ins.then_inc(ssd_r, 1)
            if c:
                pe.wait_ge(ssd_y, ny[c - 1])
                for g in range(2):
                    ins = pe.matmul(ps[:, 4 + g], xbcT[:, 10 + g, tc], prev[:, g * HALF:(g + 1) * HALF],
                                    start=True, stop=True)
                ins.then_inc(ssd_off, 1)
                pe.wait_ge(ssd_y, ny[c - 1] + 1)
            pe.wait_ge(ssd_x, 2 * c + 2)
            for h in range(HEADS):
                if h % 8 == 0:
                    pe.wait_ge(ssd_m, 2 * c + h // 8 + 1)
                ins = pe.matmul(ps[:, 4 + h // 8, (h % 8) * HD:(h % 8 + 1) * HD], mbuf[:, h],
                                xdt[c % 2][:, h * HD:(h + 1) * HD], start=True, stop=True)
            if c < NT - 1:
                for g in range(2):
                    ins = pe.matmul(ps[:, 6 + g], b_tok[:, c, g * P:(g + 1) * P], xdd[c % 2][:, g * HALF:(g + 1) * HALF],
                                    start=True, stop=True)
            ins.then_inc(ssd_mm, 1)

    def pe_gate_tp(pe):
        pe.wait_ge(gt_n, 8)
        for k in range(KD):
            if k >= 4:
                pe.wait_ge(gt_ev, k - 3)
            for t in range(NT):
                ins = pe.transpose(ps[:, 4 + k % 4, t * P:(t + 1) * P], y_tok[:, t, k * P:(k + 1) * P], ident)
            ins.then_inc(gt_tp, 1)

    def pe_cum(pe):
        pe.wait_ge(fl_dve, 12)
        for t in range(NT):
            for i in range(t + 1):
                ins = pe.matmul(ps[0:16, 1, t * P:(t + 1) * P], sm[:, 9, i], tri if i == t else ones,
                                start=i == 0, stop=i == t)
        ins.then_inc(cum_mm, 1)

    def pe_attn(pe, A, ptb, causal, q_of, k_of, v_of):
        B = 64 * A

        def weigh(h):
            bank, r = 5 + (h // 2) % 2, 64 * (h % 2)
            pe.wait_ge(at_pt, B + 4 * h + 4)
            if h % 2 == 0 and h >= 4:
                pe.wait_ge(at_o, 8 * A + h // 2 - 1)
            for c in range(NT):
                q0 = c * P if causal else 0
                ins = pe.matmul(ps[r:r + 64, bank, q0:T], v_of(h, c), ptb[:, h % 2, c, q0:T], start=c == 0, stop=c == NT - 1)
            ins.then_inc(at_pv, 1)

        for n in range(64 + LEAD):
            if n < 64:
                h, i = divmod(n, 4)
                N = (i + 1) * P if causal else T
                if n >= 4:
                    pe.wait_ge(at_exp, B + n - 3)
                ins = pe.matmul(ps[:, SBANKS[n % 4], 0:N], q_of(h, i), k_of(h, N), start=True, stop=not causal)
                if causal:
                    ins = pe.matmul(ps[:, SBANKS[n % 4], i * P:N], ident_r[:], cmask_r[:], start=False, stop=True)
                ins.then_inc(at_s, 1)
            m = n - LEAD
            if m >= 0:
                h, i = divmod(m, 4)
                pe.wait_ge(at_p, B + m + 1)
                if m >= 2:
                    pe.wait_ge(at_pt, B + m - 1)
                for c in range(i + 1 if causal else NT):
                    ins = pe.transpose(ps[:, 3 + m % 2, c * P:(c + 1) * P], pbuf[:, m % PSLOTS, c * P:(c + 1) * P], ident)
                ins.then_inc(at_tp, 1)
                if i == 1 and h:
                    weigh(h - 1)
        weigh(HEADS - 1)

    def pe_mod(pe, L):
        pe.wait_ge(ada_acc, 32 * (L + 1))
        pe.wait_ge(ff_dve, 110 * (L + 1))
        for b in range(12):
            if b >= 4:
                pe.wait_ge(mod_sum, 12 * L + b - 3)
            for i in range(4):
                ins = pe.transpose(ps[:, 4 + b % 4, i * P:(i + 1) * P], acc[:, 4 * b + i], ident)
            ins.then_inc(mod_tp, 1)

    def pe_gate(pe, s):
        pe.wait_ge(gdiag_done, KD * (s + 1))
        for k in range(KD):
            ins = pe.matmul(ps[:, 4 + k // 4, (k % 4) * P:(k % 4 + 1) * P], ones, gdiag[:, k], start=True, stop=True)
        ins.then_inc(gate_mm, 1)

    def pe_gv(pe):
        S = U0["gv"]

        def half(h, b, e0):
            for j in range(4):
                pe_t_unit(pe, S, e0 + j, j, 4 * b, xhi[:, 2 * j:2 * j + 2], xlo[:, 2 * j:2 * j + 2], j == 0)

        for b in range(2):
            if b:
                pe.wait_ge(gu_ev, NGM)
            half(b, b, 4 * b)
        with pe.Fori(1, 3) as i:
            for b in range(2):
                pe.wait_ge(gv_add, i * 8 + (4 * b - 4))
                half(None, b, i * 8 + 4 * b)
        pe.wait_ge(ws_in, 16)
        pe.wait_ge(gv_add, 20)
        for g in range(GM_GROUPS):
            ins = pe.transpose(ps[:, g // 4, (g % 4) * P:(g % 4 + 1) * P], wsraw[:, g], ident)
            if g % 4 == 3:
                ins.then_inc(ws_tp, 1)
        for b in range(4):
            pe.wait_ge(ws_ev, b + 1)
            pe.matmul(ps[:, b], ones, wsT[:, 4 * b:4 * b + 4].rearrange("p g q -> p (g q)"), start=True, stop=True
                      ).then_inc(rs_mm, 1)
        pe.wait_ge(gv_nrm, 4)
        for cc in range(NGM):
            if cc >= 4:
                pe.wait_ge(gm_z, cc - 3)
            for r0, r1, g in gm_pieces(cc):
                for t in range(NT):
                    ins = pe.matmul(ps[r0:r1, 4 + cc % 4, t * P:(t + 1) * P], vt[t][:, cc * P + r0:cc * P + r1], wsT[:, g],
                                    start=True, stop=True)
            ins.then_inc(gm_mm, 1)

    @block.tensor
    def _(pe):
        pe_xt(pe, 0)
        pe_f(pe, "xbc", lambda i, j: (xbc_conv, i * 12 + (3 * j - 9)), q=0, before_six=lambda: pe_table(pe))
        pe.wait_ge(tab_ready, 2)
        pe_small(pe, 0)
        pe_f(pe, "scp", lambda i, j: (sc_step, i * 8 + (1 + 4 * (j // 2) - 8 + 1)), first=((xbc_conv, 36),))
        pe_f(pe, "scb", lambda i, j: (scb_done, 4 * i + j - 3), first=((sc_step, 33 - 3),))
        pe_t_x(pe, "z", 2, lambda h: ((dts, 1),) if h == 0 else ((scb_done, 8),))
        pe_ssd(pe)
        pe_t_jit(pe, "out0", lambda h: ((ssd_y, 14),) if h == 0 else ((gt_ev, 8),), head=pe_gate_tp)
        pe_xt(pe, 1)
        pe_f(pe, "up0", lambda i, j: (ff_dve, i * 10 + (5 * (j // 2) - 10 + 2 + 2 * (j % 2))), q=1, first=((res_add, 8),))
        pe_t_jit(pe, "dn0", lambda h: ((xt_ev, 16),) if h == 0 else ((mod_done, 1),),
                 head=lambda pe: pe_mod(pe, 0))
        pe_xt(pe, 2)
        pe.wait_ge(xt_lo, 24)
        pe_small(pe, 1)
        pe_f(pe, "fqk", lambda i, j: (fqk_ev, i * 8 + (2 * j - 6)), first=((res_add, 16),))
        pe_cum(pe)
        pe_t_x(pe, "fv", 2, lambda h: ((aug, 8),) if h == 0 else ((fqk_ev, 32),))
        pe.wait_ge(fv_ev, 8)
        pe.wait_ge(aug, AUG)
        pe.wait_ge(mask_ready, 2)
        pe_attn(pe, 0, ptb1, True, lambda h, i: qh[:, h, i * P:(i + 1) * P], lambda h, N: kh[:, h, 0:N],
                lambda h, c: vtok[:, c, h * HD:(h + 1) * HD])
        pe_t_jit(pe, "fo", lambda h: ((at_exp, 64), (at_pt, 64)) if h == 0 else ((at_o, 8),))
        pe_xt(pe, 3)
        pe_f(pe, "up1", lambda i, j: (ff_dve, i * 10 + (110 + 5 * (j // 2) - 10 + 2 + 2 * (j % 2))), q=3,
             first=((res_add, 24),))
        pe_t_jit(pe, "dn1", lambda h: ((xt_ev, 32),) if h == 0 else ((mod_done, 2),),
                 head=lambda pe: pe_mod(pe, 1))
        pe_xt(pe, 4)
        pe.wait_ge(xt_lo, 40)
        pe_t_x(pe, "qkv", 3, lambda h: (((xt_ev, 40),), ((res_add, 32),), ((q_step, 5 * 3 + 1), (v_ev, 4)))[h])
        for r in range(10):
            if r == 0:
                pe.wait_ge(q_step, 5 * 7 + 1)
            if r == 2:
                pe.wait_ge(q_step, 40)
            if r == 6:
                pe.wait_ge(q_step, 60)
            if r >= 4:
                pe.wait_ge(q_ev, {4: 1, 5: 2}.get(r, 2 + 2 * (r - 4 - 1)))
            src, k = (k_tok, r) if r < 2 else (q_tok, r - 2)
            for t in range(NT):
                ins = pe.transpose(ps[:, 4 + r % 4, t * P:(t + 1) * P], src[:, t, k * P:(k + 1) * P], ident)
            ins.then_inc(q_tp, 1)
        pe.wait_ge(q_ev, 18)

        def kb(h):
            return slice(64 * (h // 4 % 2), 64 * (h // 4 % 2) + 64)

        pe_attn(pe, 1, ptb2, False, lambda h, i: qT2[kb(h), h // 8 * 4 + h % 4, i * P:(i + 1) * P],
                lambda h, N: kT2[kb(h), h // 8, 0:N], lambda h, c: v2[:, c, (h // 4) * HD:(h // 4 + 1) * HD])
        pe_t_jit(pe, "o", lambda h: ((at_exp, 128), (at_pt, 128)) if h == 0 else ((gate_ev, 1),),
                 head=lambda pe: (pe.wait_ge(at_o, 16), pe_gate(pe, 0)))
        pe_xt(pe, 5)
        pe_f(pe, "mu0", lambda i, j: (mlp_done, i * 4 + (j - 3)), q=5, first=((res_add, 40),))
        pe_t_jit(pe, "md0", lambda h: ((xt_ev, 48),) if h == 0 else ((gate_ev, 2),),
                 head=lambda pe: (pe.wait_ge(mlp_done, 32), pe_gate(pe, 1)))
        pe_xt(pe, 6)
        pe_f(pe, "gu", lambda i, j: (gu_ev, i * 4 + (j - 3)), q=6, first=((res_add, 48),))
        pe.wait_ge(xt_ev, 56)
        pe_gv(pe)
        pe_t_jit(pe, "go", lambda h: ((rs_ev, 4),) if h == 0 else ((gate_ev, 3),),
                 head=lambda pe: (pe.wait_ge(gm_z, NGM), pe_gate(pe, 2)))
        pe_xt(pe, 7)
        pe_f(pe, "mu1", lambda i, j: (mlp_done, i * 4 + (j + 29)), q=7, first=((res_add, 56),))
        pe_t_jit(pe, "md1", lambda h: ((xt_ev, 64),) if h == 0 else ((gate_ev, 4),),
                 head=lambda pe: (pe.wait_ge(mlp_done, 64), pe_gate(pe, 3)))


def kernel(**inputs):
    import concourse.bacc as bacc
    from concourse.bass_utils import run_bass_kernel_spmd

    nc = bacc.Bacc("TRN2", target_bir_lowering=False, num_devices=1)
    consts, cs, onehot = host_constants()
    arrays, aps = {}, {}
    for name, x in list(inputs.items()) + [("consts", consts), ("cs", cs), ("onehot", onehot)]:
        x = np.ascontiguousarray(x)
        arrays[f"in_{name}"] = x
        aps[name] = nc.dram_tensor(f"in_{name}", x.shape, mybir.dt.from_np(x.dtype), kind="ExternalInput").ap()
    out = nc.dram_tensor("out", (1, T, D), F32, kind="ExternalOutput").ap()
    build(nc, aps, out)
    r = run_bass_kernel_spmd(nc, [arrays], core_ids=[0])
    return r.results[0]["out"]
```
